# Optimizing a Trainium2 kernel written in Bass

```python
import jax, jax.numpy as jnp
from jax import lax
import numpy as np

D_MODEL = 1024
BATCH = 1
SEQ = 1024
DEPTH = 1

D_MIX = D_MODEL
D_HGRN = D_MIX // 2
D_CONV = D_MIX - D_HGRN
HGRN_HEAD_DIM = 128
HGRN_HEADS = D_HGRN // HGRN_HEAD_DIM
CHUNK = 64
CONV_WIDTH = 31
CONV_PAD = CONV_WIDTH // 2
N_IN = 5 * D_HGRN + 2 * D_CONV
PEER_HEADS = 8
PEER_KEYS = 128
PEER_EXPERTS = PEER_KEYS * PEER_KEYS
PEER_TOPK = 16
PEER_DKEY = 256
PEER_HALF = PEER_DKEY // 2
PEER_BLOCK = 128
EPS = 1e-6

kernel_name = 'hgrn2_conformer_peer_hybrid_encoder'

def _rmsnorm(x, g):
    xf = x.astype(jnp.float32)
    y = xf * lax.rsqrt(jnp.mean(xf * xf, axis=-1, keepdims=True) + EPS)
    return (y * g.astype(jnp.float32)).astype(x.dtype)

def _modulate(h, shift, scale):
    return h * (1 + scale[:, None, :]) + shift[:, None, :]

def _chunk_recurrence(q, k, v, logf):
    nb, nh, L, dk = q.shape
    dv = v.shape[-1]
    nc = L // CHUNK
    q = q.reshape(nb, nh, nc, CHUNK, dk)
    k = k.reshape(nb, nh, nc, CHUNK, dk)
    logf = logf.reshape(nb, nh, nc, CHUNK, dk)
    v = v.reshape(nb, nh, nc, CHUNK, dv)
    b = jnp.cumsum(logf, axis=3)
    b_ref = b[:, :, :, CHUNK // 2 - 1:CHUNK // 2, :]
    b_last = b[:, :, :, -1:, :]
    qr = q * jnp.exp(b - b_ref)
    kr = k * jnp.exp(b_ref - b)
    scores = jnp.einsum('bhntd,bhnsd->bhnts', qr, kr)
    incl = jnp.tril(jnp.ones((CHUNK, CHUNK), dtype=bool))
    scores = jnp.where(incl, scores, 0.0)
    o_intra = jnp.einsum('bhnts,bhnsv->bhntv', scores, v)
    u = jnp.einsum('bhnsd,bhnsv->bhndv', k * jnp.exp(b_last - b), v)
    a = jnp.exp(b_last[:, :, :, 0, :])

    def step(S, inp):
        a_n, u_n = inp
        return a_n[..., None] * S + u_n, S

    S0 = jnp.zeros((nb, nh, dk, dv), jnp.float32)
    _, S_prev = lax.scan(step, S0, (jnp.moveaxis(a, 2, 0), jnp.moveaxis(u, 2, 0)))
    S_prev = jnp.moveaxis(S_prev, 0, 2)
    o_inter = jnp.einsum('bhntd,bhndv->bhntv', q * jnp.exp(b), S_prev)
    return (o_intra + o_inter).reshape(nb, nh, L, dv)

def _hgrn2(q_raw, ff_raw, fb_raw, i_raw, g_raw, lb_fwd, lb_bwd, norm_g):
    nb, L, _ = q_raw.shape
    f32 = jnp.float32

    def heads(t):
        return t.astype(f32).reshape(nb, L, HGRN_HEADS, HGRN_HEAD_DIM).transpose(0, 2, 1, 3)

    q = jax.nn.silu(heads(q_raw))
    v = heads(i_raw)

    def gates(f_raw, lb):
        z = heads(f_raw)
        lbh = lb.astype(f32).reshape(1, HGRN_HEADS, 1, HGRN_HEAD_DIM)
        logf = jnp.log(lbh + (1 - lbh) * jax.nn.sigmoid(z))
        k = (1 - lbh) * jax.nn.sigmoid(-z)
        return k, logf

    k_f, logf_f = gates(ff_raw, lb_fwd)
    k_b, logf_b = gates(fb_raw, lb_bwd)
    o_f = _chunk_recurrence(q, k_f, v, logf_f)
    flip = lambda t: jnp.flip(t, axis=2)
    o_b = flip(_chunk_recurrence(flip(q), flip(k_b), flip(v), flip(logf_b)))
    o = (o_f + o_b).transpose(0, 2, 1, 3)
    o = o * lax.rsqrt(jnp.mean(o * o, axis=-1, keepdims=True) + EPS)
    o = o * norm_g.astype(f32).reshape(HGRN_HEADS, HGRN_HEAD_DIM)
    o = o.reshape(nb, L, D_HGRN) * jax.nn.silu(g_raw.astype(f32))
    return o.astype(q_raw.dtype)

def _conv_module(a, gate, w, bias, ln_g, ln_b):
    h = a * jax.nn.sigmoid(gate)
    h = lax.conv_general_dilated(
        h, w[:, None, :].astype(h.dtype), window_strides=(1,),
        padding=[(CONV_PAD, CONV_PAD)], dimension_numbers=('NWC', 'WIO', 'NWC'),
        feature_group_count=D_CONV) + bias
    hf = h.astype(jnp.float32)
    mu = jnp.mean(hf, axis=-1, keepdims=True)
    var = jnp.mean(jnp.square(hf - mu), axis=-1, keepdims=True)
    hf = (hf - mu) * lax.rsqrt(var + EPS) * ln_g.astype(jnp.float32) + ln_b.astype(jnp.float32)
    return jax.nn.silu(hf).astype(a.dtype)

def _peer(h, wq, keys1, keys2, u_tab, v_tab):
    nb, L, D = h.shape
    q = (h @ wq).reshape(nb, L, PEER_HEADS, PEER_DKEY)
    q1, q2 = q[..., :PEER_HALF], q[..., PEER_HALF:]
    s1 = jnp.einsum('blhd,kd->blhk', q1, keys1).astype(jnp.float32)
    s2 = jnp.einsum('blhd,kd->blhk', q2, keys2).astype(jnp.float32)
    v1, i1 = lax.top_k(s1, PEER_TOPK)
    v2, i2 = lax.top_k(s2, PEER_TOPK)
    cand = (v1[..., :, None] + v2[..., None, :]).reshape(nb, L, PEER_HEADS, PEER_TOPK * PEER_TOPK)
    sc, ci = lax.top_k(cand, PEER_TOPK)
    e = (jnp.take_along_axis(i1, ci // PEER_TOPK, axis=-1) * PEER_KEYS
         + jnp.take_along_axis(i2, ci % PEER_TOPK, axis=-1))
    w = jax.nn.softmax(sc, axis=-1)
    T = nb * L
    nsel = PEER_HEADS * PEER_TOPK
    hb = h.reshape(T // PEER_BLOCK, PEER_BLOCK, D)
    eb = e.reshape(T // PEER_BLOCK, PEER_BLOCK, nsel)
    wb = w.reshape(T // PEER_BLOCK, PEER_BLOCK, nsel)

    def block(args):
        hx, ex, wx = args
        u_sel = u_tab[ex]
        act = jax.nn.gelu(jnp.einsum('td,tjd->tj', hx, u_sel).astype(jnp.float32), approximate=False)
        coef = (wx * act).astype(hx.dtype)
        return jnp.einsum('tj,tjd->td', coef, v_tab[ex])

    y = lax.map(block, (hb, eb, wb))
    return y.reshape(nb, L, D)

def setup_inputs(seed: int = 0) -> dict:
    key = jax.random.key(seed)
    ks = jax.random.split(key, 24)
    nrm = jax.random.normal
    f32 = jnp.float32
    Dm = D_MODEL
    return {
        'x': nrm(ks[0], (BATCH, SEQ, Dm), f32),
        'c': nrm(ks[1], (BATCH, Dm), f32),
        'ada_w': nrm(ks[2], (DEPTH, Dm, 6 * Dm), f32) * (0.5 * Dm ** -0.5),
        'ada_b': nrm(ks[3], (DEPTH, 6 * Dm), f32) * 0.02,
        'norm_mix_g': 1.0 + 0.05 * nrm(ks[4], (DEPTH, Dm), f32),
        'w_in': nrm(ks[5], (DEPTH, Dm, N_IN), f32) * Dm ** -0.5,
        'lb_gamma_fwd': 0.1 * nrm(ks[6], (DEPTH + 1, D_HGRN), f32),
        'lb_gamma_bwd': 0.1 * nrm(ks[7], (DEPTH + 1, D_HGRN), f32),
        'hgrn_norm_g': 1.0 + 0.05 * nrm(ks[8], (DEPTH, D_HGRN), f32),
        'conv_w': nrm(ks[9], (DEPTH, CONV_WIDTH, D_CONV), f32) * CONV_WIDTH ** -0.5,
        'conv_b': 0.02 * nrm(ks[10], (DEPTH, D_CONV), f32),
        'conv_ln_g': 1.0 + 0.05 * nrm(ks[11], (DEPTH, D_CONV), f32),
        'conv_ln_b': 0.02 * nrm(ks[12], (DEPTH, D_CONV), f32),
        'w_out': nrm(ks[13], (DEPTH, D_MIX, Dm), f32) * D_MIX ** -0.5,
        'norm_ffn_g': 1.0 + 0.05 * nrm(ks[14], (DEPTH, Dm), f32),
        'peer_wq': nrm(ks[15], (DEPTH, Dm, PEER_HEADS * PEER_DKEY), f32) * Dm ** -0.5,
        'peer_keys1': nrm(ks[16], (DEPTH, PEER_KEYS, PEER_HALF), f32) * PEER_HALF ** -0.5,
        'peer_keys2': nrm(ks[17], (DEPTH, PEER_KEYS, PEER_HALF), f32) * PEER_HALF ** -0.5,
        'peer_u': nrm(ks[18], (DEPTH, PEER_EXPERTS, Dm), f32) * Dm ** -0.5,
        'peer_v': nrm(ks[19], (DEPTH, PEER_EXPERTS, Dm), f32),
        'final_ada_w': nrm(ks[20], (Dm, 2 * Dm), f32) * (0.5 * Dm ** -0.5),
        'final_ada_b': 0.02 * nrm(ks[21], (2 * Dm,), f32),
        'final_norm_g': 1.0 + 0.05 * nrm(ks[22], (Dm,), f32),
    }

def reference(x, c, ada_w, ada_b, norm_mix_g, w_in, lb_gamma_fwd, lb_gamma_bwd, hgrn_norm_g,
              conv_w, conv_b, conv_ln_g, conv_ln_b, w_out, norm_ffn_g, peer_wq, peer_keys1,
              peer_keys2, peer_u, peer_v, final_ada_w, final_ada_b, final_norm_g):
    c_act = jax.nn.silu(c)
    lb_fwd_all = jnp.cumsum(jax.nn.softmax(lb_gamma_fwd.astype(jnp.float32), axis=0), axis=0)
    lb_bwd_all = jnp.cumsum(jax.nn.softmax(lb_gamma_bwd.astype(jnp.float32), axis=0), axis=0)
    splits = [D_HGRN, 2 * D_HGRN, 3 * D_HGRN, 4 * D_HGRN, 5 * D_HGRN, 5 * D_HGRN + D_CONV]
    h = x
    for l in range(DEPTH):
        mod = c_act @ ada_w[l] + ada_b[l]
        sh1, sc1, g1, sh2, sc2, g2 = jnp.split(mod, 6, axis=-1)
        hn = _modulate(_rmsnorm(h, norm_mix_g[l]), sh1, sc1)
        proj = hn @ w_in[l]
        q_r, ff_r, fb_r, i_r, g_r, c_a, c_g = jnp.split(proj, splits, axis=-1)
        o_h = _hgrn2(q_r, ff_r, fb_r, i_r, g_r, lb_fwd_all[l], lb_bwd_all[l], hgrn_norm_g[l])
        o_c = _conv_module(c_a, c_g, conv_w[l], conv_b[l], conv_ln_g[l], conv_ln_b[l])
        mix = jnp.concatenate([o_h, o_c], axis=-1) @ w_out[l]
        h = h + g1[:, None, :] * mix
        hn2 = _modulate(_rmsnorm(h, norm_ffn_g[l]), sh2, sc2)
        ffn = _peer(hn2, peer_wq[l], peer_keys1[l], peer_keys2[l], peer_u[l], peer_v[l])
        h = h + g2[:, None, :] * ffn
    fsh, fsc = jnp.split(c_act @ final_ada_w + final_ada_b, 2, axis=-1)
    return _modulate(_rmsnorm(h, final_norm_g), fsh, fsc)


_drawn_inputs = setup_inputs


def setup_inputs(seed=0):
    import zlib

    import numpy as np

    out = dict(_drawn_inputs(seed))
    spreads = {}
    factors = {'norm_mix_g': 2.798,
     'lb_gamma_fwd': 8.0,
     'lb_gamma_bwd': 8.0,
     'hgrn_norm_g': 3.813,
     'conv_b': 16.163,
     'conv_ln_g': 11.946,
     'conv_ln_b': 29.683,
     'norm_ffn_g': 3.073}
    for name, (base, spread) in spreads.items():
        noise = np.random.default_rng([zlib.crc32(name.encode()), seed]).standard_normal(out[name].shape)
        drawn = base * np.exp(spread * noise) if base else spread * noise
        out[name] = __import__('jax').numpy.asarray(drawn.astype(out[name].dtype))
    for name, factor in factors.items():
        out[name] = (out[name] * factor).astype(out[name].dtype)
    return out
```

```python
from contextlib import ExitStack

import numpy as np

import concourse.bass as bass
from concourse import mybir

F32 = mybir.dt.float32
F32R = mybir.dt.float32r
U32 = mybir.dt.uint32
I32 = mybir.dt.int32
ALU = mybir.AluOpType
ACT = mybir.ActivationFunctionType
AX = mybir.AxisListType

P = 128
T = 1024
D = 1024
DC = D // P
HALF = 512
HEADS = 4
CHUNK = 64
NCH = T // CHUNK
CONV_W = 31
PAD = CONV_W // 2
CONV_C = 4
DCONV = CONV_C * P
PROJ_HEAD = 5
PH = 8
KEYS = 128
TOPK = 16
NB = T // P
EPS = 1e-6
LOWEST = -3.0e38

COL = {}
_at = 0
for _name, _n in (("mod_b", 64), ("g_mix", 8), ("g_ffn", 8), ("g_fin", 8), ("c", 8), ("g_hgrn", 4),
                  ("conv_b", 4), ("ln_g", 4), ("ln_b", 4), ("gam_f", 8), ("gam_b", 8),
                  ("conv_w", 4 * CONV_W)):
    COL[_name] = (_at, _at + _n)
    _at += _n
NCOL = _at

KB = 1024
BASE = 16512
R0 = BASE
F0 = BASE + 128 * KB
C0 = F0 + 72 * KB
CB = 7 * KB


class Mem:
    pass


def rev(ap, back):
    return ap[:, ::-1] if back else ap


def constants(nc, m, io, sem):
    dma = sem("cols_in")
    with nc.Block() as block:

        @block.sync
        def _(sp):
            sp.dma_start(m.cols[:, :], io["cols"]).then_inc(dma, 16)
            sp.dma_start(m.keysT[:, :, :], io["keysT"]).then_inc(dma, 16)
            sp.wait_ge(dma, 32)

        @block.gpsimd
        def _(pool):
            pool.memset(m.ones[:, :], 1.0)
            pool.memset(m.ident[:, :], 0.0)
            pool.iota(m.iota[:, :], [[1, KEYS]], base=0, channel_multiplier=0,
                      allow_small_or_imprecise_dtypes=True)
            pool.memset(m.mask[:, :, :], 1)
            pool.drain()
            pool.affine_select(out=m.ident[:, :], in_=m.ident[:, :], compare_op=ALU.not_equal, fill=1.0,
                               base=0, pattern=[[-1, P]], channel_multiplier=1)
            for back in range(2):
                sg = -1 if back else 1
                pool.affine_select(out=m.mask[:, back, :], in_=m.mask[:, back, :], compare_op=ALU.is_ge,
                                   fill=0, base=0, pattern=[[sg, P]], channel_multiplier=-sg)
            pool.drain()
            pool.memset(m.mask[0:CHUNK, :, CHUNK:P], 0)
            pool.memset(m.mask[CHUNK:P, :, 0:CHUNK], 0)
            pool.drain()


def step1(nc, m, io, sem):
    A_SLOTS, A_PER = 4, 2
    at = m.at
    x = at("s1_x", [P, DC, T], F32, F0)
    ada = at("s1_ada", [P, A_SLOTS, A_PER, DC, P], F32, R0 + 64 * KB)
    sq = at("s1_sq", [P, 2, T], F32, F0 + 32 * KB)
    xn = at("s1_xn", [P, 2, T], F32, F0 + 40 * KB)
    r = at("s1_r", [P, T], F32, F0 + 48 * KB)
    y = at("s1_y", [P, 2, T], F32, F0 + 52 * KB)
    cact = at("s1_cact", [P, DC], F32, F0 + 60 * KB)
    lbt = at("s1_lbt", [P, 8, HEADS], F32, F0 + 61 * KB)
    col = m.col
    ctx = ExitStack()
    with ctx:
        ps_mod = ctx.enter_context(nc.psum_tensor("s1_mod", [P, 64], F32))
        ps_ss = ctx.enter_context(nc.psum_tensor("s1_ss", [P, T], F32))
        x_in = [sem(f"s1_x_in{k}") for k in range(DC)]
        ada_in = [sem(f"s1_ada_in{k}") for k in range(A_SLOTS)]
        ada_used, cact_done, sq_ready, sq_used = sem("s1_ada_used"), sem("s1_cact"), sem("s1_sq_r"), sem("s1_sq_u")
        ss_ready, inv_ready, r_ready, mod_ready = sem("s1_ss"), sem("s1_inv"), sem("s1_r_s"), sem("s1_mod_r")
        y_ready, hi_ready, lo_ready, lbe, lbx = sem("s1_y_r"), sem("s1_hi"), sem("s1_lo"), sem("s1_lbe"), sem("s1_lbx")
        block = ctx.enter_context(nc.Block())

        @block.sync
        def _(sp):
            for k in range(DC):
                sp.dma_start(x[:, k, :], io["xT"][k]).then_inc(x_in[k], 16)
            with sp.Fori(0, 64 // (A_SLOTS * A_PER)) as it:
                for s in range(A_SLOTS):
                    sp.wait_ge(ada_used, it * A_SLOTS + s + 1)
                    sp.dma_start(ada[:, s], io["ada"][bass.ds(it * A_SLOTS + s, 1)]
                                 .rearrange("a p c k m -> p (a c) k m")).then_inc(ada_in[s], 16)

        @block.scalar
        def _(act):
            act.activation(cact[:, :], col("c"), ACT.Silu).then_inc(cact_done, 1)
            for k in range(DC):
                act.wait_ge(x_in[k], 16)
                if k >= 2:
                    act.wait_ge(sq_used, k - 1)
                act.activation(sq[:, k % 2, :], x[:, k, :], ACT.Square).then_inc(sq_ready, 1)
            act.wait_ge(lbx, 1)
            act.activation(lbt[:, 4:8, :], lbt[:, 0:4, :], ACT.Exp).then_inc(lbe, 1)
            act.wait_ge(inv_ready, 1)
            act.activation(r[:, :], r[:, :], ACT.Sqrt).then_inc(r_ready, 1)
            for k in range(DC):
                act.wait_ge(y_ready, k + 1)
                act.activation(m.hn_hi[:, k, :], y[:, k % 2, :], ACT.Copy).then_inc(hi_ready, 1)

        @block.gpsimd
        def _(pool):
            for k in range(DC):
                pool.wait_ge(hi_ready, k + 1)
                pool.tensor_tensor(m.hn_lo[:, k, :], y[:, k % 2, :], m.hn_hi[:, k, :].bitcast(F32),
                                   ALU.subtract).then_inc(lo_ready, 1)

        @block.tensor
        def _(pe):
            pe.sem_inc(ada_used, A_SLOTS)
            for k in range(DC):
                pe.wait_ge(sq_ready, k + 1)
                for h in range(2):
                    mm = pe.matmul(ps_ss[:, h * HALF:(h + 1) * HALF], m.ones[:, :],
                                   sq[:, k % 2, h * HALF:(h + 1) * HALF], start=(k == 0), stop=(k == DC - 1))
                mm.then_inc(sq_used, 1)
            mm2 = pe.drain()
            mm2.then_inc(ss_ready, 1)
            pe.wait_ge(cact_done, 1)
            with pe.Fori(0, 64 // (A_SLOTS * A_PER)) as it:
                for s in range(A_SLOTS):
                    pe.wait_ge(ada_in[s], it * 16 + 16)
                    for c in range(A_PER):
                        for k in range(DC):
                            mm = pe.matmul(ps_mod[:, bass.ds((it * A_SLOTS + s) * A_PER + c, 1)],
                                           ada[:, s, c, k, :], cact[:, k:k + 1], start=(k == 0), stop=(k == DC - 1))
                    mm.then_inc(ada_used, 1)
            pe.drain().then_inc(mod_ready, 1)

        @block.vector
        def _(dve):
            gam = m.cols[:, COL["gam_f"][0]:COL["gam_b"][1]].rearrange("p (d l h) -> p d l h", d=2, l=2)
            for d in range(2):
                dve.tensor_tensor(lbt[:, 4 + d, :], gam[:, d, 0, :], gam[:, d, 1, :], ALU.max)
            dve.drain()
            for d in range(2):
                for l in range(2):
                    dve.tensor_tensor(lbt[:, 2 * d + l, :], gam[:, d, l, :], lbt[:, 4 + d, :], ALU.subtract)
            dve.drain().then_inc(lbx, 1)
            dve.wait_ge(ss_ready, 1)
            dve.tensor_scalar(r[:, :], ps_ss[:, :], 1.0 / D, EPS, ALU.mult, ALU.add)
            dve.drain()
            dve.reciprocal(r[:, :], r[:, :]).then_inc(inv_ready, 1)
            dve.wait_ge(lbe, 1)
            for d in range(2):
                dve.tensor_tensor(lbt[:, d, :], lbt[:, 4 + 2 * d, :], lbt[:, 5 + 2 * d, :], ALU.add)
            dve.drain()
            dve.reciprocal(lbt[:, 2:4, :], lbt[:, 0:2, :])
            dve.drain()
            for d in range(2):
                dve.tensor_tensor(m.lb[:, d, :], lbt[:, 4 + 2 * d, :], lbt[:, 2 + d, :], ALU.mult)
            dve.drain()
            dve.tensor_scalar(m.omlb[:, :, :], m.lb[:, :, :], -1.0, 1.0, ALU.mult, ALU.add)
            dve.wait_ge(mod_ready, 1)
            dve.tensor_tensor(m.mods[:, :, :], ps_mod[:, :].rearrange("p (v k) -> p v k", v=8),
                              col("mod_b").rearrange("p (v k) -> p v k", v=8), ALU.add)
            dve.drain()
            for v, g in ((1, "g_mix"), (4, "g_ffn"), (7, "g_fin")):
                dve.scalar_tensor_tensor(m.mods[:, v, :], m.mods[:, v, :], 1.0, col(g), ALU.add, ALU.mult)
            dve.drain()
            dve.wait_ge(r_ready, 1)
            for k in range(DC):
                dve.tensor_tensor(xn[:, k % 2, :], x[:, k, :], r[:, :], ALU.mult)
                dve.drain()
                if k >= 2:
                    dve.wait_ge(lo_ready, k - 1)
                dve.tensor_scalar(y[:, k % 2, :], xn[:, k % 2, :], m.mods[:, 1, k:k + 1],
                                  m.mods[:, 0, k:k + 1], ALU.mult, ALU.add).then_inc(y_ready, 1)


class Weights:

    def __init__(self, m, sem, name, raw_at, part_at):
        self.raw = [m.at(f"{name}_raw{s}", [P, DC, P], F32, raw_at + s * 4 * KB) for s in range(2)]
        self.hi = [m.at(f"{name}_hi{s}", [P, DC, P], F32R, part_at + s * 8 * KB) for s in range(2)]
        self.lo = [m.at(f"{name}_lo{s}", [P, DC, P], F32R, part_at + s * 8 * KB + 4 * KB) for s in range(2)]
        self.arrived = [sem(f"{name}_arrived{s}") for s in range(2)]
        self.rounded, self.split, self.used = sem(f"{name}_rounded"), sem(f"{name}_split"), sem(f"{name}_used")

    def load(self, sp, pair, s, src):
        sp.wait_ge(self.split, pair * 2 + s + 1)
        sp.dma_start(self.raw[s][:, :, :], src).then_inc(self.arrived[s], 16)

    def round(self, act, pair, s):
        act.wait_ge(self.arrived[s], pair * 16 + 16)
        act.wait_ge(self.used, pair * 2 + s + 1)
        act.activation(self.hi[s][:, :, :], self.raw[s][:, :, :], ACT.Copy).then_inc(self.rounded, 1)

    def remainder(self, pool, pair, s):
        pool.wait_ge(self.rounded, pair * 2 + s + 1)
        pool.tensor_tensor(self.lo[s][:, :, :], self.raw[s][:, :, :], self.hi[s][:, :, :].bitcast(F32),
                           ALU.subtract).then_inc(self.split, 1)

    def ready(self, pe, pair, s):
        pe.wait_ge(self.split, pair * 2 + s + 3)


def project(pe, out, w_hi, w_lo, x_hi, x_lo):
    for k in range(DC):
        for h in range(2):
            c = slice(h * HALF, (h + 1) * HALF)
            pe.matmul(out[:, c], w_hi[:, k, :], x_hi[:, k, c], start=(k == 0), stop=False)
            pe.matmul(out[:, c], w_hi[:, k, :], x_lo[:, k, c], start=False, stop=False)
        for h in range(2):
            c = slice(h * HALF, (h + 1) * HALF)
            mm = pe.matmul(out[:, c], w_lo[:, k, :], x_hi[:, k, c], start=False, stop=(k == DC - 1))
    return mm


def step2(nc, m, io, sem):
    at, col = m.at, m.col
    hp = at("s2_hp", [P, T + 2 * PAD], F32, F0)
    sig = at("s2_sig", [P, T], F32, F0 + 5 * KB)
    acc = at("s2_acc", [P, CONV_C, T], F32, F0 + 9 * KB)
    work = at("s2_work", [P, T], F32, F0 + 25 * KB)
    tap = at("s2_tap", [P, CONV_W + 1], F32, F0 + 29 * KB)
    r = at("s2_r", [P, T], F32, F0 + 30 * KB)
    sq = at("s2_sq", [P, 2, T], F32, F0 + 34 * KB)
    ctx = ExitStack()
    with ctx:
        w = Weights(m, sem, "s2w", F0 + 44 * KB, R0 + 64 * KB)
        ps = [ctx.enter_context(nc.psum_tensor(f"s2_ps{s}", [P, T], F32)) for s in range(2)]
        ps_mu = ctx.enter_context(nc.psum_tensor("s2_mu", [P, T], F32))
        ps_var = ctx.enter_context(nc.psum_tensor("s2_var", [P, T], F32))
        gate_ready, a_ready, sig_ready, glu_done = (sem(f"s2_{n}") for n in ("gate_r", "a_r", "sig_r", "glu"))
        conv_done, mu_ready, d_ready, sq_ready, sq_used = (sem(f"s2_{n}") for n in ("conv", "mu", "d", "sqr", "squ"))
        var_ready, inv_ready, r_ready, xr, stored = (sem(f"s2_{n}") for n in ("var", "inv", "r_s", "xr", "out"))
        block = ctx.enter_context(nc.Block())

        @block.sync
        def _(sp):
            with sp.Fori(0, CONV_C) as c:
                for s in range(2):
                    w.load(sp, c, s, io["w_in"][bass.ds(c * 2 + s, 1)].rearrange("a p k m -> p (a k) m"))

        @block.scalar
        def _(act):
            def sigmoid(c):
                act.wait_ge(gate_ready, c + 1)
                act.wait_ge(glu_done, c + 1)
                act.activation(sig[:, :], ps[0][:, :], ACT.Sigmoid).then_inc(sig_ready, 1)

            act.sem_inc(sig_ready, 1)
            w.round(act, 0, 0)
            w.round(act, 0, 1)
            with act.Fori(0, CONV_C - 1) as c:
                sigmoid(c)
                w.round(act, c + 1, 0)
                w.round(act, c + 1, 1)
            sigmoid(CONV_C - 1)
            for c in range(CONV_C):
                act.wait_ge(d_ready, c + 1)
                if c >= 2:
                    act.wait_ge(sq_used, c - 1)
                act.activation(sq[:, c % 2, :], acc[:, c, :], ACT.Square).then_inc(sq_ready, 1)
            act.wait_ge(inv_ready, 1)
            act.activation(r[:, :], r[:, :], ACT.Sqrt).then_inc(r_ready, 1)
            for c in range(CONV_C):
                act.wait_ge(xr, c + 1)
                lg, lb = COL["ln_g"][0] + c, COL["ln_b"][0] + c
                act.activation(acc[:, c, :], acc[:, c, :], ACT.Silu, scale=m.cols[:, lg:lg + 1],
                               bias=m.cols[:, lb:lb + 1])
                act.drain()
                act.dma_start(m.mix[HEADS + c], acc[:, c, :]).then_inc(stored, 16)
            act.wait_ge(stored, 16 * CONV_C)

        @block.gpsimd
        def _(pool):
            pool.sem_inc(w.split, 2)
            with pool.Fori(0, CONV_C) as c:
                for s in range(2):
                    w.remainder(pool, c, s)

        @block.tensor
        def _(pe):
            pe.sem_inc(w.used, 2)
            with pe.Fori(0, CONV_C) as c:
                w.ready(pe, c, 0)
                pe.wait_ge(sig_ready, c + 1)
                project(pe, ps[0], w.hi[0], w.lo[0], m.hn_hi, m.hn_lo).then_inc(w.used, 1)
                pe.drain().then_inc(gate_ready, 1)
                w.ready(pe, c, 1)
                pe.wait_ge(glu_done, c + 1)
                project(pe, ps[1], w.hi[1], w.lo[1], m.hn_hi, m.hn_lo).then_inc(w.used, 1)
                pe.drain().then_inc(a_ready, 1)
            for c in range(CONV_C):
                pe.wait_ge(conv_done, c + 1)
                for h in range(2):
                    mm = pe.matmul(ps_mu[:, h * HALF:(h + 1) * HALF], m.ones[:, :],
                                   acc[:, c, h * HALF:(h + 1) * HALF], start=(c == 0), stop=(c == CONV_C - 1))
            mm.then_inc(mu_ready, 1)
            for c in range(CONV_C):
                pe.wait_ge(sq_ready, c + 1)
                for h in range(2):
                    mm = pe.matmul(ps_var[:, h * HALF:(h + 1) * HALF], m.ones[:, :],
                                   sq[:, c % 2, h * HALF:(h + 1) * HALF], start=(c == 0), stop=(c == CONV_C - 1))
                mm.then_inc(sq_used, 1)
            pe.drain().then_inc(var_ready, 1)

        @block.vector
        def _(dve):
            dve.sem_inc(glu_done, 1)
            dve.memset(hp[:, 0:PAD], 0.0)
            dve.memset(hp[:, PAD + T:T + 2 * PAD], 0.0)
            cw = m.cols[:, COL["conv_w"][0]:COL["conv_w"][1]].rearrange("p (c k) -> p c k", c=CONV_C)
            with dve.Fori(0, CONV_C) as c:
                dve.tensor_copy(tap[:, 0:CONV_W], cw[:, bass.ds(c, 1), :])
                dve.tensor_copy(tap[:, CONV_W:CONV_W + 1], m.cols[:, bass.ds(c + COL["conv_b"][0], 1)])
                dve.wait_ge(sig_ready, c + 2)
                dve.wait_ge(a_ready, c + 1)
                dve.tensor_tensor(hp[:, PAD:PAD + T], ps[1][:, :], sig[:, :], ALU.mult).then_inc(glu_done, 1)
                dve.drain()
                dve.tensor_scalar(work[:, :], hp[:, 0:T], tap[:, 0:1], tap[:, CONV_W:CONV_W + 1], ALU.mult, ALU.add)
                for k in range(1, CONV_W):
                    dve.drain()
                    dst = work[:, :] if k < CONV_W - 1 else acc[:, bass.ds(c, 1), :].rearrange("p a t -> p (a t)")
                    dve.scalar_tensor_tensor(dst, hp[:, k:k + T], tap[:, k:k + 1], work[:, :], ALU.mult, ALU.add)
                dve.drain().then_inc(conv_done, 1)
            dve.wait_ge(mu_ready, 1)
            for c in range(CONV_C):
                dve.scalar_tensor_tensor(acc[:, c, :], ps_mu[:, :], -1.0 / DCONV, acc[:, c, :], ALU.mult, ALU.add)
                dve.drain().then_inc(d_ready, 1)
            dve.wait_ge(var_ready, 1)
            dve.tensor_scalar(r[:, :], ps_var[:, :], 1.0 / DCONV, EPS, ALU.mult, ALU.add)
            dve.drain()
            dve.reciprocal(r[:, :], r[:, :]).then_inc(inv_ready, 1)
            dve.wait_ge(r_ready, 1)
            for c in range(CONV_C):
                dve.tensor_tensor(acc[:, c, :], acc[:, c, :], r[:, :], ALU.mult).then_inc(xr, 1)


def step3(nc, m, io, sem):
    at = m.at
    W = 4 * KB
    f = [F0 + n * W for n in range(18)]
    low = [at(f"s3_low{d}", [P, T], F32, f[d]) for d in range(2)]
    kk = [at(f"s3_k{d}", [P, T], F32, f[2 + d]) for d in range(2)]
    q, vT, g = at("s3_q", [P, T], F32, f[4]), at("s3_vT", [P, T], F32, f[5]), at("s3_g", [P, T], F32, f[6])
    vtok = at("s3_vtok", [P, NB, P], F32, f[7])
    qe = [at(f"s3_qe{d}", [P, T], F32, f[8 + 4 * d]) for d in range(2)]
    ku = [at(f"s3_ku{d}", [P, T], F32, f[9 + 4 * d]) for d in range(2)]
    qr = [at(f"s3_qr{d}", [P, T], F32, f[10 + 4 * d]) for d in range(2)]
    kr = [at(f"s3_kr{d}", [P, T], F32, f[11 + 4 * d]) for d in range(2)]
    reset, o = at("s3_reset", [P, T], F32, f[16]), at("s3_o", [P, T], F32, f[17])
    e = R0 + 80 * KB
    state = [at(f"s3_state{d}", [P, NCH, P], F32, e + 8 * KB * d) for d in range(2)]
    st = [at(f"s3_st{d}", [P, NB, P], F32, e + 16 * KB + W * d) for d in range(2)]
    kt = [at(f"s3_kt{d}", [P, NB, P], F32, e + 24 * KB + W * d) for d in range(2)]
    sq = at("s3_sq", [P, T], F32, e + 24 * KB)
    r = at("s3_r", [P, T], F32, e + 28 * KB)
    dec = at("s3_dec", [P, 2, NCH], F32, e + 32 * KB)
    ctx = ExitStack()
    with ctx:
        w = Weights(m, sem, "s3w", e + 33 * KB, R0 + 64 * KB)
        ps = [ctx.enter_context(nc.psum_tensor(f"s3_ps{s}", [P, T], F32)) for s in range(2)]
        po = ctx.enter_context(nc.psum_tensor("s3_po", [P, T], F32))
        pm = [ctx.enter_context(nc.psum_tensor(f"s3_pm{s}", [P, HALF], F32)) for s in range(2)]
        const, proj, evac = sem("s3_const"), sem("s3_proj"), sem("s3_evac")
        k_ready = [sem(f"s3_k_r{d}") for d in range(2)]
        log_ready = [sem(f"s3_log{d}") for d in range(2)]
        prep = [sem(f"s3_prep{d}") for d in range(2)]
        powers = [sem(f"s3_pow{d}") for d in range(2)]
        ku_ready = [sem(f"s3_ku_r{d}") for d in range(2)]
        factors = [sem(f"s3_fac{d}") for d in range(2)]
        q_ready, v_ready, g_ready = sem("s3_q_r"), sem("s3_v_r"), sem("s3_g_r")
        v_turned, vtok_ready = sem("s3_vturn"), sem("s3_vtok_r")
        pm_ready = [sem(f"s3_pm_r{s}") for s in range(2)]
        pm_used = [sem(f"s3_pm_u{s}") for s in range(2)]
        o_ready, o_copied, sq_ready = sem("s3_o_r"), sem("s3_o_c"), sem("s3_sq_r")
        inv, root, done, stored = sem("s3_inv"), sem("s3_root"), sem("s3_done"), sem("s3_stored")
        block = ctx.enter_context(nc.Block())
        W0, NT = 2 * CONV_C, HEADS * PROJ_HEAD

        def allowed(quad, d):
            t0 = quad // 2 * CHUNK + (quad % 2 * 32 if d == 0 else 0)
            t1 = quad // 2 * CHUNK + (CHUNK if d == 0 else quad % 2 * 32 + 32)
            return slice(32 * quad, 32 * quad + 32), t0, t1

        def place(part, d, odd, i):
            first = odd if d == 0 else 1 - odd
            n = 4 * part + 2 * i + first
            return n, (NCH - 1 - n if d else n)

        @block.sync
        def _(sp):
            with sp.Fori(0, NT // 2) as n:
                for s in range(2):
                    w.load(sp, n, s, io["w_in"][bass.ds(n * 2 + W0 + s, 1)].rearrange("a p k m -> p (a k) m"))

        @block.gpsimd
        def _(pool):
            pool.sem_inc(w.split, 2)
            pool.memset(reset[:, :], 1.0)
            pool.drain()
            pool.memset(reset[:, 0::CHUNK], 0.0)
            for d in range(2):
                pool.memset(st[d][:, :, :], 0.0)
                pool.memset(state[d][:, 0, :], 0.0)
            pool.drain().then_inc(const, 1)
            with pool.Fori(0, NT // 2) as n:
                for s in range(2):
                    w.remainder(pool, n, s)

        @block.tensor
        def _(pe):
            def project_head(h):
                for n in range(PROJ_HEAD * h, PROJ_HEAD * (h + 1)):
                    w.ready(pe, n // 2, n % 2)
                    if n >= 2:
                        pe.wait_ge(evac, n - 1)
                    project(pe, ps[n % 2], w.hi[n % 2], w.lo[n % 2], m.hn_hi, m.hn_lo).then_inc(w.used, 1)
                    pe.drain().then_inc(proj, 1)

            def recurrence(h):
                count = [0, 0]

                def batch(i, make):
                    b = i % 2
                    if 9 * h + count[b]:
                        pe.wait_ge(pm_used[b], 9 * h + count[b])
                    count[b] += 1
                    for j in range(4):
                        mm = make(pm[b][:, j * P:(j + 1) * P], j)
                    mm.then_inc(pm_ready[b], 1)

                pe.wait_ge(v_ready, h + 1)
                if h:
                    pe.wait_ge(o_copied, h)
                    pe.wait_ge(sq_ready, h)
                for b in range(NB):
                    mm = pe.transpose(po[:, b * P:(b + 1) * P], vT[:, b * P:(b + 1) * P], m.ident[:, :])
                mm.then_inc(v_turned, 1)
                for d in range(2):
                    pe.wait_ge(ku_ready[d], h + 1)
                    for half in range(2):
                        batch(half, lambda out, j: pe.transpose(
                            out, ku[d][:, (4 * half + j) * P:(4 * half + j + 1) * P], m.ident[:, :]))
                for d in range(2):
                    pe.wait_ge(factors[d], h + 1)
                    for half in range(2):
                        def scores(out, j):
                            c = (4 * half + j) * P
                            for quad in range(4):
                                rows, t0, t1 = allowed(quad, d)
                                mm = pe.matmul(out[rows, t0:t1], kr[d][:, c + 32 * quad:c + 32 * quad + 32],
                                               qr[d][:, c + t0:c + t1], start=True, stop=True)
                            return mm
                        batch(half, scores)
                pe.wait_ge(vtok_ready, h + 1)
                for part in range(4):
                    for odd in range(2):
                        def products(out, j):
                            d = j // 2
                            n, c = place(part, d, odd, j % 2)
                            rows = slice(odd * CHUNK, (odd + 1) * CHUNK)
                            return pe.matmul(out, kt[d][rows, c // 2, :], vtok[rows, c // 2, :], start=True, stop=True)
                        batch(odd, products)
                for b in range(2):
                    pe.wait_ge(pm_used[b], 9 * h + 8)
                for b in range(NB):
                    c = slice(b * P, (b + 1) * P)
                    pe.matmul(po[:, c], vtok[:, b, :], st[0][:, b, :], start=True, stop=False)
                    pe.matmul(po[:, c], vtok[:, b, :], st[1][:, b, :], start=False, stop=False)
                    for n in (2 * b, 2 * b + 1):
                        t = slice(n * CHUNK, (n + 1) * CHUNK)
                        pe.matmul(po[:, t], state[0][:, n, :], qe[0][:, t], start=False, stop=False)
                        mm = pe.matmul(po[:, t], state[1][:, NCH - 1 - n, :], qe[1][:, t], start=False, stop=(n % 2 == 1))
                mm.then_inc(o_ready, 1)
                pe.wait_ge(sq_ready, h + 1)
                for b in range(2):
                    pe.matmul(pm[b][:, :], m.ones[:, :], sq[:, b * HALF:(b + 1) * HALF],
                              start=True, stop=True).then_inc(pm_ready[b], 1)

            pe.sem_inc(w.used, 2)
            project_head(0)
            for h in range(HEADS):
                if h + 1 < HEADS:
                    project_head(h + 1)
                recurrence(h)

        @block.scalar
        def _(act):
            def round_tile(n):
                if n < NT:
                    w.round(act, n // 2, n % 2)

            def forget(h, d):
                n = PROJ_HEAD * h + d
                act.wait_ge(proj, n + 1)
                if h:
                    act.wait_ge(factors[d], h)
                act.activation(low[d][:, :], ps[n % 2][:, :], ACT.Sigmoid)
                act.activation(kk[d][:, :], ps[n % 2][:, :], ACT.Sigmoid, scale=-1.0)
                act.drain().then_inc(k_ready[d], 1)
                act.sem_inc(evac, 1)

            def query(h):
                n = PROJ_HEAD * h + 2
                act.wait_ge(proj, n + 1)
                if h:
                    act.wait_ge(factors[1], h)
                act.activation(q[:, :], ps[n % 2][:, :], ACT.Silu)
                act.drain().then_inc(q_ready, 1)
                act.sem_inc(evac, 1)

            def value(h):
                n = PROJ_HEAD * h + 3
                act.wait_ge(proj, n + 1)
                if h:
                    act.wait_ge(v_turned, h)
                act.activation(vT[:, :], ps[n % 2][:, :], ACT.Copy)
                act.drain().then_inc(v_ready, 1)
                act.sem_inc(evac, 1)

            def gate(h):
                n = PROJ_HEAD * h + 4
                act.wait_ge(proj, n + 1)
                if h:
                    act.wait_ge(done, h)
                act.activation(g[:, :], ps[n % 2][:, :], ACT.Silu)
                act.drain().then_inc(g_ready, 1)
                act.sem_inc(evac, 1)

            def power(h, d):
                act.wait_ge(prep[d], h + 1)
                last = CHUNK - 1 if d == 0 else 0
                act.activation(ku[d][:, :], ku[d][:, :], ACT.Exp)
                act.activation(kr[d][:, :], qr[d][:, :], ACT.Exp, scale=-1.0)
                act.activation(dec[:, d, :], qe[d][:, last::CHUNK], ACT.Exp)
                act.drain()
                act.activation(qr[d][:, :], qr[d][:, :], ACT.Exp)
                act.activation(qe[d][:, :], qe[d][:, :], ACT.Exp)
                act.drain().then_inc(powers[d], 1)

            for n in range(2):
                round_tile(n)
            for c, take in enumerate((lambda: forget(0, 0), lambda: forget(0, 1), lambda: query(0), lambda: value(0))):
                round_tile(2 + c)
                take()
            round_tile(6)
            for h in range(HEADS):
                t = PROJ_HEAD * (h + 1)
                nxt = h + 1 < HEADS
                for d in range(2):
                    act.activation(low[d][:, :], low[d][:, :], ACT.Ln, scale=m.omlb[:, d, h:h + 1],
                                   bias=m.lb[:, d, h:h + 1])
                    act.drain().then_inc(log_ready[d], 1)
                gate(h)
                power(h, 0)
                round_tile(t + 2) if nxt else None
                power(h, 1)
                if nxt:
                    forget(h + 1, 0)
                    round_tile(t + 3)
                    forget(h + 1, 1)
                    round_tile(t + 4)
                    query(h + 1)
                act.wait_ge(v_turned, h + 1)
                act.activation(vtok[:, :, :], po[:, :].rearrange("p (b v) -> p b v", b=NB), ACT.Copy)
                act.drain().then_inc(vtok_ready, 1)
                if nxt:
                    value(h + 1)
                for d in range(2):
                    for half in range(2):
                        act.wait_ge(pm_ready[half], 9 * h + d + 1)
                        act.activation(kt[d][:, 4 * half:4 * half + 4, :],
                                       pm[half][:, :].rearrange("p (b v) -> p b v", b=4), ACT.Copy)
                        act.drain().then_inc(pm_used[half], 1)
                if nxt:
                    round_tile(t + 5)
                    round_tile(t + 6)
                act.wait_ge(o_copied, h + 1)
                act.activation(sq[:, :], o[:, :], ACT.Square)
                act.drain().then_inc(sq_ready, 1)
                act.wait_ge(inv, h + 1)
                act.activation(r[:, :], r[:, :], ACT.Sqrt)
                act.drain().then_inc(root, 1)
                act.wait_ge(done, h + 1)
                act.dma_start(m.mix[h], o[:, :]).then_inc(stored, 16)
            act.wait_ge(stored, 16 * HEADS)

        @block.vector
        def _(dve):
            chunks = lambda ap: ap.rearrange("p (n c) -> p n c", c=CHUNK)
            for h in range(HEADS):
                for d in range(2):
                    mid, last = (CHUNK // 2 - 1, CHUNK - 1) if d == 0 else (CHUNK // 2, 0)
                    dve.wait_ge(k_ready[d], h + 1)
                    dve.tensor_scalar(kk[d][:, :], kk[d][:, :], m.omlb[:, d, h:h + 1], None, ALU.mult)
                    if h:
                        dve.wait_ge(o_ready, h)
                    elif d == 0:
                        dve.wait_ge(const, 1)
                    dve.wait_ge(log_ready[d], h + 1)
                    dve.tensor_tensor_scan(rev(qe[d][:, :], d), reset[:, :], rev(low[d][:, :], d), 0.0,
                                           ALU.mult, ALU.add)
                    dve.drain()
                    b = chunks(qe[d][:, :])
                    spread = lambda i: b[:, :, i:i + 1].broadcast_to([P, NCH, CHUNK])
                    dve.tensor_tensor(chunks(qr[d][:, :]), b, spread(mid), ALU.subtract)
                    dve.tensor_tensor(chunks(ku[d][:, :]), spread(last), b, ALU.subtract)
                    dve.drain().then_inc(prep[d], 1)
                dve.wait_ge(q_ready, h + 1)
                for d in range(2):
                    dve.wait_ge(powers[d], h + 1)
                    dve.tensor_tensor(ku[d][:, :], ku[d][:, :], kk[d][:, :], ALU.mult).then_inc(ku_ready[d], 1)
                    dve.tensor_tensor(kr[d][:, :], kr[d][:, :], kk[d][:, :], ALU.mult)
                    dve.tensor_tensor(qr[d][:, :], qr[d][:, :], q[:, :], ALU.mult)
                    dve.tensor_tensor(qe[d][:, :], qe[d][:, :], q[:, :], ALU.mult)
                    dve.drain().then_inc(factors[d], 1)
                for d in range(2):
                    for half in range(2):
                        dve.wait_ge(pm_ready[half], 9 * h + 3 + d)
                        for quad in range(4):
                            rows, t0, t1 = allowed(quad, d)
                            mask = m.mask[rows, d:d + 1, t0:t1].broadcast_to([32, 4, t1 - t0])
                            dve.copy_predicated(st[d][rows, 4 * half:4 * half + 4, t0:t1], mask,
                                                pm[half][rows, :].rearrange("p (b t) -> p b t", b=4)[:, :, t0:t1])
                        dve.drain().then_inc(pm_used[half], 1)
                for part in range(4):
                    for odd in range(2):
                        dve.wait_ge(pm_ready[odd], 9 * h + 5 + part)
                    for j in range(4):
                        for d in range(2):
                            n = 4 * part + j
                            c = NCH - 1 - n if d else n
                            if n < NCH - 1:
                                slot = 2 * d + j // 2
                                dve.scalar_tensor_tensor(state[d][:, n + 1, :], state[d][:, n, :], dec[:, d, c:c + 1],
                                                         pm[c % 2][:, slot * P:(slot + 1) * P], ALU.mult, ALU.add)
                        dve.drain()
                    for odd in range(2):
                        dve.drain().then_inc(pm_used[odd], 1)
                dve.wait_ge(o_ready, h + 1)
                if h:
                    dve.wait_ge(stored, 16 * h)
                dve.tensor_copy(o[:, :], po[:, :])
                dve.drain().then_inc(o_copied, 1)
                for b in range(2):
                    dve.wait_ge(pm_ready[b], 9 * h + 9)
                    dve.tensor_scalar(r[:, b * HALF:(b + 1) * HALF], pm[b][:, :], 1.0 / P, EPS, ALU.mult, ALU.add)
                    dve.drain().then_inc(pm_used[b], 1)
                dve.reciprocal(r[:, :], r[:, :])
                dve.drain().then_inc(inv, 1)
                dve.wait_ge(root, h + 1)
                dve.wait_ge(g_ready, h + 1)
                dve.tensor_tensor(o[:, :], o[:, :], r[:, :], ALU.mult)
                dve.drain()
                gain = COL["g_hgrn"][0] + h
                dve.scalar_tensor_tensor(o[:, :], o[:, :], m.cols[:, gain:gain + 1], g[:, :], ALU.mult, ALU.mult)
                dve.drain().then_inc(done, 1)


def step4(nc, m, io, sem):
    at = m.at
    h1 = at("s4_h1", [P, DC, T], F32, F0)
    raw = at("s4_raw", [P, 2, T], F32, F0 + 32 * KB)
    x = at("s4_x", [P, 2, T], F32, F0 + 40 * KB)
    sq = at("s4_sq", [P, 2, T], F32, F0 + 56 * KB)
    r = at("s4_r", [P, T], F32, F0 + 64 * KB)
    xn = at("s4_xn", [P, T], F32, F0 + 68 * KB)
    ctx = ExitStack()
    with ctx:
        w = Weights(m, sem, "s4w", F0 + 48 * KB, R0 + 64 * KB)
        ps = [ctx.enter_context(nc.psum_tensor(f"s4_ps{s}", [P, T], F32)) for s in range(2)]
        ps_ss = ctx.enter_context(nc.psum_tensor("s4_ss", [P, T], F32))
        raw_in = [sem(f"s4_raw_in{s}") for s in range(2)]
        x_in = [sem(f"s4_x_in{s}") for s in range(2)]
        mix_hi, mix_lo, made, h1_ready, sq_ready, sq_used = (sem(f"s4_{n}") for n in ("mhi", "mlo", "made", "h1r", "sqr", "squ"))
        ss_ready, inv, root, y_ready, y_hi, y_lo, stored = (sem(f"s4_{n}") for n in ("ss", "inv", "root", "yr", "yhi", "ylo", "st"))
        block = ctx.enter_context(nc.Block())

        @block.sync
        def _(sp):
            for k in range(DC):
                if k < 2:
                    w.load(sp, 0, k, io["w_out"][k])
                if k >= 2:
                    sp.wait_ge(mix_lo, k - 1)
                sp.dma_start(raw[:, k % 2, :], m.mix[k]).then_inc(raw_in[k % 2], 16)
            for k in range(DC):
                if k >= 2:
                    w.load(sp, k // 2, k % 2, io["w_out"][k])
                    sp.wait_ge(h1_ready, k - 1)
                sp.dma_start(x[:, k % 2, :], io["xT"][k]).then_inc(x_in[k % 2], 16)
            for k in range(DC):
                sp.wait_ge(h1_ready, k + 1)
                sp.dma_start(m.h1[k], h1[:, k, :]).then_inc(stored, 16)
            sp.wait_ge(stored, 16 * DC)

        @block.scalar
        def _(act):
            for k in range(DC):
                act.wait_ge(raw_in[k % 2], 16 * (k // 2 + 1))
                act.activation(m.hn_hi[:, k, :], raw[:, k % 2, :], ACT.Copy).then_inc(mix_hi, 1)
                if k < 2:
                    w.round(act, 0, k)
            for k in range(DC):
                if k + 2 < DC:
                    w.round(act, (k + 2) // 2, k % 2)
                act.wait_ge(h1_ready, k + 1)
                if k >= 2:
                    act.wait_ge(sq_used, k - 1)
                act.activation(sq[:, k % 2, :], h1[:, k, :], ACT.Square).then_inc(sq_ready, 1)
            act.wait_ge(inv, 1)
            act.activation(r[:, :], r[:, :], ACT.Sqrt).then_inc(root, 1)
            for k in range(DC):
                act.wait_ge(y_ready, k + 1)
                act.activation(m.hn_hi[:, k, :], raw[:, k % 2, :], ACT.Copy).then_inc(y_hi, 1)

        @block.gpsimd
        def _(pool):
            pool.sem_inc(w.split, 2)
            for k in range(DC):
                pool.wait_ge(mix_hi, k + 1)
                pool.tensor_tensor(m.hn_lo[:, k, :], raw[:, k % 2, :], m.hn_hi[:, k, :].bitcast(F32),
                                   ALU.subtract).then_inc(mix_lo, 1)
                if k < 2:
                    w.remainder(pool, 0, k)
            for k in range(2, DC):
                w.remainder(pool, k // 2, k % 2)
            for k in range(DC):
                pool.wait_ge(y_hi, k + 1)
                pool.tensor_tensor(m.hn_lo[:, k, :], raw[:, k % 2, :], m.hn_hi[:, k, :].bitcast(F32),
                                   ALU.subtract).then_inc(y_lo, 1)

        @block.tensor
        def _(pe):
            def sums(k):
                pe.wait_ge(sq_ready, k + 1)
                for h in range(2):
                    mm = pe.matmul(ps_ss[:, h * HALF:(h + 1) * HALF], m.ones[:, :],
                                   sq[:, k % 2, h * HALF:(h + 1) * HALF], start=(k == 0), stop=(k == DC - 1))
                mm.then_inc(sq_used, 1)

            pe.sem_inc(w.used, 2)
            pe.wait_ge(mix_lo, DC)
            for k in range(DC):
                w.ready(pe, k // 2, k % 2)
                if k >= 2:
                    pe.wait_ge(h1_ready, k - 1)
                project(pe, ps[k % 2], w.hi[k % 2], w.lo[k % 2], m.hn_hi, m.hn_lo).then_inc(w.used, 1)
                pe.drain().then_inc(made, 1)
                if k:
                    sums(k - 1)
            sums(DC - 1)
            pe.drain().then_inc(ss_ready, 1)

        @block.vector
        def _(dve):
            for k in range(DC):
                dve.wait_ge(made, k + 1)
                dve.wait_ge(x_in[k % 2], 16 * (k // 2 + 1))
                dve.scalar_tensor_tensor(h1[:, k, :], ps[k % 2][:, :], m.mods[:, 2, k:k + 1], x[:, k % 2, :],
                                         ALU.mult, ALU.add).then_inc(h1_ready, 1)
            dve.wait_ge(ss_ready, 1)
            dve.tensor_scalar(r[:, :], ps_ss[:, :], 1.0 / D, EPS, ALU.mult, ALU.add)
            dve.drain()
            dve.reciprocal(r[:, :], r[:, :]).then_inc(inv, 1)
            dve.wait_ge(root, 1)
            for k in range(DC):
                dve.tensor_tensor(xn[:, :], h1[:, k, :], r[:, :], ALU.mult)
                dve.drain()
                if k >= 2:
                    dve.wait_ge(y_lo, k - 1)
                dve.tensor_scalar(raw[:, k % 2, :], xn[:, :], m.mods[:, 4, k:k + 1], m.mods[:, 3, k:k + 1],
                                  ALU.mult, ALU.add)
                dve.drain().then_inc(y_ready, 1)


def step5(nc, m, io, sem):
    at = m.at
    q = [at(f"s5_q{s}", [P, T], F32, F0 + s * 4 * KB) for s in range(2)]
    sc = [at(f"s5_sc{s}", [P, NB, KEYS], F32, F0 + 8 * KB + s * 4 * KB) for s in range(2)]
    ctx = ExitStack()
    with ctx:
        w = Weights(m, sem, "s5w", F0 + 16 * KB, R0 + 64 * KB)
        ps = [ctx.enter_context(nc.psum_tensor(f"s5_ps{s}", [P, T], F32)) for s in range(2)]
        pk = [ctx.enter_context(nc.psum_tensor(f"s5_pk{s}", [P, T], F32)) for s in range(2)]
        made, q_ready, sc_made, sc_taken = (sem(f"s5_{n}") for n in ("made", "qr", "scm", "sct"))
        stored = [sem(f"s5_stored{s}") for s in range(2)]
        block = ctx.enter_context(nc.Block())

        @block.sync
        def _(sp):
            with sp.Fori(0, PH) as h:
                for s in range(2):
                    w.load(sp, h, s, io["wq"][bass.ds(h * 2 + s, 1)].rearrange("a p k m -> p (a k) m"))

        @block.gpsimd
        def _(pool):
            pool.sem_inc(w.split, 2)
            with pool.Fori(0, PH) as h:
                for s in range(2):
                    w.remainder(pool, h, s)

        def scores(pe, h, s):
            pe.wait_ge(q_ready, h * 2 + s + 3)
            pe.wait_ge(sc_taken, h * 2 + s + 1)
            for b in range(NB):
                mm = pe.matmul(pk[s][:, b * P:(b + 1) * P], q[s][:, b * P:(b + 1) * P], m.keysT[:, s, :],
                               start=True, stop=True)
            mm.then_inc(sc_made, 1)

        @block.tensor
        def _(pe):
            pe.sem_inc(w.used, 2)
            pe.sem_inc(q_ready, 2)
            with pe.Fori(0, PH) as h:
                for s in range(2):
                    w.ready(pe, h, s)
                    pe.wait_ge(q_ready, h * 2 + s + 1)
                    project(pe, ps[s], w.hi[s], w.lo[s], m.hn_hi, m.hn_lo).then_inc(w.used, 1)
                    pe.drain().then_inc(made, 1)
                    if s:
                        scores(pe, h, 0)
                scores(pe, h, 1)

        @block.scalar
        def _(act):
            w.round(act, 0, 0)
            w.round(act, 0, 1)

            def query(h, s, again=True):
                act.wait_ge(made, h * 2 + s + 1)
                if again:
                    act.wait_ge(sc_made, h * 2 + s - 1)
                act.activation(q[s][:, :], ps[s][:, :], ACT.Copy).then_inc(q_ready, 1)

            def store(h, s):
                act.wait_ge(sc_taken, h * 2 + s + 3)
                act.dma_start(m.scores[:, :, bass.ds(h * 2 + s, 1), :].rearrange("b p c k -> p (b c) k"),
                              sc[s][:, :, :]).then_inc(stored[s], 16)

            query(0, 0, again=False)
            w.round(act, 1, 0)
            query(0, 1, again=False)
            w.round(act, 1, 1)
            store(0, 0)
            store(0, 1)
            with act.Fori(1, PH - 1) as h:
                query(h, 0)
                w.round(act, h + 1, 0)
                query(h, 1)
                w.round(act, h + 1, 1)
                store(h, 0)
                store(h, 1)
            for s in range(2):
                query(PH - 1, s)
            for s in range(2):
                store(PH - 1, s)
            for s in range(2):
                act.wait_ge(stored[s], 16 * PH + 16)

        @block.vector
        def _(dve):
            dve.sem_inc(sc_taken, 2)
            for s in range(2):
                dve.sem_inc(stored[s], 16)
            with dve.Fori(0, PH) as h:
                for s in range(2):
                    dve.wait_ge(sc_made, h * 2 + s + 1)
                    dve.wait_ge(stored[s], h * 16 + 16)
                    dve.tensor_copy(sc[s][:, :, :], pk[s][:, :].rearrange("p (b k) -> p b k", b=NB))\
                       .then_inc(sc_taken, 1)


def step6(nc, m, io, sem):
    at = m.at
    G0 = R0 + 80 * KB
    wb = [at(f"s6_wb{s}", [P, KEYS, CHUNK], F32, F0 + 32 * KB * s) for s in range(2)]
    gst = [at(f"s6_g{s}", [P, T], F32, G0 + 4 * KB * s) for s in range(2)]
    oh1 = [at(f"s6_oh1{s}", [P, 4, KEYS], F32, G0 + 8 * KB + 2 * KB * s) for s in range(2)]
    oh2 = [at(f"s6_oh2{s}", [P, 4, KEYS], F32, G0 + 12 * KB + 2 * KB * s) for s in range(2)]
    sc = at("s6_sc", [P, 2 * PH, KEYS], F32, G0 + 16 * KB)
    eq = at("s6_eq", [P, P, TOPK], F32, G0 + 24 * KB)
    c = G0 + 32 * KB

    def small(name, shape, dt=F32):
        nonlocal c
        t = at(f"s6_{name}", shape, dt, c)
        c += -(-int(np.prod(shape[1:])) * 4 // 32) * 32
        return t

    val = small("val", [P, 2 * PH, TOPK])
    key = small("key", [P, 2 * PH, TOPK], U32)
    keyf = small("keyf", [P, 2 * PH, TOPK])
    rep = [small(f"rep{s}", [P, KEYS]) for s in range(2)]
    cand = small("cand", [P, TOPK, TOPK])
    cand2 = small("cand2", [P, TOPK, TOPK])
    best = small("best", [P, PH, TOPK])
    place = small("place", [P, PH, TOPK], U32)
    half = [small(f"half{s}", [P, P], U32) for s in range(2)]
    halff = [small(f"halff{s}", [P, P]) for s in range(2)]
    pick = small("pick", [P, 3, P])
    pickT = small("pickT", [P, 3, P])
    some = small("some", [P, 3, 16])
    four = small("four", [P, 3, 4])
    norm = small("norm", [P, 2, PH])
    assert c <= R0 + 128 * KB
    ctx = ExitStack()
    with ctx:
        w = Weights(m, sem, "s6u", F0 + 64 * KB, R0 + 64 * KB)
        ps = [ctx.enter_context(nc.psum_tensor(f"s6_ps{s}", [P, T], F32)) for s in range(2)]
        pw = [ctx.enter_context(nc.psum_tensor(f"s6_pw{s}", [P, 4, KEYS], F32)) for s in range(2)]
        pt = ctx.enter_context(nc.psum_tensor("s6_pt", [P, 3, P], F32))
        made, gelu = sem("s6_made"), sem("s6_gelu")
        g_stored = [sem(f"s6_gst{s}") for s in range(2)]
        oh_ready, oh_used = sem("s6_ohr"), sem("s6_ohu")
        w_taken = sem("s6_wt")
        w_stored = [sem(f"s6_wst{s}") for s in range(2)]
        sc_in, sc_used = sem("s6_scin"), sem("s6_scu")
        ex_in, ex_out, pick_ready, turned, pickT_ready, staged = (sem(f"s6_{n}") for n in ("exi", "exo", "pick", "turn", "pkt", "stg"))
        block = ctx.enter_context(nc.Block())
        PAIRS = 4


        @block.sync
        def _(sp):
            with sp.Fori(0, NB) as b:
                sp.wait_ge(sc_used, b + 1)
                sp.dma_start(sc[:, :, :], m.scores[bass.ds(b, 1)].rearrange("b p c k -> p (b c) k")).then_inc(sc_in, 16)
                with sp.Fori(0, 2 * PAIRS) as i:
                    for s in range(2):
                        w.load(sp, b * 2 * PAIRS + i, s,
                               io["u"][bass.ds((b * 2 * PAIRS + i) * 2 + s, 1)].rearrange("a p k m -> p (a k) m"))

        @block.scalar
        def _(act):
            def gelu_tile(n, s):
                act.wait_ge(made, n * 2 + s + 1)
                act.wait_ge(g_stored[s], n * 16 + 16)
                act.activation(gst[s][:, :], ps[s][:, :], ACT.Gelu)
                act.drain().then_inc(gelu, 1)
                act.dma_start(m.g[bass.ds(n * 2 + s, 1)].rearrange("a p t -> p (a t)"), gst[s][:, :])\
                   .then_inc(g_stored[s], 16)

            def take_w(r, hh, i, q):
                act.wait_ge(oh_used, r * 32 + hh * 16 + i * 4 + q + 3)
                act.activation(wb[hh][:, :, bass.ds(i * 16 + q * 4, 4)].rearrange("p k t -> p t k"),
                               pw[q % 2][:, :, :], ACT.Copy).then_inc(w_taken, 1)

            def pair(b, r, hh, i, last):
                for s in range(2):
                    if b is not None:
                        n = (b * 2 + hh) * PAIRS + i
                        gelu_tile(n, s)
                        if not last:
                            w.round(act, n + 1, s)
                    if r is not None:
                        for q in (2 * s, 2 * s + 1):
                            take_w(r, hh, i, q)

            def half_block(b, r, hh, last=False):
                if r is not None:
                    act.wait_ge(w_stored[hh], r * 16 + 16)
                with act.Fori(0, PAIRS - 1 if last else PAIRS) as i:
                    pair(b, r, hh, i, False)
                if last:
                    pair(b, r, hh, PAIRS - 1, True)
                if r is not None:
                    act.drain()
                    act.dma_start(m.w[bass.ds(r * 2 + hh, 1)].rearrange("a p k -> p (a k)"),
                                  wb[hh][:, :, :].rearrange("p k t -> p (k t)")).then_inc(w_stored[hh], 16)

            def softmax(b):
                act.wait_ge(ex_in, b + 1)
                act.activation(pick[:, 2, :], pick[:, 2, :], ACT.Exp)
                act.drain().then_inc(ex_out, 1)

            for s in range(2):
                act.sem_inc(g_stored[s], 16)
                act.sem_inc(w_stored[s], 16)
                w.round(act, 0, s)
            for hh in range(2):
                half_block(0, None, hh)
            softmax(0)
            with act.Fori(1, NB - 1) as b:
                for hh in range(2):
                    half_block(b, b - 1, hh)
                softmax(b)
            for hh in range(2):
                half_block(NB - 1, NB - 2, hh, last=hh == 1)
            softmax(NB - 1)
            for hh in range(2):
                half_block(None, NB - 1, hh)
            for s in range(2):
                act.wait_ge(w_stored[s], 16 * NB + 16)
                act.wait_ge(g_stored[s], 16 * NB * 2 * PAIRS + 16)

        @block.gpsimd
        def _(pool):
            def half_block(b, r, hh):
                with pool.Fori(0, PAIRS) as i:
                    if r is not None:
                        pool.tensor_copy(some[:, :, :], pickT[:, :, bass.ds(hh * 64 + i * 16, 16)])
                        pool.drain()
                    for s in range(2):
                        if b is not None:
                            w.remainder(pool, (b * 2 + hh) * PAIRS + i, s)
                        if r is not None:
                            for q in (2 * s, 2 * s + 1):
                                pool.wait_ge(oh_used, r * 32 + hh * 16 + i * 4 + q + 1)
                                pool.tensor_tensor(four[:, :, :], some[:, :, 4 * q:4 * q + 4],
                                                   m.ones[:, 0:12].rearrange("p (v t) -> p v t", v=3), ALU.mult)
                                pool.drain()
                                for j in range(4):
                                    pool.tensor_scalar(oh2[q % 2][:, j, :], m.iota[:, :], four[:, 1, j:j + 1], None,
                                                       ALU.is_equal)
                                    pool.tensor_scalar(oh1[q % 2][:, j, :], m.iota[:, :], four[:, 0, j:j + 1],
                                                       four[:, 2, j:j + 1], ALU.is_equal, ALU.mult)
                                pool.drain().then_inc(oh_ready, 1)

            def take_picks(b):
                pool.drain().then_inc(staged, 1)
                pool.wait_ge(pickT_ready, b + 1)

            pool.sem_inc(w.split, 2)
            for hh in range(2):
                half_block(0, None, hh)
            take_picks(0)
            with pool.Fori(1, NB) as b:
                for hh in range(2):
                    half_block(b, b - 1, hh)
                take_picks(b)
            for hh in range(2):
                half_block(None, NB - 1, hh)

        @block.tensor
        def _(pe):
            def half_block(b, r, hh):
                with pe.Fori(0, PAIRS) as i:
                    for s in range(2):
                        if b is not None:
                            n = (b * 2 + hh) * PAIRS + i
                            w.ready(pe, n, s)
                            pe.wait_ge(gelu, n * 2 + s + 1)
                            project(pe, ps[s], w.hi[s], w.lo[s], m.hn_hi, m.hn_lo).then_inc(w.used, 1)
                            pe.drain().then_inc(made, 1)
                        if r is not None:
                            for q in (2 * s, 2 * s + 1):
                                k = r * 32 + hh * 16 + i * 4 + q
                                pe.wait_ge(oh_ready, k + 1)
                                pe.wait_ge(w_taken, k + 1)
                                for j in range(4):
                                    mm = pe.matmul(pw[q % 2][:, j, :], oh2[q % 2][:, j, :], oh1[q % 2][:, j, :],
                                                   start=True, stop=True)
                                mm.then_inc(oh_used, 1)

            def turn_picks(b):
                pe.wait_ge(pick_ready, b + 1)
                for v in range(3):
                    mm = pe.transpose(pt[:, v, :], pick[:, v, :], m.ident[:, :])
                mm.then_inc(turned, 1)

            pe.sem_inc(w.used, 2)
            pe.sem_inc(gelu, 2)
            pe.sem_inc(oh_used, 2)
            pe.sem_inc(w_taken, 2)
            for hh in range(2):
                half_block(0, None, hh)
            turn_picks(0)
            with pe.Fori(1, NB) as b:
                for hh in range(2):
                    half_block(b, b - 1, hh)
                turn_picks(b)
            for hh in range(2):
                half_block(None, NB - 1, hh)

        @block.vector
        def _(dve):
            def best16(h):
                both = [2 * h, 2 * h + 1]
                for n in both:
                    dve.max(out=val[:, n, 0:8], in_=sc[:, n, :])
                dve.drain()
                for n in both:
                    dve.max_index(key[:, n, 0:8], val[:, n, 0:8], sc[:, n, :])
                    dve.match_replace(out=rep[n % 2][:, :], in_to_replace=val[:, n, 0:8], in_values=sc[:, n, :],
                                      imm_value=LOWEST)
                dve.drain()
                for n in both:
                    dve.max(out=val[:, n, 8:16], in_=rep[n % 2][:, :])
                dve.drain()
                for n in both:
                    dve.max_index(key[:, n, 8:16], val[:, n, 8:16], rep[n % 2][:, :])
                dve.tensor_tensor(cand[:, :, :], val[:, 2 * h, :].unsqueeze(2).broadcast_to([P, TOPK, TOPK]),
                                  val[:, 2 * h + 1, :].unsqueeze(1).broadcast_to([P, TOPK, TOPK]), ALU.add)
                dve.drain()
                flat = [x[:, :, :].rearrange("p a b -> p (a b)") for x in (cand, cand2)]
                dve.max(out=best[:, h, 0:8], in_=flat[0])
                dve.drain()
                dve.max_index(place[:, h, 0:8], best[:, h, 0:8], flat[0])
                dve.match_replace(out=flat[1], in_to_replace=best[:, h, 0:8], in_values=flat[0], imm_value=LOWEST)
                dve.drain()
                dve.max(out=best[:, h, 8:16], in_=flat[1])
                dve.drain()
                dve.max_index(place[:, h, 8:16], best[:, h, 8:16], flat[1])

            def rank(b):
                dve.wait_ge(sc_in, b * 16 + 16)
                dve.memset(norm[:, :, :], 0.0)
                dve.drain()
                for h in range(PH):
                    best16(h)
                dve.drain().then_inc(sc_used, 1)
                dve.wait_ge(turned, b + 1)
                pw_ = pick[:, 2, :].rearrange("p (h j) -> p h j", h=PH)
                dve.tensor_tensor(pw_, best[:, :, :], best[:, :, 0:1].broadcast_to([P, PH, TOPK]), ALU.subtract)
                dve.drain().then_inc(ex_in, 1)
                flat = place[:, :, :].rearrange("p h j -> p (h j)")
                dve.tensor_scalar(half[0][:, :], flat, 4, None, ALU.logical_shift_right)
                dve.tensor_scalar(half[1][:, :], flat, 15, None, ALU.bitwise_and)
                dve.tensor_copy(keyf[:, :, :], key[:, :, :])
                dve.drain()
                for s in range(2):
                    dve.tensor_copy(halff[s][:, :], half[s][:, :])
                dve.drain()
                for s in range(2):
                    dve.tensor_tensor(eq[:, :, :], halff[s][:, :].unsqueeze(2).broadcast_to([P, P, TOPK]),
                                      m.iota[:, 0:TOPK].unsqueeze(1).broadcast_to([P, P, TOPK]), ALU.is_equal)
                    dve.drain()
                    e4 = eq[:, :, :].rearrange("p (h j) a -> p h j a", h=PH)
                    ranked = keyf[:, :, :].rearrange("p (h s) a -> p h s a", s=2)[:, :, s, :].unsqueeze(2)
                    dve.tensor_tensor(e4, e4, ranked.broadcast_to([P, PH, TOPK, TOPK]), ALU.mult)
                    dve.drain()
                    dve.tensor_reduce(pick[:, s, :], eq[:, :, :], AX.X, ALU.add)
                    dve.drain()
                dve.wait_ge(ex_out, b + 1)
                dve.tensor_reduce(norm[:, 0, :], pw_, AX.X, ALU.add)
                dve.drain()
                dve.reciprocal(norm[:, 1, :], norm[:, 0, :])
                dve.drain()
                dve.tensor_tensor(pw_, pw_, norm[:, 1, :].unsqueeze(2).broadcast_to([P, PH, TOPK]), ALU.mult)
                dve.drain().then_inc(pick_ready, 1)
                dve.wait_ge(turned, b + 2)
                dve.wait_ge(staged, b + 1)
                dve.tensor_copy(pickT[:, :, :], pt[:, :, :])
                dve.drain().then_inc(pickT_ready, 1)

            dve.sem_inc(turned, 1)
            dve.sem_inc(sc_used, 1)
            with dve.Fori(0, NB) as b:
                rank(b)


def step7(nc, m, io, sem):
    GT, Q = 4, 4
    NG = KEYS // GT
    at = m.at
    v_hi = [at(f"s7_vhi{g}", [P, GT, D], F32R, R0 + 32 * KB * g) for g in range(2)]
    v_lo = [at(f"s7_vlo{g}", [P, GT, D], F32R, R0 + 32 * KB * g + 16 * KB) for g in range(2)]
    c_hi = [at(f"s7_chi{g}", [P, GT, T], F32R, R0 + 64 * KB + 32 * KB * g) for g in range(2)]
    c_lo = [at(f"s7_clo{g}", [P, GT, T], F32R, R0 + 64 * KB + 32 * KB * g + 16 * KB) for g in range(2)]
    y = m.y
    vr = [at(f"s7_vr{s}", [P, D], F32, F0 + 32 * KB + 4 * KB * s) for s in range(2)]
    gr = [at(f"s7_gr{s}", [P, T], F32, F0 + 40 * KB + 4 * KB * s) for s in range(2)]
    wr = [at(f"s7_wr{s}", [P, 2 * NB, 2, CHUNK], F32, F0 + 48 * KB + 8 * KB * s) for s in range(2)]
    ctx = ExitStack()
    with ctx:
        ps = [ctx.enter_context(nc.psum_tensor(f"s7_ps{s}", [P, 2, T], F32)) for s in range(2)]
        v_in = [sem(f"s7_v_in{s}") for s in range(2)]
        g_in = [sem(f"s7_g_in{s}") for s in range(2)]
        w_in = [sem(f"s7_w_in{s}") for s in range(2)]
        v_rounded, v_split, coef, c_rounded, c_split = (sem(f"s7_{n}") for n in ("vr_", "vs", "co", "cr", "cs"))
        used, made, taken = sem("s7_used"), sem("s7_made"), sem("s7_taken")
        block = ctx.enter_context(nc.Block())
        PER = 2 * GT
        w4 = m.w.rearrange("n p (k t) -> p n k t", t=CHUNK)

        @block.sync
        def _(sp):
            with sp.Fori(0, NG // 2) as it:
                for t in range(PER):
                    n = it * PER + t
                    s, p = t % 2, t // 2 % 2
                    sp.wait_ge(v_split, n + 1)
                    sp.dma_start(vr[s][:, :], io["v"][bass.ds(n, 1)].rearrange("a p d -> p (a d)")).then_inc(v_in[s], 16)
                    sp.wait_ge(c_split, n + 1)
                    sp.dma_start(gr[s][:, :], m.g[bass.ds(n, 1)].rearrange("a p t -> p (a t)")).then_inc(g_in[s], 16)
                    if s == 0:
                        sp.dma_start(wr[p][:, :, :, :], w4[:, :, bass.ds(n, 2), :]).then_inc(w_in[p], 16)

        @block.scalar
        def _(act):
            with act.Fori(0, NG // 2) as it:
                for t in range(PER):
                    n, s, g = it * PER + t, t % 2, t // GT
                    if t % GT == 0:
                        act.wait_ge(used, it * 2 + g + 1)
                    act.wait_ge(v_in[s], (it * (PER // 2) + t // 2 + 1) * 16)
                    act.activation(v_hi[g][:, t % GT, :], vr[s][:, :], ACT.Copy).then_inc(v_rounded, 1)
                    act.wait_ge(coef, n + 1)
                    act.activation(c_hi[g][:, t % GT, :], gr[s][:, :], ACT.Copy).then_inc(c_rounded, 1)

        @block.gpsimd
        def _(pool):
            pool.sem_inc(v_split, 2)
            with pool.Fori(0, NG // 2) as it:
                for t in range(PER):
                    n, s, g = it * PER + t, t % 2, t // GT
                    pool.wait_ge(v_rounded, n + 1)
                    pool.tensor_tensor(v_lo[g][:, t % GT, :], vr[s][:, :], v_hi[g][:, t % GT, :].bitcast(F32),
                                       ALU.subtract).then_inc(v_split, 1)

        @block.tensor
        def _(pe):
            pe.sem_inc(used, 2)
            pe.sem_inc(taken, 2)
            with pe.Fori(0, NG // 2) as it:
                for g in range(2):
                    pe.wait_ge(v_split, (it * 2 + g + 1) * GT + 2)
                    pe.wait_ge(c_split, (it * 2 + g + 1) * GT + 2)
                    for qd in range(Q):
                        out = ps[qd % 2]
                        pe.wait_ge(taken, (it * 2 + g) * Q + qd + 1)
                        for dc in range(2):
                            d = slice((2 * qd + dc) * P, (2 * qd + dc + 1) * P)
                            for t in range(GT):
                                halves = [slice(h * HALF, (h + 1) * HALF) for h in range(2)]
                                for c in halves:
                                    pe.matmul(out[:, dc, c], v_hi[g][:, t, d], c_hi[g][:, t, c], start=(t == 0), stop=False)
                                    pe.matmul(out[:, dc, c], v_hi[g][:, t, d], c_lo[g][:, t, c], start=False, stop=False)
                                for c in halves:
                                    mm = pe.matmul(out[:, dc, c], v_lo[g][:, t, d], c_hi[g][:, t, c], start=False,
                                                   stop=(t == GT - 1))
                        mm.then_inc(made, 1)
                    pe.drain().then_inc(used, 1)

        @block.vector
        def _(dve):
            def coefficients(it, t):
                n, s, g, p = it * PER + t, t % 2, t // GT, t // 2 % 2
                dve.wait_ge(g_in[s], (it * (PER // 2) + t // 2 + 1) * 16)
                dve.wait_ge(w_in[p], (it * (PER // 4) + t // 4 + 1) * 16)
                if t % GT == 0:
                    dve.wait_ge(used, it * 2 + g + 1)
                g3 = gr[s][:, :].rearrange("p (n t) -> p n t", t=CHUNK)
                dve.tensor_tensor(g3, g3, wr[p][:, :, s, :], ALU.mult)
                dve.drain().then_inc(coef, 1)
                dve.wait_ge(c_rounded, n + 1)
                dve.tensor_tensor(c_lo[g][:, t % GT, :], gr[s][:, :], c_hi[g][:, t % GT, :].bitcast(F32),
                                  ALU.subtract).then_inc(c_split, 1)

            def add(group, qd):
                dve.wait_ge(made, group * Q + qd + 1)
                dve.tensor_tensor(y[:, 2 * qd:2 * qd + 2, :], y[:, 2 * qd:2 * qd + 2, :], ps[qd % 2][:, :, :], ALU.add)\
                   .then_inc(taken, 1)

            dve.sem_inc(c_split, 2)
            dve.memset(y[:, :, :], 0.0)
            for t in range(GT):
                coefficients(0, t)
            def turn(it, more):
                for g in range(2):
                    for qd in range(Q):
                        if g == 0:
                            coefficients(it, GT + qd)
                        elif more:
                            coefficients(it + 1, qd)
                        add(it * 2 + g, qd)

            with dve.Fori(0, NG // 2 - 1) as it:
                turn(it, True)
            turn(NG // 2 - 1, False)


def step8(nc, m, io, sem):
    at, y = m.at, m.y
    h1 = at("s8_h1", [P, DC, T], F32, R0)
    sq = at("s8_sq", [P, 2, T], F32, R0 + 32 * KB)
    r = at("s8_r", [P, T], F32, R0 + 40 * KB)
    ctx = ExitStack()
    with ctx:
        ps_ss = ctx.enter_context(nc.psum_tensor("s8_ss", [P, T], F32))
        h1_in = [sem(f"s8_h1_in{k}") for k in range(DC)]
        h2_ready, sq_ready, sq_used, ss_ready, inv, root, done, stored = (
            sem(f"s8_{n}") for n in ("h2", "sqr", "squ", "ss", "inv", "root", "done", "st"))
        block = ctx.enter_context(nc.Block())

        @block.sync
        def _(sp):
            for k in range(DC):
                sp.dma_start(h1[:, k, :], m.h1[k]).then_inc(h1_in[k], 16)
            for k in range(DC):
                sp.wait_ge(done, k + 1)
                sp.dma_start(io["out"][k], y[:, k, :]).then_inc(stored, 16)
            sp.wait_ge(stored, 16 * DC)

        @block.scalar
        def _(act):
            for k in range(DC):
                act.wait_ge(h2_ready, k + 1)
                if k >= 2:
                    act.wait_ge(sq_used, k - 1)
                act.activation(sq[:, k % 2, :], y[:, k, :], ACT.Square).then_inc(sq_ready, 1)
            act.wait_ge(inv, 1)
            act.activation(r[:, :], r[:, :], ACT.Sqrt).then_inc(root, 1)

        @block.tensor
        def _(pe):
            for k in range(DC):
                pe.wait_ge(sq_ready, k + 1)
                for h in range(2):
                    mm = pe.matmul(ps_ss[:, h * HALF:(h + 1) * HALF], m.ones[:, :],
                                   sq[:, k % 2, h * HALF:(h + 1) * HALF], start=(k == 0), stop=(k == DC - 1))
                mm.then_inc(sq_used, 1)
            pe.drain().then_inc(ss_ready, 1)

        @block.vector
        def _(dve):
            for k in range(DC):
                dve.wait_ge(h1_in[k], 16)
                dve.scalar_tensor_tensor(y[:, k, :], y[:, k, :], m.mods[:, 5, k:k + 1], h1[:, k, :], ALU.mult,
                                         ALU.add).then_inc(h2_ready, 1)
            dve.wait_ge(ss_ready, 1)
            dve.tensor_scalar(r[:, :], ps_ss[:, :], 1.0 / D, EPS, ALU.mult, ALU.add)
            dve.drain()
            dve.reciprocal(r[:, :], r[:, :]).then_inc(inv, 1)
            dve.wait_ge(root, 1)
            for k in range(DC):
                dve.tensor_tensor(y[:, k, :], y[:, k, :], r[:, :], ALU.mult)
                dve.drain()
                dve.tensor_scalar(y[:, k, :], y[:, k, :], m.mods[:, 7, k:k + 1], m.mods[:, 6, k:k + 1],
                                  ALU.mult, ALU.add).then_inc(done, 1)


STEPS = (step1, step2, step3, step4, step5, step6, step7, step8)


def encoder_layer(nc, io, out, steps=8, scratch="Internal"):
    m = Mem()
    m.at = lambda name, shape, dt, off: nc.alloc_sbuf_tensor_at(name, shape, dt, offset=off)
    m.arena = nc.alloc_sbuf_tensor("arena", [P, (C0 + CB - BASE) // 4], F32)
    free = C0

    def constant(name, shape, dt=F32):
        nonlocal free
        t = m.at(name, shape, dt, free)
        free += -(-int(np.prod(shape[1:])) * 4 // 32) * 32
        assert free <= C0 + CB
        return t

    m.cols = constant("cols", [P, NCOL])
    m.ident = constant("ident", [P, P])
    m.ones = constant("ones", [P, P])
    m.iota = constant("iota", [P, KEYS])
    m.mask = constant("mask", [P, 2, P], I32)
    m.keysT = constant("keysT", [P, 2, KEYS])
    m.mods = constant("mods", [P, 8, DC])
    m.lb = constant("lb", [P, 2, HEADS])
    m.omlb = constant("omlb", [P, 2, HEADS])
    m.hn_hi = m.at("hn_hi", [P, DC, T], F32R, R0)
    m.hn_lo = m.at("hn_lo", [P, DC, T], F32R, R0 + 32 * KB)
    m.y = m.at("y", [P, DC, T], F32, F0)
    m.col = lambda name: m.cols[:, COL[name][0]:COL[name][1]]
    dram = lambda name, shape: nc.dram_tensor(name, shape, F32, kind=scratch).ap()
    m.mix = dram("s_mix", [2 * HEADS, P, T])
    m.h1 = dram("s_h1", [DC, P, T])
    m.scores = dram("s_scores", [NB, P, 2 * PH, KEYS])
    m.g = dram("s_g", [KEYS, KEYS, T])
    m.w = dram("s_w", [2 * NB, P, KEYS * CHUNK])
    for n, step in enumerate((constants,) + STEPS[:steps]):
        sems = []

        def sem(name):
            sems.append(nc.alloc_semaphore(name))
            return sems[-1]

        step(nc, m, io if n < 8 else {**io, "out": out}, sem)
        nc.clear_and_free_semaphores(sems)
        nc.all_engine_barrier()


def kernel(**inputs):
    from concourse import bacc
    from concourse.bass_utils import run_bass_kernel_spmd

    arrays = layouts(inputs)
    nc = bacc.Bacc("TRN2", target_bir_lowering=False, num_devices=1)
    io = {k: nc.dram_tensor(f"in_{k}", v.shape, mybir.dt.from_np(v.dtype), kind="ExternalInput").ap()
          for k, v in arrays.items()}
    out = nc.dram_tensor("out_T", (DC, P, T), F32, kind="ExternalOutput").ap()
    encoder_layer(nc, io, out)
    r = run_bass_kernel_spmd(nc, [{f"in_{k}": v for k, v in arrays.items()}], core_ids=[0])
    got = r.results[0]["out_T"].reshape(D, T)
    return np.ascontiguousarray(got.T).reshape(1, T, D)


def layouts(inputs):
    a = {k: np.asarray(v) for k, v in inputs.items()}
    chunks = lambda v: v.reshape(-1, P).T

    def tiles(w):
        return w.reshape(DC, P, -1, P).transpose(2, 1, 0, 3)

    w = tiles(a["w_in"][0])
    q, ff, fb, i, g, ca, cg = (4 * n for n in range(7))
    order = [x for c in range(CONV_C) for x in (cg + c, ca + c)]
    order += [x for h in range(HEADS) for x in (ff + h, fb + h, q + h, i + h, g + h)]
    mods = np.concatenate([a["ada_w"][0], a["final_ada_w"]], axis=1)
    cols = np.concatenate(
        [chunks(a["ada_b"][0]), chunks(a["final_ada_b"]), chunks(a["norm_mix_g"][0]), chunks(a["norm_ffn_g"][0]),
         chunks(a["final_norm_g"]), chunks(a["c"][0]), chunks(a["hgrn_norm_g"][0]), chunks(a["conv_b"][0]),
         chunks(a["conv_ln_g"][0]), chunks(a["conv_ln_b"][0]), chunks(a["lb_gamma_fwd"]),
         chunks(a["lb_gamma_bwd"]),
         a["conv_w"][0].T.reshape(CONV_C, P, CONV_W).transpose(1, 0, 2).reshape(P, -1)], axis=1)
    out = {
        "xT": a["x"][0].T.reshape(DC, P, T),
        "cols": cols,
        "ada": tiles(mods).reshape(32, 2, P, DC, P).transpose(0, 2, 1, 3, 4),
        "w_in": w[order],
        "w_out": tiles(a["w_out"][0]),
        "wq": tiles(a["peer_wq"][0]),
        "keysT": np.stack([a["peer_keys1"][0].T, a["peer_keys2"][0].T], axis=1),
        "u": a["peer_u"][0].reshape(KEYS, KEYS, DC, P).transpose(0, 3, 2, 1),
        "v": a["peer_v"][0].reshape(KEYS, KEYS, D),
    }
    return {k: np.ascontiguousarray(v) for k, v in out.items()}
```

```python
from contextlib import ExitStack

import numpy as np

import concourse.bass as bass
from concourse import mybir

F32 = mybir.dt.float32
BF16 = mybir.dt.bfloat16
F32R = mybir.dt.float32r
U32 = mybir.dt.uint32
I32 = mybir.dt.int32
ALU = mybir.AluOpType
ACT = mybir.ActivationFunctionType
AX = mybir.AxisListType

P = 128
T = 1024
D = 1024
DC = D // P
HALF = 512
HEADS = 4
CHUNK = 64
NCH = T // CHUNK
CONV_W = 31
PAD = CONV_W // 2
CONV_C = 4
DCONV = CONV_C * P
PROJ_HEAD = 5
PH = 8
KEYS = 128
TOPK = 16
NB = T // P
EPS = 1e-6
LOWEST = -3.0e38

COL = {}
_at = 0
for _name, _n in (("mod_b", 64), ("g_mix", 8), ("g_ffn", 8), ("g_fin", 8), ("c", 8), ("g_hgrn", 4),
                  ("conv_b", 4), ("ln_g", 4), ("ln_b", 4), ("gam_f", 8), ("gam_b", 8),
                  ("conv_w", 4 * CONV_W)):
    COL[_name] = (_at, _at + _n)
    _at += _n
NCOL = _at

KB = 1024
BASE = 16512
R0 = BASE
F0 = BASE + 128 * KB
C0 = F0 + 72 * KB
CB = 7 * KB


class Mem:
    pass


def rev(ap, back):
    return ap[:, ::-1] if back else ap


def constants(nc, m, io, sem):
    dma = sem("cols_in")
    with nc.Block() as block:

        @block.sync
        def _(sp):
            sp.dma_start(m.cols[:, :], io["cols"]).then_inc(dma, 16)
            sp.dma_start(m.keysT[:, :, :], io["keysT"]).then_inc(dma, 16)
            sp.wait_ge(dma, 32)

        @block.gpsimd
        def _(pool):
            pool.memset(m.ones[:, :], 1.0)
            pool.memset(m.ident[:, :], 0.0)
            pool.iota(m.iota[:, :], [[1, KEYS]], base=0, channel_multiplier=0,
                      allow_small_or_imprecise_dtypes=True)
            pool.memset(m.mask[:, :, :], 1)
            pool.drain()
            pool.affine_select(out=m.ident[:, :], in_=m.ident[:, :], compare_op=ALU.not_equal, fill=1.0,
                               base=0, pattern=[[-1, P]], channel_multiplier=1)
            for back in range(2):
                sg = -1 if back else 1
                pool.affine_select(out=m.mask[:, back, :], in_=m.mask[:, back, :], compare_op=ALU.is_ge,
                                   fill=0, base=0, pattern=[[sg, P]], channel_multiplier=-sg)
            pool.drain()
            pool.memset(m.mask[0:CHUNK, :, CHUNK:P], 0)
            pool.memset(m.mask[CHUNK:P, :, 0:CHUNK], 0)
            pool.drain()


def step1(nc, m, io, sem):
    at = m.at
    x = at("s1_x", [P, DC, T], F32, F0)
    ada = at("s1_ada", [P, 2, DC, D], F32, R0 + 64 * KB)
    acc = at("s1_acc", [P, 2, D], F32, F0 + 62 * KB)
    sq = at("s1_sq", [P, 2, T], F32, F0 + 32 * KB)
    xn = at("s1_xn", [P, 2, T], F32, F0 + 40 * KB)
    r = at("s1_r", [P, T], F32, F0 + 48 * KB)
    y = at("s1_y", [P, 2, T], F32, F0 + 52 * KB)
    lbt = at("s1_lbt", [P, 8, HEADS], F32, F0 + 61 * KB)
    col = m.col
    ctx = ExitStack()
    with ctx:
        ps_mod = ctx.enter_context(nc.psum_tensor("s1_mod", [P, 2 * DC], F32))
        ps_ss = ctx.enter_context(nc.psum_tensor("s1_ss", [P, T], F32))
        x_in = [sem(f"s1_x_in{k}") for k in range(DC)]
        ada_in = [sem(f"s1_ada_in{k}") for k in range(4)]
        acc_ready, cact_done, sq_ready, sq_used = sem("s1_acc_r"), sem("s1_cact"), sem("s1_sq_r"), sem("s1_sq_u")
        ss_ready, inv_ready, r_ready, mod_ready = sem("s1_ss"), sem("s1_inv"), sem("s1_r_s"), sem("s1_mod_r")
        y_ready, hi_ready, lo_ready, lbe, lbx = sem("s1_y_r"), sem("s1_hi"), sem("s1_lo"), sem("s1_lbe"), sem("s1_lbx")
        block = ctx.enter_context(nc.Block())

        @block.sync
        def _(sp):
            for k in range(DC):
                sp.dma_start(x[:, k, :], io["xT"][k]).then_inc(x_in[k], 16)
            for n in range(4):
                v, ks = n // 2, slice(n % 2 * 4, n % 2 * 4 + 4)
                sp.dma_start(ada[:, v, ks, :], io["ada"][v][:, ks, :]).then_inc(ada_in[n], 16)

        @block.scalar
        def _(act):
            act.activation(m.cact[:, :], col("c"), ACT.Silu).then_inc(cact_done, 1)
            for k in range(DC):
                act.wait_ge(x_in[k], 16)
                if k >= 2:
                    act.wait_ge(sq_used, k - 1)
                act.activation(sq[:, k % 2, :], x[:, k, :], ACT.Square).then_inc(sq_ready, 1)
            act.wait_ge(lbx, 1)
            act.activation(lbt[:, 4:8, :], lbt[:, 0:4, :], ACT.Exp).then_inc(lbe, 1)
            act.wait_ge(inv_ready, 1)
            act.activation(r[:, :], r[:, :], ACT.Sqrt).then_inc(r_ready, 1)
            for k in range(DC):
                act.wait_ge(y_ready, k + 1)
                act.activation(m.hn_hi[:, k, :], y[:, k % 2, :], ACT.Copy).then_inc(hi_ready, 1)

        @block.gpsimd
        def _(pool):
            for k in range(DC):
                pool.wait_ge(hi_ready, k + 1)
                pool.tensor_tensor(m.hn_lo[:, k, :], y[:, k % 2, :], m.hn_hi[:, k, :].bitcast(F32),
                                   ALU.subtract).then_inc(lo_ready, 1)

        @block.tensor
        def _(pe):
            for k in range(DC):
                pe.wait_ge(sq_ready, k + 1)
                for h in range(2):
                    mm = pe.matmul(ps_ss[:, h * HALF:(h + 1) * HALF], m.ones[:, :],
                                   sq[:, k % 2, h * HALF:(h + 1) * HALF], start=(k == 0), stop=(k == DC - 1))
                mm.then_inc(sq_used, 1)
            mm2 = pe.drain()
            mm2.then_inc(ss_ready, 1)
            for v in range(2):
                pe.wait_ge(acc_ready, v + 1)
                for c in range(DC):
                    pe.matmul(ps_mod[:, v * DC + c:v * DC + c + 1], acc[:, v, c * P:(c + 1) * P], m.ones[:, 0:1],
                              start=True, stop=True)
            pe.drain().then_inc(mod_ready, 1)

        @block.vector
        def _(dve):
            gam = m.cols[:, COL["gam_f"][0]:COL["gam_b"][1]].rearrange("p (d l h) -> p d l h", d=2, l=2)
            for d in range(2):
                dve.tensor_tensor(lbt[:, 4 + d, :], gam[:, d, 0, :], gam[:, d, 1, :], ALU.max)
            dve.drain()
            for d in range(2):
                for l in range(2):
                    dve.tensor_tensor(lbt[:, 2 * d + l, :], gam[:, d, l, :], lbt[:, 4 + d, :], ALU.subtract)
            dve.drain().then_inc(lbx, 1)
            dve.wait_ge(ss_ready, 1)
            dve.tensor_scalar(r[:, :], ps_ss[:, :], 1.0 / D, EPS, ALU.mult, ALU.add)
            dve.drain()
            dve.reciprocal(r[:, :], r[:, :]).then_inc(inv_ready, 1)
            dve.wait_ge(lbe, 1)
            for d in range(2):
                dve.tensor_tensor(lbt[:, d, :], lbt[:, 4 + 2 * d, :], lbt[:, 5 + 2 * d, :], ALU.add)
            dve.drain()
            dve.reciprocal(lbt[:, 2:4, :], lbt[:, 0:2, :])
            dve.drain()
            for d in range(2):
                dve.tensor_tensor(m.lb[:, d, :], lbt[:, 4 + 2 * d, :], lbt[:, 2 + d, :], ALU.mult)
            dve.drain()
            dve.tensor_scalar(m.omlb[:, :, :], m.lb[:, :, :], -1.0, 1.0, ALU.mult, ALU.add)
            dve.wait_ge(cact_done, 1)
            for v in range(2):
                for k in range(DC):
                    if k % 4 == 0:
                        dve.wait_ge(ada_in[2 * v + k // 4], 16)
                    if k == 0:
                        dve.tensor_scalar(acc[:, v, :], ada[:, v, k, :], m.cact[:, k:k + 1], None, ALU.mult)
                    else:
                        dve.scalar_tensor_tensor(acc[:, v, :], ada[:, v, k, :], m.cact[:, k:k + 1], acc[:, v, :],
                                                 ALU.mult, ALU.add)
                    dve.drain()
                dve.drain().then_inc(acc_ready, 1)
            dve.wait_ge(mod_ready, 1)
            dve.tensor_tensor(m.mods[:, 0:2, :], ps_mod[:, :].rearrange("p (v k) -> p v k", v=2),
                              col("mod_b")[:, 0:2 * DC].rearrange("p (v k) -> p v k", v=2), ALU.add)
            dve.drain()
            dve.scalar_tensor_tensor(m.mods[:, 1, :], m.mods[:, 1, :], 1.0, col("g_mix"), ALU.add, ALU.mult)
            dve.drain()
            dve.wait_ge(r_ready, 1)
            for k in range(DC):
                dve.tensor_tensor(xn[:, k % 2, :], x[:, k, :], r[:, :], ALU.mult)
                dve.drain()
                if k >= 2:
                    dve.wait_ge(lo_ready, k - 1)
                dve.tensor_scalar(y[:, k % 2, :], xn[:, k % 2, :], m.mods[:, 1, k:k + 1],
                                  m.mods[:, 0, k:k + 1], ALU.mult, ALU.add).then_inc(y_ready, 1)


class Weights:

    def __init__(self, m, sem, name, raw_at, part_at):
        self.raw = [m.at(f"{name}_raw{s}", [P, DC, P], F32, raw_at + s * 4 * KB) for s in range(2)]
        self.hi = [m.at(f"{name}_hi{s}", [P, DC, P], F32R, part_at + s * 8 * KB) for s in range(2)]
        self.lo = [m.at(f"{name}_lo{s}", [P, DC, P], F32R, part_at + s * 8 * KB + 4 * KB) for s in range(2)]
        self.arrived = [sem(f"{name}_arrived{s}") for s in range(2)]
        self.rounded, self.split, self.used = sem(f"{name}_rounded"), sem(f"{name}_split"), sem(f"{name}_used")

    def load(self, sp, pair, s, src):
        sp.wait_ge(self.split, pair * 2 + s + 1)
        sp.dma_start(self.raw[s][:, :, :], src).then_inc(self.arrived[s], 16)

    def round(self, act, pair, s):
        act.wait_ge(self.arrived[s], pair * 16 + 16)
        act.wait_ge(self.used, pair * 2 + s + 1)
        act.activation(self.hi[s][:, :, :], self.raw[s][:, :, :], ACT.Copy).then_inc(self.rounded, 1)

    def remainder(self, pool, pair, s):
        pool.wait_ge(self.rounded, pair * 2 + s + 1)
        pool.tensor_tensor(self.lo[s][:, :, :], self.raw[s][:, :, :], self.hi[s][:, :, :].bitcast(F32),
                           ALU.subtract).then_inc(self.split, 1)

    def ready(self, pe, pair, s):
        pe.wait_ge(self.split, pair * 2 + s + 3)


def project(pe, out, w_hi, w_lo, x_hi, x_lo):
    for k in range(DC):
        for h in range(2):
            c = slice(h * HALF, (h + 1) * HALF)
            pe.matmul(out[:, c], w_hi[:, k, :], x_hi[:, k, c], start=(k == 0), stop=False)
            pe.matmul(out[:, c], w_hi[:, k, :], x_lo[:, k, c], start=False, stop=False)
        for h in range(2):
            c = slice(h * HALF, (h + 1) * HALF)
            mm = pe.matmul(out[:, c], w_lo[:, k, :], x_hi[:, k, c], start=False, stop=(k == DC - 1))
    return mm


def head_inputs(m):
    h, W = Mem(), 4 * KB
    h.low = [m.at(f"head_low{d}", [P, T], F32, F0 + W * d) for d in range(2)]
    h.kk = [m.at(f"head_k{d}", [P, T], F32, F0 + W * (2 + d)) for d in range(2)]
    h.q, h.vT = (m.at(f"head_{n}", [P, T], F32, F0 + W * k) for n, k in (("q", 4), ("vT", 5)))
    return h


def step2(nc, m, io, sem):
    at, col = m.at, m.col
    A_SLOTS, A_PER = 3, 12
    head0 = m.head
    f = F0 + 28 * KB
    hp = at("s2_hp", [P, T + 2 * PAD], F32, f)
    acc = at("s2_acc", [P, CONV_C, T], F32, f + 5 * KB)
    work = at("s2_work", [P, T], F32, f + 21 * KB)
    tap = at("s2_tap", [P, CONV_W + 1], F32, f + 25 * KB)
    ccol = at("s2_ccol", [P, 2], F32, f + 25 * KB + 512)
    r = at("s2_r", [P, T], F32, f + 26 * KB)
    sig = at("s2_sig", [P, T], F32, f + 38 * KB)
    e = R0 + 80 * KB
    vec = at("s2_vec", [P, 6, D], F32, e)
    ada = at("s2_ada", [P, A_SLOTS, D], F32, e + 24 * KB)
    prod = at("s2_prod", [P, 2, D], F32, e + 36 * KB)
    sq = [at(f"s2_sq{s}", [P, T], F32, (e + 44 * KB, f + 38 * KB)[s]) for s in range(2)]
    ctx = ExitStack()
    with ctx:
        w = Weights(m, sem, "s2w", f + 30 * KB, R0 + 64 * KB)
        ps = [ctx.enter_context(nc.psum_tensor(f"s2_ps{s}", [P, T], F32)) for s in range(2)]
        ps_mu = ctx.enter_context(nc.psum_tensor("s2_mu", [P, T], F32))
        ps_var = ctx.enter_context(nc.psum_tensor("s2_var", [P, T], F32))
        sig_ready, glu_done = sem("s2_sig_r"), sem("s2_glu")
        conv_done, mu_ready, d_ready, sq_ready, sq_used = (sem(f"s2_{n}") for n in ("conv", "mu", "d", "sqr", "squ"))
        var_ready, inv_ready, r_ready, xr, stored = (sem(f"s2_{n}") for n in ("var", "inv", "r_s", "xr", "out"))
        ada_in = [sem(f"s2_ada_in{s}") for s in range(A_SLOTS)]
        ada_used, prod_ready, prod_used, vec_ready, mod_ready = (
            sem(f"s2_{n}") for n in ("adau", "pr", "pu", "vec", "mod"))
        evac = sem("s2_evac")
        H0 = 2 * CONV_C
        block = ctx.enter_context(nc.Block())

        @block.sync
        def _(sp):
            def load(c):
                for s in range(2):
                    w.load(sp, c, s, io["w_in"][bass.ds(c * 2 + s, 1)].rearrange("a p k m -> p (a k) m"))

            def rows(c, items):
                for i in items:
                    sp.wait_ge(ada_used, c * A_PER + i + 1)
                    sp.dma_start(ada[:, i % A_SLOTS, :], io["ada"][2 + i % 6][:, bass.ds(c * 2 + i // 6, 1), :]
                                 .rearrange("p a m -> p (a m)")).then_inc(ada_in[i % A_SLOTS], 16)

            load(0)
            with sp.Fori(0, CONV_C - 1) as c:
                load(c + 1)
                rows(c, range(A_PER))
            load(CONV_C)
            rows(CONV_C - 1, range(6))
            load(CONV_C + 1)
            rows(CONV_C - 1, range(6, A_PER))

        @block.scalar
        def _(act):
            def sigmoid(c):
                act.wait_ge(w.used, c * 2 + 3)
                act.wait_ge(glu_done, c + 1)
                act.activation(sig[:, :], ps[0][:, :], ACT.Sigmoid).then_inc(sig_ready, 1)

            def scale_rows(c, items):
                for i in items:
                    if i == 0:
                        act.activation(ccol[:, :], m.cact[:, bass.ds(c * 2, 2)], ACT.Copy)
                        act.drain()
                    act.wait_ge(ada_in[i % A_SLOTS], (c * (A_PER // A_SLOTS) + i // A_SLOTS + 1) * 16)
                    act.wait_ge(prod_used, c * A_PER + i + 1)
                    act.activation(prod[:, i % 2, :], ada[:, i % A_SLOTS, :], ACT.Copy,
                                   scale=ccol[:, i // 6:i // 6 + 1])
                    act.drain().then_inc(prod_ready, 1)
                    act.sem_inc(ada_used, 1)

            def take(n):
                act.wait_ge(w.used, H0 + n + 3)
                src = ps[n % 2][:, :]
                if n < 2:
                    act.activation(head0.low[n][:, :], src, ACT.Sigmoid)
                    act.activation(head0.kk[n][:, :], src, ACT.Sigmoid, scale=-1.0)
                elif n == 2:
                    act.activation(head0.q[:, :], src, ACT.Silu)
                else:
                    act.activation(head0.vT[:, :], src, ACT.Copy)
                act.drain().then_inc(evac, 1)

            act.sem_inc(sig_ready, 1)
            act.sem_inc(ada_used, A_SLOTS)
            act.sem_inc(prod_used, 2)
            w.round(act, 0, 0)
            w.round(act, 0, 1)
            with act.Fori(0, CONV_C - 1) as c:
                sigmoid(c)
                w.round(act, c + 1, 0)
                w.round(act, c + 1, 1)
                scale_rows(c, range(A_PER))
            sigmoid(CONV_C - 1)
            w.round(act, CONV_C, 0)
            w.round(act, CONV_C, 1)
            scale_rows(CONV_C - 1, range(6))
            for n in range(2):
                take(n)
                w.round(act, CONV_C + 1, n)
            scale_rows(CONV_C - 1, range(6, A_PER))
            take(2)
            take(3)
            for c in range(CONV_C):
                act.wait_ge(d_ready, c + 1)
                if c >= 2:
                    act.wait_ge(sq_used, c - 1)
                act.activation(sq[c % 2][:, :], acc[:, c, :], ACT.Square).then_inc(sq_ready, 1)
            act.wait_ge(inv_ready, 1)
            act.activation(r[:, :], r[:, :], ACT.Sqrt).then_inc(r_ready, 1)
            for c in range(CONV_C):
                act.wait_ge(xr, c + 1)
                lg, lb = COL["ln_g"][0] + c, COL["ln_b"][0] + c
                act.activation(acc[:, c, :], acc[:, c, :], ACT.Silu, scale=m.cols[:, lg:lg + 1],
                               bias=m.cols[:, lb:lb + 1])
                act.drain()
                act.dma_start(m.mix[HEADS + c], acc[:, c, :]).then_inc(stored, 16)
            act.wait_ge(stored, 16 * CONV_C)

        @block.gpsimd
        def _(pool):
            pool.sem_inc(w.split, 2)
            pool.memset(vec[:, :, :], 0.0)

            def remainders(c):
                for s in range(2):
                    w.remainder(pool, c, s)

            def add_rows(c, items):
                for i in items:
                    if i % 6 == 0:
                        pool.drain()
                    pool.wait_ge(prod_ready, c * A_PER + i + 1)
                    pool.tensor_tensor(vec[:, i % 6, :], vec[:, i % 6, :], prod[:, i % 2, :], ALU.add)\
                        .then_inc(prod_used, 1)

            remainders(0)
            with pool.Fori(0, CONV_C - 1) as c:
                remainders(c + 1)
                add_rows(c, range(A_PER))
            remainders(CONV_C)
            add_rows(CONV_C - 1, range(6))
            remainders(CONV_C + 1)
            add_rows(CONV_C - 1, range(6, A_PER))
            pool.drain().then_inc(vec_ready, 1)

        @block.tensor
        def _(pe):
            pe.sem_inc(w.used, 2)
            with pe.Fori(0, CONV_C) as c:
                w.ready(pe, c, 0)
                pe.wait_ge(sig_ready, c + 1)
                project(pe, ps[0], w.hi[0], w.lo[0], m.hn_hi, m.hn_lo).then_inc(w.used, 1)
                w.ready(pe, c, 1)
                pe.wait_ge(glu_done, c + 1)
                project(pe, ps[1], w.hi[1], w.lo[1], m.hn_hi, m.hn_lo).then_inc(w.used, 1)
            for n in range(4):
                w.ready(pe, (H0 + n) // 2, n % 2)
                if n == 0:
                    pe.wait_ge(sig_ready, CONV_C + 1)
                elif n == 1:
                    pe.wait_ge(glu_done, CONV_C + 1)
                else:
                    pe.wait_ge(evac, n - 1)
                project(pe, ps[n % 2], w.hi[n % 2], w.lo[n % 2], m.hn_hi, m.hn_lo).then_inc(w.used, 1)
            for c in range(CONV_C):
                pe.wait_ge(conv_done, c + 1)
                for h in range(2):
                    mm = pe.matmul(ps_mu[:, h * HALF:(h + 1) * HALF], m.ones[:, :],
                                   acc[:, c, h * HALF:(h + 1) * HALF], start=(c == 0), stop=(c == CONV_C - 1))
            mm.then_inc(mu_ready, 1)
            for c in range(CONV_C):
                pe.wait_ge(sq_ready, c + 1)
                for h in range(2):
                    mm = pe.matmul(ps_var[:, h * HALF:(h + 1) * HALF], m.ones[:, :],
                                   sq[c % 2][:, h * HALF:(h + 1) * HALF], start=(c == 0), stop=(c == CONV_C - 1))
                mm.then_inc(sq_used, 1)
            pe.drain().then_inc(var_ready, 1)
            pe.wait_ge(vec_ready, 1)
            for v in range(6):
                for c in range(DC):
                    mm = pe.matmul(ps_mu[:, v * DC + c:v * DC + c + 1], vec[:, v, c * P:(c + 1) * P], m.ones[:, 0:1],
                                   start=True, stop=True)
            pe.drain().then_inc(mod_ready, 1)

        @block.vector
        def _(dve):
            dve.sem_inc(glu_done, 1)
            dve.memset(hp[:, 0:PAD], 0.0)
            dve.memset(hp[:, PAD + T:T + 2 * PAD], 0.0)
            cw = m.cols[:, COL["conv_w"][0]:COL["conv_w"][1]].rearrange("p (c k) -> p c k", c=CONV_C)
            with dve.Fori(0, CONV_C) as c:
                dve.tensor_copy(tap[:, 0:CONV_W], cw[:, bass.ds(c, 1), :])
                dve.tensor_copy(tap[:, CONV_W:CONV_W + 1], m.cols[:, bass.ds(c + COL["conv_b"][0], 1)])
                dve.wait_ge(sig_ready, c + 2)
                dve.wait_ge(w.used, c * 2 + 4)
                dve.tensor_tensor(hp[:, PAD:PAD + T], ps[1][:, :], sig[:, :], ALU.mult).then_inc(glu_done, 1)
                dve.drain()
                dve.tensor_scalar(work[:, :], hp[:, 0:T], tap[:, 0:1], tap[:, CONV_W:CONV_W + 1], ALU.mult, ALU.add)
                for k in range(1, CONV_W):
                    dve.drain()
                    dst = work[:, :] if k < CONV_W - 1 else acc[:, bass.ds(c, 1), :].rearrange("p a t -> p (a t)")
                    dve.scalar_tensor_tensor(dst, hp[:, k:k + T], tap[:, k:k + 1], work[:, :], ALU.mult, ALU.add)
                dve.drain().then_inc(conv_done, 1)
            dve.wait_ge(mu_ready, 1)
            for c in range(CONV_C):
                dve.scalar_tensor_tensor(acc[:, c, :], ps_mu[:, :], -1.0 / DCONV, acc[:, c, :], ALU.mult, ALU.add)
                dve.drain().then_inc(d_ready, 1)
            dve.wait_ge(var_ready, 1)
            dve.tensor_scalar(r[:, :], ps_var[:, :], 1.0 / DCONV, EPS, ALU.mult, ALU.add)
            dve.drain()
            dve.reciprocal(r[:, :], r[:, :]).then_inc(inv_ready, 1)
            dve.wait_ge(r_ready, 1)
            for c in range(CONV_C):
                dve.tensor_tensor(acc[:, c, :], acc[:, c, :], r[:, :], ALU.mult).then_inc(xr, 1)
            dve.wait_ge(mod_ready, 1)
            dve.tensor_tensor(m.mods[:, 2:8, :], ps_mu[:, 0:6 * DC].rearrange("p (v k) -> p v k", v=6),
                              col("mod_b")[:, 2 * DC:].rearrange("p (v k) -> p v k", v=6), ALU.add)
            dve.drain()
            for v, g in ((4, "g_ffn"), (7, "g_fin")):
                dve.scalar_tensor_tensor(m.mods[:, v, :], m.mods[:, v, :], 1.0, col(g), ALU.add, ALU.mult)
            dve.drain()


def step3(nc, m, io, sem):
    at = m.at
    W = 4 * KB
    f = [F0 + n * W for n in range(18)]
    low, kk, q, vT = m.head.low, m.head.kk, m.head.q, m.head.vT
    vtok = at("s3_vtok", [P, NB, P], F32, f[7])
    qe = [at(f"s3_qe{d}", [P, T], F32, f[8 + 4 * d]) for d in range(2)]
    ku = [at(f"s3_ku{d}", [P, T], F32, f[9 + 4 * d]) for d in range(2)]
    qr = [at(f"s3_qr{d}", [P, T], F32, f[10 + 4 * d]) for d in range(2)]
    kr = [at(f"s3_kr{d}", [P, T], F32, f[11 + 4 * d]) for d in range(2)]
    reset, o = at("s3_reset", [P, T], F32, f[16]), at("s3_o", [P, T], F32, f[17])
    e = R0 + 80 * KB
    state = [at(f"s3_state{d}", [P, NCH, P], F32, e + 8 * KB * d) for d in range(2)]
    st = [at(f"s3_st{d}", [P, NB, P], F32, e + 16 * KB + W * d) for d in range(2)]
    kt = [at(f"s3_kt{d}", [P, NB, P], F32, e + 24 * KB + W * d) for d in range(2)]
    sq = at("s3_sq", [P, T], F32, e + 24 * KB)
    r = at("s3_r", [P, T], F32, e + 28 * KB)
    dec = at("s3_dec", [P, 2, NCH], F32, e + 32 * KB)
    g = [at(f"s3_g{s}", [P, T], F32, (f[6], e + 41 * KB)[s]) for s in range(2)]
    ctx = ExitStack()
    with ctx:
        w = Weights(m, sem, "s3w", e + 33 * KB, R0 + 64 * KB)
        ps = [ctx.enter_context(nc.psum_tensor(f"s3_ps{s}", [P, T], F32)) for s in range(2)]
        po = ctx.enter_context(nc.psum_tensor("s3_po", [P, T], F32))
        pm = [ctx.enter_context(nc.psum_tensor(f"s3_pm{s}", [P, HALF], F32)) for s in range(2)]
        const, evac = sem("s3_const"), sem("s3_evac")
        k_ready = [sem(f"s3_k_r{d}") for d in range(2)]
        log_ready = [sem(f"s3_log{d}") for d in range(2)]
        prep = [sem(f"s3_prep{d}") for d in range(2)]
        powers = [sem(f"s3_pow{d}") for d in range(2)]
        ku_ready = [sem(f"s3_ku_r{d}") for d in range(2)]
        factors = [sem(f"s3_fac{d}") for d in range(2)]
        q_ready, v_ready, g_ready = sem("s3_q_r"), sem("s3_v_r"), sem("s3_g_r")
        v_turned, vtok_ready = sem("s3_vturn"), sem("s3_vtok_r")
        pm_ready = [sem(f"s3_pm_r{s}") for s in range(2)]
        pm_used = [sem(f"s3_pm_u{s}") for s in range(2)]
        o_ready, o_copied, sq_ready = sem("s3_o_r"), sem("s3_o_c"), sem("s3_sq_r")
        inv, root, done, stored = sem("s3_inv"), sem("s3_root"), sem("s3_done"), sem("s3_stored")
        block = ctx.enter_context(nc.Block())
        MADE = 4
        W0, NT = 2 * CONV_C + MADE, HEADS * PROJ_HEAD - MADE

        def allowed(quad, d):
            t0 = quad // 2 * CHUNK + (quad % 2 * 32 if d == 0 else 0)
            t1 = quad // 2 * CHUNK + (CHUNK if d == 0 else quad % 2 * 32 + 32)
            return slice(32 * quad, 32 * quad + 32), t0, t1

        def place(part, d, odd, i):
            first = odd if d == 0 else 1 - odd
            n = 4 * part + 2 * i + first
            return n, (NCH - 1 - n if d else n)

        @block.sync
        def _(sp):
            with sp.Fori(0, NT // 2) as n:
                for s in range(2):
                    w.load(sp, n, s, io["w_in"][bass.ds(n * 2 + W0 + s, 1)].rearrange("a p k m -> p (a k) m"))

        @block.gpsimd
        def _(pool):
            pool.sem_inc(w.split, 2)
            pool.memset(reset[:, :], 1.0)
            pool.drain()
            pool.memset(reset[:, 0::CHUNK], 0.0)
            for d in range(2):
                pool.memset(st[d][:, :, :], 0.0)
                pool.memset(state[d][:, 0, :], 0.0)
            pool.drain().then_inc(const, 1)
            with pool.Fori(0, NT // 2) as n:
                for s in range(2):
                    w.remainder(pool, n, s)

        @block.tensor
        def _(pe):
            def project_head(h, first, last):
                for n in range(PROJ_HEAD * h + first - MADE, PROJ_HEAD * h + last - MADE):
                    w.ready(pe, n // 2, n % 2)
                    if n >= 2:
                        pe.wait_ge(evac, n - 1)
                    project(pe, ps[n % 2], w.hi[n % 2], w.lo[n % 2], m.hn_hi, m.hn_lo).then_inc(w.used, 1)

            def recurrence(h):
                count = [0, 0]

                def batch(i, make):
                    b = i % 2
                    if 9 * h + count[b]:
                        pe.wait_ge(pm_used[b], 9 * h + count[b])
                    count[b] += 1
                    for j in range(4):
                        mm = make(pm[b][:, j * P:(j + 1) * P], j)
                    mm.then_inc(pm_ready[b], 1)

                pe.wait_ge(v_ready, h + 1)
                if h:
                    pe.wait_ge(o_copied, h)
                    pe.wait_ge(sq_ready, h)
                for b in range(NB):
                    mm = pe.transpose(po[:, b * P:(b + 1) * P], vT[:, b * P:(b + 1) * P], m.ident[:, :])
                mm.then_inc(v_turned, 1)
                for d in range(2):
                    pe.wait_ge(ku_ready[d], h + 1)
                    for half in range(2):
                        batch(half, lambda out, j: pe.transpose(
                            out, ku[d][:, (4 * half + j) * P:(4 * half + j + 1) * P], m.ident[:, :]))
                for d in range(2):
                    pe.wait_ge(factors[d], h + 1)
                    for half in range(2):
                        def scores(out, j):
                            c = (4 * half + j) * P
                            for quad in range(4):
                                rows, t0, t1 = allowed(quad, d)
                                mm = pe.matmul(out[rows, t0:t1], kr[d][:, c + 32 * quad:c + 32 * quad + 32],
                                               qr[d][:, c + t0:c + t1], start=True, stop=True)
                            return mm
                        batch(half, scores)
                if h + 1 < HEADS:
                    project_head(h + 1, 3, 4)
                pe.wait_ge(vtok_ready, h + 1)
                for part in range(4):
                    for odd in range(2):
                        def products(out, j):
                            d = j // 2
                            n, c = place(part, d, odd, j % 2)
                            rows = slice(odd * CHUNK, (odd + 1) * CHUNK)
                            return pe.matmul(out, kt[d][rows, c // 2, :], vtok[rows, c // 2, :], start=True, stop=True)
                        batch(odd, products)
                if h + 1 < HEADS:
                    project_head(h + 1, 4, 5)
                for b in range(2):
                    pe.wait_ge(pm_used[b], 9 * h + 8)
                for b in range(NB):
                    c = slice(b * P, (b + 1) * P)
                    pe.matmul(po[:, c], vtok[:, b, :], st[0][:, b, :], start=True, stop=False)
                    pe.matmul(po[:, c], vtok[:, b, :], st[1][:, b, :], start=False, stop=False)
                    for n in (2 * b, 2 * b + 1):
                        t = slice(n * CHUNK, (n + 1) * CHUNK)
                        pe.matmul(po[:, t], state[0][:, n, :], qe[0][:, t], start=False, stop=False)
                        mm = pe.matmul(po[:, t], state[1][:, NCH - 1 - n, :], qe[1][:, t], start=False, stop=(n % 2 == 1))
                mm.then_inc(o_ready, 1)
                pe.wait_ge(sq_ready, h + 1)
                for b in range(2):
                    pe.matmul(pm[b][:, :], m.ones[:, :], sq[:, b * HALF:(b + 1) * HALF],
                              start=True, stop=True).then_inc(pm_ready[b], 1)

            pe.sem_inc(w.used, 2)
            project_head(0, MADE, PROJ_HEAD)
            for h in range(HEADS):
                if h + 1 < HEADS:
                    project_head(h + 1, 0, 3)
                recurrence(h)

        @block.scalar
        def _(act):
            def round_tile(n):
                if n < NT:
                    w.round(act, n // 2, n % 2)

            def forget(h, d):
                n = PROJ_HEAD * h + d - MADE
                act.wait_ge(w.used, n + 3)
                if h:
                    act.wait_ge(factors[d], h)
                act.activation(low[d][:, :], ps[n % 2][:, :], ACT.Sigmoid)
                act.activation(kk[d][:, :], ps[n % 2][:, :], ACT.Sigmoid, scale=-1.0)
                act.drain().then_inc(k_ready[d], 1)
                act.sem_inc(evac, 1)

            def query(h):
                n = PROJ_HEAD * h + 2 - MADE
                act.wait_ge(w.used, n + 3)
                if h:
                    act.wait_ge(factors[1], h)
                act.activation(q[:, :], ps[n % 2][:, :], ACT.Silu)
                act.drain().then_inc(q_ready, 1)
                act.sem_inc(evac, 1)

            def value(h):
                n = PROJ_HEAD * h + 3 - MADE
                act.wait_ge(w.used, n + 3)
                if h:
                    act.wait_ge(v_turned, h)
                act.activation(vT[:, :], ps[n % 2][:, :], ACT.Copy)
                act.drain().then_inc(v_ready, 1)
                act.sem_inc(evac, 1)

            def gate(h):
                n = PROJ_HEAD * h + 4 - MADE
                act.wait_ge(w.used, n + 3)
                if h >= 2:
                    act.wait_ge(done, h - 1)
                act.activation(g[h % 2][:, :], ps[n % 2][:, :], ACT.Silu)
                act.drain().then_inc(g_ready, 1)
                act.sem_inc(evac, 1)

            def power(h, d):
                act.wait_ge(prep[d], h + 1)
                last = CHUNK - 1 if d == 0 else 0
                act.activation(ku[d][:, :], ku[d][:, :], ACT.Exp)
                act.activation(kr[d][:, :], qr[d][:, :], ACT.Exp, scale=-1.0)
                act.activation(dec[:, d, :], qe[d][:, last::CHUNK], ACT.Exp)
                act.drain()
                act.activation(qr[d][:, :], qr[d][:, :], ACT.Exp)
                act.activation(qe[d][:, :], qe[d][:, :], ACT.Exp)
                act.drain().then_inc(powers[d], 1)

            def logs(h):
                for d in range(2):
                    act.activation(low[d][:, :], low[d][:, :], ACT.Ln, scale=m.omlb[:, d, h:h + 1],
                                   bias=m.lb[:, d, h:h + 1])
                    act.drain().then_inc(log_ready[d], 1)

            for n in range(2):
                round_tile(n)
            for made in (*k_ready, q_ready, v_ready):
                act.sem_inc(made, 1)
            logs(0)
            gate(0)
            round_tile(2)
            power(0, 0)
            power(0, 1)
            for h in range(HEADS):
                t = PROJ_HEAD * (h + 1) - MADE
                nxt = h + 1 < HEADS
                if nxt:
                    round_tile(t + 2)
                    forget(h + 1, 0)
                    round_tile(t + 3)
                    forget(h + 1, 1)
                    round_tile(t + 4)
                    query(h + 1)
                act.wait_ge(v_turned, h + 1)
                act.activation(vtok[:, :, :], po[:, :].rearrange("p (b v) -> p b v", b=NB), ACT.Copy)
                act.drain().then_inc(vtok_ready, 1)
                for d in range(2):
                    for half in range(2):
                        act.wait_ge(pm_ready[half], 9 * h + d + 1)
                        act.activation(kt[d][:, 4 * half:4 * half + 4, :],
                                       pm[half][:, :].rearrange("p (b v) -> p b v", b=4), ACT.Copy)
                        act.drain().then_inc(pm_used[half], 1)
                if nxt:
                    value(h + 1)
                    round_tile(t + 5)
                    logs(h + 1)
                    round_tile(t + 6)
                    gate(h + 1)
                act.wait_ge(o_copied, h + 1)
                act.activation(sq[:, :], o[:, :], ACT.Square)
                act.drain().then_inc(sq_ready, 1)
                if nxt:
                    power(h + 1, 0)
                act.wait_ge(inv, h + 1)
                act.activation(r[:, :], r[:, :], ACT.Sqrt)
                act.drain().then_inc(root, 1)
                if nxt:
                    power(h + 1, 1)
                act.wait_ge(done, h + 1)
                act.dma_start(m.mix[h], o[:, :]).then_inc(stored, 16)
            act.wait_ge(stored, 16 * HEADS)

        @block.vector
        def _(dve):
            chunks = lambda ap: ap.rearrange("p (n c) -> p n c", c=CHUNK)
            def prepare(h):
                for d in range(2):
                    mid, last = (CHUNK // 2 - 1, CHUNK - 1) if d == 0 else (CHUNK // 2, 0)
                    dve.wait_ge(k_ready[d], h + 1)
                    dve.tensor_scalar(kk[d][:, :], kk[d][:, :], m.omlb[:, d, h:h + 1], None, ALU.mult)
                    if h:
                        dve.wait_ge(o_ready, h)
                    elif d == 0:
                        dve.wait_ge(const, 1)
                    dve.wait_ge(log_ready[d], h + 1)
                    dve.tensor_tensor_scan(rev(qe[d][:, :], d), reset[:, :], rev(low[d][:, :], d), 0.0,
                                           ALU.mult, ALU.add)
                    dve.drain()
                    b = chunks(qe[d][:, :])
                    spread = lambda i: b[:, :, i:i + 1].broadcast_to([P, NCH, CHUNK])
                    dve.tensor_tensor(chunks(qr[d][:, :]), b, spread(mid), ALU.subtract)
                    dve.tensor_tensor(chunks(ku[d][:, :]), spread(last), b, ALU.subtract)
                    dve.drain().then_inc(prep[d], 1)

            prepare(0)
            for h in range(HEADS):
                dve.wait_ge(q_ready, h + 1)
                for d in range(2):
                    dve.wait_ge(powers[d], h + 1)
                    dve.tensor_tensor(ku[d][:, :], ku[d][:, :], kk[d][:, :], ALU.mult).then_inc(ku_ready[d], 1)
                    dve.tensor_tensor(kr[d][:, :], kr[d][:, :], kk[d][:, :], ALU.mult)
                    dve.tensor_tensor(qr[d][:, :], qr[d][:, :], q[:, :], ALU.mult)
                    dve.tensor_tensor(qe[d][:, :], qe[d][:, :], q[:, :], ALU.mult)
                    dve.drain().then_inc(factors[d], 1)
                for d in range(2):
                    for half in range(2):
                        dve.wait_ge(pm_ready[half], 9 * h + 3 + d)
                        for quad in range(4):
                            rows, t0, t1 = allowed(quad, d)
                            mask = m.mask[rows, d:d + 1, t0:t1].broadcast_to([32, 4, t1 - t0])
                            dve.copy_predicated(st[d][rows, 4 * half:4 * half + 4, t0:t1], mask,
                                                pm[half][rows, :].rearrange("p (b t) -> p b t", b=4)[:, :, t0:t1])
                        dve.drain().then_inc(pm_used[half], 1)
                for part in range(4):
                    for odd in range(2):
                        dve.wait_ge(pm_ready[odd], 9 * h + 5 + part)
                    for j in range(4):
                        for d in range(2):
                            n = 4 * part + j
                            c = NCH - 1 - n if d else n
                            if n < NCH - 1:
                                slot = 2 * d + j // 2
                                dve.scalar_tensor_tensor(state[d][:, n + 1, :], state[d][:, n, :], dec[:, d, c:c + 1],
                                                         pm[c % 2][:, slot * P:(slot + 1) * P], ALU.mult, ALU.add)
                        dve.drain()
                    for odd in range(2):
                        dve.drain().then_inc(pm_used[odd], 1)
                dve.wait_ge(o_ready, h + 1)
                if h:
                    dve.wait_ge(stored, 16 * h)
                dve.tensor_copy(o[:, :], po[:, :])
                dve.drain().then_inc(o_copied, 1)
                if h + 1 < HEADS:
                    prepare(h + 1)
                for b in range(2):
                    dve.wait_ge(pm_ready[b], 9 * h + 9)
                    dve.tensor_scalar(r[:, b * HALF:(b + 1) * HALF], pm[b][:, :], 1.0 / P, EPS, ALU.mult, ALU.add)
                    dve.drain().then_inc(pm_used[b], 1)
                dve.reciprocal(r[:, :], r[:, :])
                dve.drain().then_inc(inv, 1)
                dve.wait_ge(root, h + 1)
                dve.wait_ge(g_ready, h + 1)
                dve.tensor_tensor(o[:, :], o[:, :], r[:, :], ALU.mult)
                dve.drain()
                gain = COL["g_hgrn"][0] + h
                dve.scalar_tensor_tensor(o[:, :], o[:, :], m.cols[:, gain:gain + 1], g[h % 2][:, :], ALU.mult, ALU.mult)
                dve.drain().then_inc(done, 1)


def step4(nc, m, io, sem):
    at = m.at
    h1 = at("s4_h1", [P, DC, T], F32, F0)
    raw = at("s4_raw", [P, 2, T], F32, F0 + 32 * KB)
    x = at("s4_x", [P, 2, T], F32, F0 + 40 * KB)
    sq = at("s4_sq", [P, 2, T], F32, F0 + 56 * KB)
    r = at("s4_r", [P, T], F32, F0 + 64 * KB)
    xn = at("s4_xn", [P, T], F32, F0 + 68 * KB)
    ctx = ExitStack()
    with ctx:
        w = Weights(m, sem, "s4w", F0 + 48 * KB, R0 + 64 * KB)
        ps = [ctx.enter_context(nc.psum_tensor(f"s4_ps{s}", [P, T], F32)) for s in range(2)]
        ps_ss = ctx.enter_context(nc.psum_tensor("s4_ss", [P, T], F32))
        raw_in = [sem(f"s4_raw_in{s}") for s in range(2)]
        x_in = [sem(f"s4_x_in{s}") for s in range(2)]
        mix_hi, mix_lo, h1_ready, sq_ready, sq_used = (sem(f"s4_{n}") for n in ("mhi", "mlo", "h1r", "sqr", "squ"))
        ss_ready, inv, root, y_ready, y_hi, y_lo, stored = (sem(f"s4_{n}") for n in ("ss", "inv", "root", "yr", "yhi", "ylo", "st"))
        block = ctx.enter_context(nc.Block())

        @block.sync
        def _(sp):
            for k in range(DC):
                if k < 2:
                    w.load(sp, 0, k, io["w_out"][k])
                if k >= 2:
                    sp.wait_ge(mix_lo, k - 1)
                sp.dma_start(raw[:, k % 2, :], m.mix[k]).then_inc(raw_in[k % 2], 16)
            for k in range(DC):
                if k >= 2:
                    w.load(sp, k // 2, k % 2, io["w_out"][k])
                    sp.wait_ge(h1_ready, k - 1)
                sp.dma_start(x[:, k % 2, :], io["xT"][k]).then_inc(x_in[k % 2], 16)
            for k in range(DC):
                sp.wait_ge(h1_ready, k + 1)
                sp.dma_start(m.h1[k], h1[:, k, :]).then_inc(stored, 16)
            sp.wait_ge(stored, 16 * DC)

        @block.scalar
        def _(act):
            for k in range(DC):
                act.wait_ge(raw_in[k % 2], 16 * (k // 2 + 1))
                act.activation(m.hn_hi[:, k, :], raw[:, k % 2, :], ACT.Copy).then_inc(mix_hi, 1)
                if k < 2:
                    w.round(act, 0, k)
            for k in range(DC):
                if k + 2 < DC:
                    w.round(act, (k + 2) // 2, k % 2)
                act.wait_ge(h1_ready, k + 1)
                if k >= 2:
                    act.wait_ge(sq_used, k - 1)
                act.activation(sq[:, k % 2, :], h1[:, k, :], ACT.Square).then_inc(sq_ready, 1)
            act.wait_ge(inv, 1)
            act.activation(r[:, :], r[:, :], ACT.Sqrt).then_inc(root, 1)
            for k in range(DC):
                act.wait_ge(y_ready, k + 1)
                act.activation(m.hn_hi[:, k, :], raw[:, k % 2, :], ACT.Copy).then_inc(y_hi, 1)

        @block.gpsimd
        def _(pool):
            pool.sem_inc(w.split, 2)
            for k in range(DC):
                pool.wait_ge(mix_hi, k + 1)
                pool.tensor_tensor(m.hn_lo[:, k, :], raw[:, k % 2, :], m.hn_hi[:, k, :].bitcast(F32),
                                   ALU.subtract).then_inc(mix_lo, 1)
                if k < 2:
                    w.remainder(pool, 0, k)
            for k in range(2, DC):
                w.remainder(pool, k // 2, k % 2)
            for k in range(DC):
                pool.wait_ge(y_hi, k + 1)
                pool.tensor_tensor(m.hn_lo[:, k, :], raw[:, k % 2, :], m.hn_hi[:, k, :].bitcast(F32),
                                   ALU.subtract).then_inc(y_lo, 1)

        @block.tensor
        def _(pe):
            def sums(k):
                pe.wait_ge(sq_ready, k + 1)
                for h in range(2):
                    mm = pe.matmul(ps_ss[:, h * HALF:(h + 1) * HALF], m.ones[:, :],
                                   sq[:, k % 2, h * HALF:(h + 1) * HALF], start=(k == 0), stop=(k == DC - 1))
                mm.then_inc(sq_used, 1)

            pe.sem_inc(w.used, 2)
            pe.wait_ge(mix_lo, DC)
            for k in range(DC):
                w.ready(pe, k // 2, k % 2)
                if k >= 2:
                    pe.wait_ge(h1_ready, k - 1)
                project(pe, ps[k % 2], w.hi[k % 2], w.lo[k % 2], m.hn_hi, m.hn_lo).then_inc(w.used, 1)
                if k:
                    sums(k - 1)
            sums(DC - 1)
            pe.drain().then_inc(ss_ready, 1)

        @block.vector
        def _(dve):
            for k in range(DC):
                dve.wait_ge(w.used, k + 3)
                dve.wait_ge(x_in[k % 2], 16 * (k // 2 + 1))
                dve.scalar_tensor_tensor(h1[:, k, :], ps[k % 2][:, :], m.mods[:, 2, k:k + 1], x[:, k % 2, :],
                                         ALU.mult, ALU.add).then_inc(h1_ready, 1)
            dve.wait_ge(ss_ready, 1)
            dve.tensor_scalar(r[:, :], ps_ss[:, :], 1.0 / D, EPS, ALU.mult, ALU.add)
            dve.drain()
            dve.reciprocal(r[:, :], r[:, :]).then_inc(inv, 1)
            dve.wait_ge(root, 1)
            for k in range(DC):
                dve.tensor_tensor(xn[:, :], h1[:, k, :], r[:, :], ALU.mult)
                dve.drain()
                if k >= 2:
                    dve.wait_ge(y_lo, k - 1)
                dve.tensor_scalar(raw[:, k % 2, :], xn[:, :], m.mods[:, 4, k:k + 1], m.mods[:, 3, k:k + 1],
                                  ALU.mult, ALU.add)
                dve.drain().then_inc(y_ready, 1)


def step5(nc, m, io, sem):
    at = m.at
    q = [at(f"s5_q{s}", [P, T], F32, F0 + s * 4 * KB) for s in range(2)]
    sc = at("s5_sc", [P, 2, NB, KEYS], F32, F0 + 8 * KB)
    ctx = ExitStack()
    with ctx:
        w = Weights(m, sem, "s5w", F0 + 16 * KB, R0 + 64 * KB)
        ps = [ctx.enter_context(nc.psum_tensor(f"s5_ps{s}", [P, T], F32)) for s in range(2)]
        pk = [ctx.enter_context(nc.psum_tensor(f"s5_pk{s}", [P, T], F32)) for s in range(2)]
        q_ready, sc_made, sc_taken = (sem(f"s5_{n}") for n in ("qr", "scm", "sct"))
        stored = [sem(f"s5_stored{s}") for s in range(2)]
        block = ctx.enter_context(nc.Block())

        @block.sync
        def _(sp):
            with sp.Fori(0, PH) as h:
                for s in range(2):
                    w.load(sp, h, s, io["wq"][bass.ds(h * 2 + s, 1)].rearrange("a p k m -> p (a k) m"))

        @block.gpsimd
        def _(pool):
            pool.sem_inc(w.split, 2)
            with pool.Fori(0, PH) as h:
                for s in range(2):
                    w.remainder(pool, h, s)

        def scores(pe, h, s):
            pe.wait_ge(q_ready, h * 2 + s + 3)
            pe.wait_ge(sc_taken, h * 2 + s + 1)
            for b in range(NB):
                mm = pe.matmul(pk[s][:, b * P:(b + 1) * P], q[s][:, b * P:(b + 1) * P], m.keysT[:, s, :],
                               start=True, stop=True)
            mm.then_inc(sc_made, 1)

        @block.tensor
        def _(pe):
            pe.sem_inc(w.used, 2)
            pe.sem_inc(q_ready, 2)
            with pe.Fori(0, PH) as h:
                for s in range(2):
                    w.ready(pe, h, s)
                    pe.wait_ge(q_ready, h * 2 + s + 1)
                    project(pe, ps[s], w.hi[s], w.lo[s], m.hn_hi, m.hn_lo).then_inc(w.used, 1)
                    if s:
                        scores(pe, h, 0)
                scores(pe, h, 1)

        @block.scalar
        def _(act):
            w.round(act, 0, 0)
            w.round(act, 0, 1)

            def query(h, s, again=True):
                act.wait_ge(w.used, h * 2 + s + 3)
                if again:
                    act.wait_ge(sc_made, h * 2 + s - 1)
                act.activation(q[s][:, :], ps[s][:, :], ACT.Copy).then_inc(q_ready, 1)

            def store(h, s):
                act.wait_ge(sc_taken, h * 2 + s + 3)
                act.dma_start(m.scores[:, :, bass.ds(h * 2 + s, 1), :].rearrange("b p c k -> p (b c) k"),
                              sc[:, s, :, :]).then_inc(stored[s], 16)

            query(0, 0, again=False)
            w.round(act, 1, 0)
            query(0, 1, again=False)
            w.round(act, 1, 1)
            store(0, 0)
            store(0, 1)
            with act.Fori(1, PH - 1) as h:
                query(h, 0)
                w.round(act, h + 1, 0)
                query(h, 1)
                w.round(act, h + 1, 1)
                store(h, 0)
                store(h, 1)
            for s in range(2):
                query(PH - 1, s)
            for s in range(2):
                store(PH - 1, s)
            for s in range(2):
                act.wait_ge(stored[s], 16 * PH)

        @block.vector
        def _(dve):
            dve.sem_inc(sc_taken, 2)
            for h in range(PH):
                for s in range(2):
                    dve.wait_ge(sc_made, h * 2 + s + 1)
                    if h:
                        dve.wait_ge(stored[s], h * 16)
                    dve.tensor_copy(sc[:, s, :, :], pk[s][:, :].rearrange("p (b k) -> p b k", b=NB))\
                       .then_inc(sc_taken, 1)
                dve.drain()
                for part in range(3):
                    m.picks.part(dve, h, part, sc[:, :, 0, :])


class Picks:

    def __init__(self, m, at):
        def buffer(name, shape, dt=F32):
            t = m.at(f"pk_{name}", shape, dt, self.end)
            self.end += -(-int(np.prod(shape[1:])) * 4 // 32) * 32
            return t

        self.end = at
        self.val = buffer("val", [P, 2 * PH, TOPK])
        self.key = buffer("key", [P, 2 * PH, TOPK], U32)
        self.rep = [buffer(f"rep{s}", [P, KEYS]) for s in range(2)]
        self.cand = buffer("cand", [P, TOPK, TOPK])
        self.cand2 = buffer("cand2", [P, TOPK, TOPK])
        self.best = buffer("best", [P, PH, TOPK])
        self.place = buffer("place", [P, PH, TOPK], U32)

    def part(self, dve, h, part, sc):
        (self.best8, self.next8, self.best_sums)[part](dve, h, sc)

    def best8(self, dve, h, sc):
        for n in (2 * h, 2 * h + 1):
            dve.max(out=self.val[:, n, 0:8], in_=sc[:, n % 2, :])
        dve.drain()
        for n in (2 * h, 2 * h + 1):
            dve.max_index(self.key[:, n, 0:8], self.val[:, n, 0:8], sc[:, n % 2, :])
            dve.match_replace(out=self.rep[n % 2][:, :], in_to_replace=self.val[:, n, 0:8], in_values=sc[:, n % 2, :],
                              imm_value=LOWEST)
        dve.drain()

    def next8(self, dve, h, sc):
        for n in (2 * h, 2 * h + 1):
            dve.max(out=self.val[:, n, 8:16], in_=self.rep[n % 2][:, :])
        dve.drain()
        for n in (2 * h, 2 * h + 1):
            dve.max_index(self.key[:, n, 8:16], self.val[:, n, 8:16], self.rep[n % 2][:, :])
        dve.tensor_tensor(self.cand[:, :, :], self.val[:, 2 * h, :].unsqueeze(2).broadcast_to([P, TOPK, TOPK]),
                          self.val[:, 2 * h + 1, :].unsqueeze(1).broadcast_to([P, TOPK, TOPK]), ALU.add)
        dve.drain()

    def best_sums(self, dve, h, sc):
        flat = [x[:, :, :].rearrange("p a b -> p (a b)") for x in (self.cand, self.cand2)]
        dve.max(out=self.best[:, h, 0:8], in_=flat[0])
        dve.drain()
        dve.max_index(self.place[:, h, 0:8], self.best[:, h, 0:8], flat[0])
        dve.match_replace(out=flat[1], in_to_replace=self.best[:, h, 0:8], in_values=flat[0], imm_value=LOWEST)
        dve.drain()
        dve.max(out=self.best[:, h, 8:16], in_=flat[1])
        dve.drain()
        dve.max_index(self.place[:, h, 8:16], self.best[:, h, 8:16], flat[1])
        dve.drain()


def step6(nc, m, io, sem):
    at = m.at
    G0 = R0 + 80 * KB
    wb = [at(f"s6_wb{s}", [P, KEYS, CHUNK], F32, F0 + 32 * KB * s) for s in range(2)]
    gst = [at(f"s6_g{s}", [P, T], F32, G0 + 4 * KB * s) for s in range(2)]
    oh = [at(f"s6_oh{s}", [P, 3, 4, KEYS], F32R, G0 + 8 * KB + 6 * KB * s) for s in range(2)]
    TW = 8
    sc = at("s6_sc", [P, 2 * PH, KEYS], F32, G0 + 20 * KB)
    eq = at("s6_eq", [P, P, TOPK], BF16, G0 + 28 * KB)
    c = m.picks.end

    def small(name, shape, dt=F32):
        nonlocal c
        t = at(f"s6_{name}", shape, dt, c)
        c += -(-int(np.prod(shape[1:])) * (2 if dt == BF16 else 4) // 32) * 32
        return t

    picks = m.picks
    key, best, place = picks.key, picks.best, picks.place
    keyf = small("keyf", [P, 2 * PH, TOPK], BF16)
    half = [small(f"half{s}", [P, P], U32) for s in range(2)]
    halff = [small(f"halff{s}", [P, P], BF16) for s in range(2)]
    count = small("count", [P, TOPK], BF16)
    pick = small("pick", [P, 3, P])
    pickT = small("pickT", [P, 3, P])
    w_hi = small("w_hi", [P, P], F32R)
    norm = small("norm", [P, 2, PH])
    w_lo = small("w_lo", [P, TW, KEYS])
    assert c <= R0 + 128 * KB
    ctx = ExitStack()
    with ctx:
        w = Weights(m, sem, "s6u", F0 + 64 * KB, R0 + 64 * KB)
        ps = [ctx.enter_context(nc.psum_tensor(f"s6_ps{s}", [P, T], F32)) for s in range(2)]
        pw = ctx.enter_context(nc.psum_tensor("s6_pw", [P, TW, 2, KEYS], F32))
        pt = pw[:, 0:2, :, :].rearrange("p t s k -> p (t s) k")
        gelu = sem("s6_gelu")
        g_stored = [sem(f"s6_gst{s}") for s in range(2)]
        oh_ready, oh_used = sem("s6_ohr"), sem("s6_ohu")
        w_taken, w_added = sem("s6_wt"), sem("s6_wa")
        w_stored = [sem(f"s6_wst{s}") for s in range(2)]
        sc_in, sc_used = sem("s6_scin"), sem("s6_scu")
        ex_in, ex_out, pick_ready, turned = (sem(f"s6_{n}") for n in ("exi", "exo", "pick", "turn"))
        block = ctx.enter_context(nc.Block())
        PAIRS = 4


        @block.sync
        def _(sp):
            def tiles(b):
                with sp.Fori(0, 2 * PAIRS) as i:
                    for s in range(2):
                        w.load(sp, b * 2 * PAIRS + i, s,
                               io["u"][bass.ds((b * 2 * PAIRS + i) * 2 + s, 1)].rearrange("a p k m -> p (a k) m"))

            with sp.Fori(0, NB - 1) as b:
                sp.wait_ge(sc_used, b + 1)
                sp.dma_start(sc[:, :, :], m.scores[bass.ds(b + 1, 1)].rearrange("b p c k -> p (b c) k")).then_inc(sc_in, 16)
                tiles(b)
            tiles(NB - 1)

        @block.scalar
        def _(act):
            def gelu_tile(n, s):
                act.wait_ge(w.used, n * 2 + s + 3)
                act.wait_ge(g_stored[s], n * 16 + 16)
                act.activation(gst[s][:, :], ps[s][:, :], ACT.Gelu)
                act.drain().then_inc(gelu, 1)
                act.dma_start(m.g[bass.ds(n * 2 + s, 1)].rearrange("a p t -> p (a t)"), gst[s][:, :])\
                   .then_inc(g_stored[s], 16)

            def take_w(b, hh, i, s):
                n = (b * 2 + hh) * 2 * PAIRS + i * 2 + s
                act.wait_ge(oh_used, n * 2 + 4)
                act.activation(wb[hh][:, :, bass.ds((i * 2 + s) * TW, TW)].rearrange("p k t -> p t k"),
                               pw[:, :, 0, :], ACT.Copy)
                act.wait_ge(w_added, n + 1)
                act.activation(w_lo[:, :, :], pw[:, :, 1, :], ACT.Copy)
                act.drain().then_inc(w_taken, 1)

            def pair(b, hh, i, last):
                for s in range(2):
                    n = (b * 2 + hh) * PAIRS + i
                    gelu_tile(n, s)
                    if not last:
                        w.round(act, n + 1, s)
                    take_w(b, hh, i, s)

            def store_w(b, hh):
                act.wait_ge(w_added, (b * 2 + hh) * 2 * PAIRS + 2 * PAIRS + 1)
                act.dma_start(m.w[bass.ds(b * 2 + hh, 1)].rearrange("a p k -> p (a k)"),
                              wb[hh][:, :, :].rearrange("p k t -> p (k t)")).then_inc(w_stored[hh], 16)

            def softmax(b):
                act.wait_ge(ex_in, b + 1)
                act.activation(pick[:, 2, :], pick[:, 2, :], ACT.Exp)
                act.drain().then_inc(ex_out, 1)

            def whole_block(b, last=False):
                for hh in range(2):
                    act.wait_ge(w_stored[hh], b * 16 + 16)
                    with act.Fori(0, PAIRS - hh) as i:
                        pair(b, hh, i, False)
                    if hh:
                        if not last:
                            softmax(b + 1)
                        pair(b, hh, PAIRS - 1, last)
                    store_w(b, hh)

            for s in range(2):
                act.sem_inc(g_stored[s], 16)
                act.sem_inc(w_stored[s], 16)
                w.round(act, 0, s)
            softmax(0)
            with act.Fori(0, NB - 1) as b:
                whole_block(b)
            whole_block(NB - 1, last=True)
            for s in range(2):
                act.wait_ge(w_stored[s], 16 * NB + 16)
                act.wait_ge(g_stored[s], 16 * NB * 2 * PAIRS + 16)

        @block.gpsimd
        def _(pool):
            pool.sem_inc(w.split, 2)
            pool.sem_inc(w_added, 1)
            for s in range(2):
                w.remainder(pool, 0, s)

            def pair(b, hh, i, last=False):
                for s in range(2):
                    n = (b * 2 + hh) * PAIRS + i
                    out = wb[hh][:, :, bass.ds((i * 2 + s) * TW, TW)].rearrange("p k t -> p t k")
                    pool.wait_ge(w_taken, n * 2 + s + 2)
                    pool.tensor_tensor(out, out, w_lo[:, :, :], ALU.add).then_inc(w_added, 1)
                    if not last:
                        w.remainder(pool, n + 1, s)

            with pool.Fori(0, NB - 1) as b:
                for hh in range(2):
                    with pool.Fori(0, PAIRS) as i:
                        pair(b, hh, i)
            for hh in range(2):
                with pool.Fori(0, PAIRS - hh) as i:
                    pair(NB - 1, hh, i)
            pair(NB - 1, 1, PAIRS - 1, last=True)

        @block.tensor
        def _(pe):
            def pair(b, hh, i, first=False):
                for s in range(2):
                    n = (b * 2 + hh) * PAIRS + i
                    w.ready(pe, n, s)
                    pe.wait_ge(gelu, n * 2 + s + 1)
                    project(pe, ps[s], w.hi[s], w.lo[s], m.hn_hi, m.hn_lo).then_inc(w.used, 1)
                    if first and s == 0:
                        turn_picks(0)
                    pe.wait_ge(w_taken, n * 2 + s + 1)
                    for q in range(2):
                        pe.wait_ge(oh_ready, (n * 2 + s) * 2 + q + 1)
                        for j in range(4):
                            mm = pe.matmul(pw[:, 4 * q + j, :, :], oh[q][:, 0, j, :], oh[q][:, 1:3, j, :],
                                           start=True, stop=True)
                        mm.then_inc(oh_used, 1)

            def half_block(b, hh):
                with pe.Fori(0, PAIRS) as i:
                    pair(b, hh, i)

            def turn_picks(b):
                pe.wait_ge(pick_ready, b + 1)
                pe.wait_ge(w_taken, b * 2 * 2 * PAIRS + 1)
                for v in range(3):
                    mm = pe.transpose(pt[:, v, :], pick[:, v, :], m.ident[:, :])
                mm.then_inc(turned, 1)

            pe.sem_inc(w.used, 2)
            pe.sem_inc(gelu, 2)
            pe.sem_inc(oh_used, 2)
            pe.sem_inc(w_taken, 1)
            pair(0, 0, 0, first=True)
            with pe.Fori(1, PAIRS) as i:
                pair(0, 0, i)
            half_block(0, 1)
            turn_picks(1)
            with pe.Fori(1, NB - 1) as b:
                for hh in range(2):
                    half_block(b, hh)
                turn_picks(b + 1)
            for hh in range(2):
                half_block(NB - 1, hh)

        @block.vector
        def _(dve):
            def one_hots(r, x):
                dve.wait_ge(oh_used, r * 32 + x + 1)
                for j in range(4):
                    t, o = 4 * x + j, oh[x % 2]
                    dve.tensor_scalar(o[:, 0, j, :], m.iota[:, :], pickT[:, 1, t:t + 1], None, ALU.is_equal)
                    dve.tensor_scalar(o[:, 1, j, :], m.iota[:, :], pickT[:, 0, t:t + 1],
                                      w_hi[:, t:t + 1].bitcast(F32), ALU.is_equal, ALU.mult)
                    dve.tensor_scalar(o[:, 2, j, :], m.iota[:, :], pickT[:, 0, t:t + 1], pickT[:, 2, t:t + 1],
                                      ALU.is_equal, ALU.mult)
                dve.drain().then_inc(oh_ready, 1)

            weights = pick[:, 2, :].rearrange("p (h j) -> p h j", h=PH)
            eq4 = eq[:, :, :].rearrange("p (h j) a -> p h j a", h=PH)

            def places(b):
                flat = place[:, :, :].rearrange("p h j -> p (h j)")
                dve.wait_ge(turned, b + 1)
                dve.tensor_tensor(weights, best[:, :, :], best[:, :, 0:1].broadcast_to([P, PH, TOPK]), ALU.subtract)
                dve.tensor_scalar(half[0][:, :], flat, 4, None, ALU.logical_shift_right)
                dve.tensor_scalar(half[1][:, :], flat, 15, None, ALU.bitwise_and)
                dve.tensor_copy(keyf[:, :, :], key[:, :, :])
                dve.drain().then_inc(ex_in, 1)
                for s in range(2):
                    dve.tensor_copy(halff[s][:, :], half[s][:, :])
                dve.drain()

            def ranked_key(s, part):
                if part == 0:
                    dve.tensor_tensor(eq[:, :, :], halff[s][:, :].unsqueeze(2).broadcast_to([P, P, TOPK]),
                                      count[:, :].unsqueeze(1).broadcast_to([P, P, TOPK]), ALU.is_equal)
                elif part == 1:
                    ranked = keyf[:, :, :].rearrange("p (h s) a -> p h s a", s=2)[:, :, s, :].unsqueeze(2)
                    dve.tensor_tensor(eq4, eq4, ranked.broadcast_to([P, PH, TOPK, TOPK]), ALU.mult)
                else:
                    dve.tensor_reduce(pick[:, s, :], eq[:, :, :], AX.X, ALU.add)
                dve.drain()

            def normalise(b):
                dve.wait_ge(ex_out, b + 1)
                dve.tensor_reduce(norm[:, 0, :], weights, AX.X, ALU.add)
                dve.drain()
                dve.reciprocal(norm[:, 1, :], norm[:, 0, :])
                dve.drain()
                dve.tensor_tensor(weights, weights, norm[:, 1, :].unsqueeze(2).broadcast_to([P, PH, TOPK]), ALU.mult)
                dve.drain().then_inc(pick_ready, 1)

            def take_picks(b):
                dve.wait_ge(turned, b + 2)
                dve.tensor_copy(pickT[:, 0:2, :], pt[:, 0:2, :])
                dve.tensor_copy(w_hi[:, :], pt[:, 2, :])
                dve.drain()
                dve.tensor_tensor(pickT[:, 2, :], pt[:, 2, :], w_hi[:, :].bitcast(F32), ALU.subtract)
                dve.drain()

            def ranking(b, x):
                if x < 3 * PH:
                    picks.part(dve, x // 3, x % 3, sc[:, x // 3 * 2:x // 3 * 2 + 2, :])
                elif x == 24:
                    dve.drain().then_inc(sc_used, 1)
                    places(b)
                elif x < 31:
                    ranked_key((x - 25) // 3, (x - 25) % 3)
                else:
                    normalise(b)
                    take_picks(b)

            dve.sem_inc(turned, 1)
            dve.sem_inc(sc_used, 1)
            dve.tensor_copy(count[:, :], m.iota[:, 0:TOPK])
            dve.memset(norm[:, :, :], 0.0)
            dve.drain()
            places(0)
            for x in range(25, 31):
                ranking(0, x)
            normalise(0)
            take_picks(0)
            with dve.Fori(0, NB - 1) as b:
                dve.wait_ge(sc_in, b * 16 + 16)
                dve.memset(norm[:, :, :], 0.0)
                dve.drain()
                for x in range(32):
                    one_hots(b, x)
                    ranking(b + 1, x)
            for x in range(32):
                one_hots(NB - 1, x)


def step7(nc, m, io, sem):
    GT, Q = 4, 4
    NG = KEYS // GT
    at = m.at
    v_hi = [at(f"s7_vhi{g}", [P, GT, D], F32R, R0 + 32 * KB * g) for g in range(2)]
    v_lo = [at(f"s7_vlo{g}", [P, GT, D], F32R, R0 + 32 * KB * g + 16 * KB) for g in range(2)]
    c_hi = [at(f"s7_chi{g}", [P, GT, T], F32R, R0 + 64 * KB + 32 * KB * g) for g in range(2)]
    c_lo = [at(f"s7_clo{g}", [P, GT, T], F32R, R0 + 64 * KB + 32 * KB * g + 16 * KB) for g in range(2)]
    y = m.y
    vr = [at(f"s7_vr{s}", [P, D], F32, F0 + 32 * KB + 4 * KB * s) for s in range(2)]
    gr = [at(f"s7_gr{s}", [P, T], F32, F0 + 40 * KB + 4 * KB * s) for s in range(2)]
    wr = [at(f"s7_wr{s}", [P, 2 * NB, 2, CHUNK], F32, F0 + 48 * KB + 8 * KB * s) for s in range(2)]
    ctx = ExitStack()
    with ctx:
        ps = [ctx.enter_context(nc.psum_tensor(f"s7_ps{s}", [P, 2, T], F32)) for s in range(2)]
        v_in = [sem(f"s7_v_in{s}") for s in range(2)]
        g_in = [sem(f"s7_g_in{s}") for s in range(2)]
        w_in = [sem(f"s7_w_in{s}") for s in range(2)]
        v_rounded, v_split, coef, c_rounded, c_split = (sem(f"s7_{n}") for n in ("vr_", "vs", "co", "cr", "cs"))
        made, taken = sem("s7_made"), sem("s7_taken")
        block = ctx.enter_context(nc.Block())
        PER = 2 * GT
        w4 = m.w.rearrange("n p (k t) -> p n k t", t=CHUNK)

        @block.sync
        def _(sp):
            with sp.Fori(0, NG // 2) as it:
                for t in range(PER):
                    n = it * PER + t
                    s, p = t % 2, t // 2 % 2
                    sp.wait_ge(v_split, n + 1)
                    sp.dma_start(vr[s][:, :], io["v"][bass.ds(n, 1)].rearrange("a p d -> p (a d)")).then_inc(v_in[s], 16)
                    sp.wait_ge(c_split, n + 1)
                    sp.dma_start(gr[s][:, :], m.g[bass.ds(n, 1)].rearrange("a p t -> p (a t)")).then_inc(g_in[s], 16)
                    if s == 0:
                        sp.dma_start(wr[p][:, :, :, :], w4[:, :, bass.ds(n, 2), :]).then_inc(w_in[p], 16)

        @block.scalar
        def _(act):
            with act.Fori(0, NG // 2) as it:
                for t in range(PER):
                    n, s, g = it * PER + t, t % 2, t // GT
                    if t % GT == 0:
                        act.wait_ge(made, (it * 2 + g + 1) * Q)
                    act.wait_ge(v_in[s], (it * (PER // 2) + t // 2 + 1) * 16)
                    act.activation(v_hi[g][:, t % GT, :], vr[s][:, :], ACT.Copy).then_inc(v_rounded, 1)
                    act.wait_ge(coef, n + 1)
                    act.activation(c_hi[g][:, t % GT, :], gr[s][:, :], ACT.Copy).then_inc(c_rounded, 1)

        @block.gpsimd
        def _(pool):
            pool.sem_inc(v_split, 2)
            with pool.Fori(0, NG // 2) as it:
                for t in range(PER):
                    n, s, g = it * PER + t, t % 2, t // GT
                    pool.wait_ge(v_rounded, n + 1)
                    pool.tensor_tensor(v_lo[g][:, t % GT, :], vr[s][:, :], v_hi[g][:, t % GT, :].bitcast(F32),
                                       ALU.subtract).then_inc(v_split, 1)

        @block.tensor
        def _(pe):
            pe.sem_inc(made, 2 * Q)
            pe.sem_inc(taken, 2)
            with pe.Fori(0, NG // 2) as it:
                for g in range(2):
                    pe.wait_ge(v_split, (it * 2 + g + 1) * GT + 2)
                    pe.wait_ge(c_split, (it * 2 + g + 1) * GT + 2)
                    for qd in range(Q):
                        out = ps[qd % 2]
                        pe.wait_ge(taken, (it * 2 + g) * Q + qd + 1)
                        for dc in range(2):
                            d = slice((2 * qd + dc) * P, (2 * qd + dc + 1) * P)
                            for t in range(GT):
                                halves = [slice(h * HALF, (h + 1) * HALF) for h in range(2)]
                                for c in halves:
                                    pe.matmul(out[:, dc, c], v_hi[g][:, t, d], c_hi[g][:, t, c], start=(t == 0), stop=False)
                                    pe.matmul(out[:, dc, c], v_hi[g][:, t, d], c_lo[g][:, t, c], start=False, stop=False)
                                for c in halves:
                                    mm = pe.matmul(out[:, dc, c], v_lo[g][:, t, d], c_hi[g][:, t, c], start=False,
                                                   stop=(t == GT - 1))
                        mm.then_inc(made, 1)

        @block.vector
        def _(dve):
            def coefficients(it, t):
                n, s, g, p = it * PER + t, t % 2, t // GT, t // 2 % 2
                dve.wait_ge(g_in[s], (it * (PER // 2) + t // 2 + 1) * 16)
                dve.wait_ge(w_in[p], (it * (PER // 4) + t // 4 + 1) * 16)
                if t % GT == 0:
                    dve.wait_ge(made, (it * 2 + g + 1) * Q)
                g3 = gr[s][:, :].rearrange("p (n t) -> p n t", t=CHUNK)
                dve.tensor_tensor(g3, g3, wr[p][:, :, s, :], ALU.mult)
                dve.drain().then_inc(coef, 1)
                dve.wait_ge(c_rounded, n + 1)
                dve.tensor_tensor(c_lo[g][:, t % GT, :], gr[s][:, :], c_hi[g][:, t % GT, :].bitcast(F32),
                                  ALU.subtract).then_inc(c_split, 1)

            def add(group, qd):
                dve.wait_ge(made, (group + 2) * Q + qd + 1)
                dve.tensor_tensor(y[:, 2 * qd:2 * qd + 2, :], y[:, 2 * qd:2 * qd + 2, :], ps[qd % 2][:, :, :], ALU.add)\
                   .then_inc(taken, 1)

            dve.sem_inc(c_split, 2)
            dve.memset(y[:, :, :], 0.0)
            for t in range(GT):
                coefficients(0, t)
            def turn(it, more):
                for g in range(2):
                    for qd in range(Q):
                        if g == 0:
                            coefficients(it, GT + qd)
                        elif more:
                            coefficients(it + 1, qd)
                        add(it * 2 + g, qd)

            with dve.Fori(0, NG // 2 - 1) as it:
                turn(it, True)
            turn(NG // 2 - 1, False)


def step8(nc, m, io, sem):
    at, y = m.at, m.y
    h1 = at("s8_h1", [P, DC, T], F32, R0)
    sq = at("s8_sq", [P, 2, T], F32, R0 + 32 * KB)
    r = at("s8_r", [P, T], F32, R0 + 40 * KB)
    ctx = ExitStack()
    with ctx:
        ps_ss = ctx.enter_context(nc.psum_tensor("s8_ss", [P, T], F32))
        h1_in = [sem(f"s8_h1_in{k}") for k in range(DC)]
        h2_ready, sq_ready, sq_used, ss_ready, inv, root, done, stored = (
            sem(f"s8_{n}") for n in ("h2", "sqr", "squ", "ss", "inv", "root", "done", "st"))
        block = ctx.enter_context(nc.Block())

        @block.sync
        def _(sp):
            for k in range(DC):
                sp.dma_start(h1[:, k, :], m.h1[k]).then_inc(h1_in[k], 16)
            for k in range(DC):
                sp.wait_ge(done, k + 1)
                sp.dma_start(io["out"][k], y[:, k, :]).then_inc(stored, 16)
            sp.wait_ge(stored, 16 * DC)

        @block.scalar
        def _(act):
            for k in range(DC):
                act.wait_ge(h2_ready, k + 1)
                if k >= 2:
                    act.wait_ge(sq_used, k - 1)
                act.activation(sq[:, k % 2, :], y[:, k, :], ACT.Square).then_inc(sq_ready, 1)
            act.wait_ge(inv, 1)
            act.activation(r[:, :], r[:, :], ACT.Sqrt).then_inc(root, 1)

        @block.tensor
        def _(pe):
            for k in range(DC):
                pe.wait_ge(sq_ready, k + 1)
                for h in range(2):
                    mm = pe.matmul(ps_ss[:, h * HALF:(h + 1) * HALF], m.ones[:, :],
                                   sq[:, k % 2, h * HALF:(h + 1) * HALF], start=(k == 0), stop=(k == DC - 1))
                mm.then_inc(sq_used, 1)
            pe.drain().then_inc(ss_ready, 1)

        @block.vector
        def _(dve):
            for k in range(DC):
                dve.wait_ge(h1_in[k], 16)
                dve.scalar_tensor_tensor(y[:, k, :], y[:, k, :], m.mods[:, 5, k:k + 1], h1[:, k, :], ALU.mult,
                                         ALU.add).then_inc(h2_ready, 1)
            dve.wait_ge(ss_ready, 1)
            dve.tensor_scalar(r[:, :], ps_ss[:, :], 1.0 / D, EPS, ALU.mult, ALU.add)
            dve.drain()
            dve.reciprocal(r[:, :], r[:, :]).then_inc(inv, 1)
            dve.wait_ge(root, 1)
            for k in range(DC):
                dve.tensor_tensor(y[:, k, :], y[:, k, :], r[:, :], ALU.mult)
                dve.drain()
                dve.tensor_scalar(y[:, k, :], y[:, k, :], m.mods[:, 7, k:k + 1], m.mods[:, 6, k:k + 1],
                                  ALU.mult, ALU.add).then_inc(done, 1)


STEPS = (step1, step2, step3, step4, step5, step6, step7, step8)


def encoder_layer(nc, io, out, steps=8, scratch="Internal"):
    m = Mem()
    m.at = lambda name, shape, dt, off: nc.alloc_sbuf_tensor_at(name, shape, dt, offset=off)
    m.arena = nc.alloc_sbuf_tensor("arena", [P, (C0 + CB - BASE) // 4], F32)
    free = C0

    def constant(name, shape, dt=F32):
        nonlocal free
        t = m.at(name, shape, dt, free)
        free += -(-int(np.prod(shape[1:])) * 4 // 32) * 32
        assert free <= C0 + CB
        return t

    m.cols = constant("cols", [P, NCOL])
    m.ident = constant("ident", [P, P])
    m.ones = constant("ones", [P, P])
    m.iota = constant("iota", [P, KEYS])
    m.mask = constant("mask", [P, 2, P], I32)
    m.keysT = constant("keysT", [P, 2, KEYS])
    m.mods = constant("mods", [P, 8, DC])
    m.cact = constant("cact", [P, DC])
    m.lb = constant("lb", [P, 2, HEADS])
    m.omlb = constant("omlb", [P, 2, HEADS])
    m.hn_hi = m.at("hn_hi", [P, DC, T], F32R, R0)
    m.hn_lo = m.at("hn_lo", [P, DC, T], F32R, R0 + 32 * KB)
    m.head = head_inputs(m)
    m.picks = Picks(m, R0 + 112 * KB)
    m.y = m.at("y", [P, DC, T], F32, F0)
    m.col = lambda name: m.cols[:, COL[name][0]:COL[name][1]]
    dram = lambda name, shape: nc.dram_tensor(name, shape, F32, kind=scratch).ap()
    m.mix = dram("s_mix", [2 * HEADS, P, T])
    m.h1 = dram("s_h1", [DC, P, T])
    m.scores = dram("s_scores", [NB, P, 2 * PH, KEYS])
    m.g = dram("s_g", [KEYS, KEYS, T])
    m.w = dram("s_w", [2 * NB, P, KEYS * CHUNK])
    for n, step in enumerate((constants,) + STEPS[:steps]):
        sems = []

        def sem(name):
            sems.append(nc.alloc_semaphore(name))
            return sems[-1]

        step(nc, m, io if n < 8 else {**io, "out": out}, sem)
        nc.clear_and_free_semaphores(sems)
        nc.all_engine_barrier()


def kernel(**inputs):
    from concourse import bacc
    from concourse.bass_utils import run_bass_kernel_spmd

    arrays = layouts(inputs)
    nc = bacc.Bacc("TRN2", target_bir_lowering=False, num_devices=1)
    io = {k: nc.dram_tensor(f"in_{k}", v.shape, mybir.dt.from_np(v.dtype), kind="ExternalInput").ap()
          for k, v in arrays.items()}
    out = nc.dram_tensor("out_T", (DC, P, T), F32, kind="ExternalOutput").ap()
    encoder_layer(nc, io, out)
    r = run_bass_kernel_spmd(nc, [{f"in_{k}": v for k, v in arrays.items()}], core_ids=[0])
    got = r.results[0]["out_T"].reshape(D, T)
    return np.ascontiguousarray(got.T).reshape(1, T, D)


def layouts(inputs):
    a = {k: np.asarray(v) for k, v in inputs.items()}
    chunks = lambda v: v.reshape(-1, P).T

    def tiles(w):
        return w.reshape(DC, P, -1, P).transpose(2, 1, 0, 3)

    w = tiles(a["w_in"][0])
    q, ff, fb, i, g, ca, cg = (4 * n for n in range(7))
    order = [x for c in range(CONV_C) for x in (cg + c, ca + c)]
    order += [x for h in range(HEADS) for x in (ff + h, fb + h, q + h, i + h, g + h)]
    mods = np.concatenate([a["ada_w"][0], a["final_ada_w"]], axis=1)
    cols = np.concatenate(
        [chunks(a["ada_b"][0]), chunks(a["final_ada_b"]), chunks(a["norm_mix_g"][0]), chunks(a["norm_ffn_g"][0]),
         chunks(a["final_norm_g"]), chunks(a["c"][0]), chunks(a["hgrn_norm_g"][0]), chunks(a["conv_b"][0]),
         chunks(a["conv_ln_g"][0]), chunks(a["conv_ln_b"][0]), chunks(a["lb_gamma_fwd"]),
         chunks(a["lb_gamma_bwd"]),
         a["conv_w"][0].T.reshape(CONV_C, P, CONV_W).transpose(1, 0, 2).reshape(P, -1)], axis=1)
    out = {
        "xT": a["x"][0].T.reshape(DC, P, T),
        "cols": cols,
        "ada": mods.reshape(DC, P, 8, D).transpose(2, 1, 0, 3),
        "w_in": w[order],
        "w_out": tiles(a["w_out"][0]),
        "wq": tiles(a["peer_wq"][0]),
        "keysT": np.stack([a["peer_keys1"][0].T, a["peer_keys2"][0].T], axis=1),
        "u": a["peer_u"][0].reshape(KEYS, KEYS, DC, P).transpose(0, 3, 2, 1),
        "v": a["peer_v"][0].reshape(KEYS, KEYS, D),
    }
    return {k: np.ascontiguousarray(v) for k, v in out.items()}
```

```python
from contextlib import ExitStack

import numpy as np

import concourse.bass as bass
from concourse import mybir

F32 = mybir.dt.float32
BF16 = mybir.dt.bfloat16
F32R = mybir.dt.float32r
U32 = mybir.dt.uint32
I32 = mybir.dt.int32
ALU = mybir.AluOpType
ACT = mybir.ActivationFunctionType
AX = mybir.AxisListType

P = 128
T = 1024
D = 1024
DC = D // P
HALF = 512
HEADS = 4
CHUNK = 64
NCH = T // CHUNK
CONV_W = 31
PAD = CONV_W // 2
CONV_C = 4
DCONV = CONV_C * P
PROJ_HEAD = 5
HEAD_TILES = ([(x, 0) for x in ("ff", "fb", "q", "v")]
              + [t for h in range(HEADS - 2)
                 for t in (("ff", h + 1), ("fb", h + 1), ("q", h + 1), ("v", h + 1), ("g", h))]
              + [(x, HEADS - 1) for x in ("ff", "fb", "q")] + [("g", HEADS - 2), ("v", HEADS - 1), ("g", HEADS - 1)])
MADE = 4
PH = 8
KEYS = 128
TOPK = 16
NB = T // P
EPS = 1e-6
LOWEST = -3.0e38

COL = {}
_at = 0
for _name, _n in (("mod_b", 64), ("g_mix", 8), ("g_ffn", 8), ("g_fin", 8), ("c", 8), ("g_hgrn", 4),
                  ("conv_b", 4), ("ln_g", 4), ("ln_b", 4), ("gam_f", 8), ("gam_b", 8),
                  ("conv_w", 4 * CONV_W)):
    COL[_name] = (_at, _at + _n)
    _at += _n
NCOL = _at

KB = 1024
BASE = 16512
R0 = BASE
F0 = BASE + 128 * KB
C0 = F0 + 72 * KB
CB = 7 * KB


class Mem:
    pass


def rev(ap, back):
    return ap[:, ::-1] if back else ap


def constants(nc, m, io, sem):
    dma = sem("cols_in")
    with nc.Block() as block:

        @block.sync
        def _(sp):
            sp.dma_start(m.cols[:, :], io["cols"]).then_inc(dma, 16)
            sp.dma_start(m.keysT[:, :, :], io["keysT"]).then_inc(dma, 16)
            sp.wait_ge(dma, 32)

        @block.gpsimd
        def _(pool):
            pool.memset(m.ones[:, :], 1.0)
            pool.memset(m.ident[:, :], 0.0)
            pool.iota(m.iota[:, :], [[1, KEYS]], base=0, channel_multiplier=0,
                      allow_small_or_imprecise_dtypes=True)
            pool.memset(m.mask[:, :, :], 1)
            pool.drain()
            pool.affine_select(out=m.ident[:, :], in_=m.ident[:, :], compare_op=ALU.not_equal, fill=1.0,
                               base=0, pattern=[[-1, P]], channel_multiplier=1)
            for back in range(2):
                sg = -1 if back else 1
                pool.affine_select(out=m.mask[:, back, :], in_=m.mask[:, back, :], compare_op=ALU.is_ge,
                                   fill=0, base=0, pattern=[[sg, P]], channel_multiplier=-sg)
            pool.drain()
            pool.memset(m.mask[0:CHUNK, :, CHUNK:P], 0)
            pool.memset(m.mask[CHUNK:P, :, 0:CHUNK], 0)
            pool.drain()


def step1(nc, m, io, sem):
    at = m.at
    x = at("s1_x", [P, DC, T], F32, F0)
    ada = at("s1_ada", [P, 2, DC, D], F32, R0 + 64 * KB)
    acc = at("s1_acc", [P, 2, D], F32, F0 + 62 * KB)
    sq = at("s1_sq", [P, 2, T], F32, F0 + 32 * KB)
    r = at("s1_r", [P, T], F32, F0 + 48 * KB)
    raw = at("s1_raw", [P, 2, T], F32, F0 + 40 * KB)
    LO_POOL = 3
    lbt = at("s1_lbt", [P, 8, HEADS], F32, F0 + 61 * KB)
    col = m.col
    ctx = ExitStack()
    with ctx:
        ps_mod = ctx.enter_context(nc.psum_tensor("s1_mod", [P, 2 * DC], F32))
        ps_ss = ctx.enter_context(nc.psum_tensor("s1_ss", [P, T], F32))
        x_in = [sem(f"s1_x_in{k}") for k in range(DC)]
        ada_in = [sem(f"s1_ada_in{k}") for k in range(4)]
        acc_ready, cact_done, sq_ready, sq_used = sem("s1_acc_r"), sem("s1_cact"), sem("s1_sq_r"), sem("s1_sq_u")
        ss_ready, inv_ready, r_ready, mod_ready = sem("s1_ss"), sem("s1_inv"), sem("s1_r_s"), sem("s1_mod_r")
        y_ready, hi_ready, xn_ready, lbe, lbx = sem("s1_y_r"), sem("s1_hi"), sem("s1_xn"), sem("s1_lbe"), sem("s1_lbx")
        w_in, w_rounded = [sem(f"s1_w_in{s}") for s in range(2)], sem("s1_w_r")
        block = ctx.enter_context(nc.Block())

        @block.sync
        def _(sp):
            for k in range(DC):
                sp.dma_start(x[:, k, :], io["xT"][k]).then_inc(x_in[k], 16)
            for n in range(4):
                v, ks = n // 2, slice(n % 2 * 4, n % 2 * 4 + 4)
                sp.dma_start(ada[:, v, ks, :], io["ada"][v][:, ks, :]).then_inc(ada_in[n], 16)
            sp.wait_ge(sq_used, DC)
            for n in range(2):
                sp.dma_start(raw[:, n, :], io["w_in"][n].rearrange("p k m -> p (k m)")).then_inc(w_in[n], 16)

        @block.scalar
        def _(act):
            act.activation(m.cact[:, :], col("c"), ACT.Silu).then_inc(cact_done, 1)
            for k in range(DC):
                act.wait_ge(x_in[k], 16)
                if k >= 2:
                    act.wait_ge(sq_used, k - 1)
                act.activation(sq[:, k % 2, :], x[:, k, :], ACT.Square).then_inc(sq_ready, 1)
            act.wait_ge(lbx, 1)
            act.activation(lbt[:, 4:8, :], lbt[:, 0:4, :], ACT.Exp).then_inc(lbe, 1)
            act.wait_ge(inv_ready, 1)
            act.activation(r[:, :], r[:, :], ACT.Sqrt).then_inc(r_ready, 1)
            act.wait_ge(acc_ready, 1)
            for n in range(2):
                act.wait_ge(w_in[n], 16)
                act.activation(m.w_hi[n][:, :, :].rearrange("p k m -> p (k m)"), raw[:, n, :], ACT.Copy)\
                    .then_inc(w_rounded, 1)
            for k in range(DC):
                act.wait_ge(y_ready, k + 1)
                act.activation(m.hn_hi[:, k, :], x[:, k, :], ACT.Copy).then_inc(hi_ready, 1)

        @block.gpsimd
        def _(pool):
            pool.wait_ge(r_ready, 1)
            for k in range(DC):
                pool.tensor_tensor(x[:, k, :], x[:, k, :], r[:, :], ALU.mult).then_inc(xn_ready, 1)
            for n in range(2):
                pool.wait_ge(w_rounded, n + 1)
                flat = [x[n][:, :, :].rearrange("p k m -> p (k m)") for x in (m.w_lo, m.w_hi)]
                pool.tensor_tensor(flat[0], raw[:, n, :], flat[1].bitcast(F32), ALU.subtract)
            for k in range(DC - LO_POOL, DC):
                pool.wait_ge(hi_ready, k + 1)
                pool.tensor_tensor(m.hn_lo[:, k, :], x[:, k, :], m.hn_hi[:, k, :].bitcast(F32), ALU.subtract)

        @block.tensor
        def _(pe):
            for k in range(DC):
                pe.wait_ge(sq_ready, k + 1)
                for h in range(2):
                    mm = pe.matmul(ps_ss[:, h * HALF:(h + 1) * HALF], m.ones[:, :],
                                   sq[:, k % 2, h * HALF:(h + 1) * HALF], start=(k == 0), stop=(k == DC - 1))
                mm.then_inc(sq_used, 1)
            mm2 = pe.drain()
            mm2.then_inc(ss_ready, 1)
            for v in range(2):
                pe.wait_ge(acc_ready, v + 1)
                for c in range(DC):
                    pe.matmul(ps_mod[:, v * DC + c:v * DC + c + 1], acc[:, v, c * P:(c + 1) * P], m.ones[:, 0:1],
                              start=True, stop=True)
            pe.drain().then_inc(mod_ready, 1)

        @block.vector
        def _(dve):
            def accumulate(v):
                for k in range(DC):
                    if k % 4 == 0:
                        dve.wait_ge(ada_in[2 * v + k // 4], 16)
                    if k == 0:
                        dve.tensor_scalar(acc[:, v, :], ada[:, v, k, :], m.cact[:, k:k + 1], None, ALU.mult)
                    else:
                        dve.scalar_tensor_tensor(acc[:, v, :], ada[:, v, k, :], m.cact[:, k:k + 1], acc[:, v, :],
                                                 ALU.mult, ALU.add)
                    dve.drain()
                dve.drain().then_inc(acc_ready, 1)

            gam = m.cols[:, COL["gam_f"][0]:COL["gam_b"][1]].rearrange("p (d l h) -> p d l h", d=2, l=2)
            for d in range(2):
                dve.tensor_tensor(lbt[:, 4 + d, :], gam[:, d, 0, :], gam[:, d, 1, :], ALU.max)
            dve.drain()
            for d in range(2):
                for l in range(2):
                    dve.tensor_tensor(lbt[:, 2 * d + l, :], gam[:, d, l, :], lbt[:, 4 + d, :], ALU.subtract)
            dve.drain().then_inc(lbx, 1)
            dve.wait_ge(cact_done, 1)
            accumulate(0)
            dve.wait_ge(ss_ready, 1)
            dve.tensor_scalar(r[:, :], ps_ss[:, :], 1.0 / D, EPS, ALU.mult, ALU.add)
            dve.drain()
            dve.reciprocal(r[:, :], r[:, :]).then_inc(inv_ready, 1)
            accumulate(1)
            dve.wait_ge(lbe, 1)
            for d in range(2):
                dve.tensor_tensor(lbt[:, d, :], lbt[:, 4 + 2 * d, :], lbt[:, 5 + 2 * d, :], ALU.add)
            dve.drain()
            dve.reciprocal(lbt[:, 2:4, :], lbt[:, 0:2, :])
            dve.drain()
            for d in range(2):
                dve.tensor_tensor(m.lb[:, d, :], lbt[:, 4 + 2 * d, :], lbt[:, 2 + d, :], ALU.mult)
            dve.drain()
            dve.tensor_scalar(m.omlb[:, :, :], m.lb[:, :, :], -1.0, 1.0, ALU.mult, ALU.add)
            dve.wait_ge(mod_ready, 1)
            dve.tensor_tensor(m.mods[:, 0:2, :], ps_mod[:, :].rearrange("p (v k) -> p v k", v=2),
                              col("mod_b")[:, 0:2 * DC].rearrange("p (v k) -> p v k", v=2), ALU.add)
            dve.drain()
            dve.scalar_tensor_tensor(m.mods[:, 1, :], m.mods[:, 1, :], 1.0, col("g_mix"), ALU.add, ALU.mult)
            dve.drain()
            def remainder(k):
                dve.wait_ge(hi_ready, k + 1)
                dve.tensor_tensor(m.hn_lo[:, k, :], x[:, k, :], m.hn_hi[:, k, :].bitcast(F32), ALU.subtract)

            for k in range(DC):
                dve.wait_ge(xn_ready, k + 1)
                dve.tensor_scalar(x[:, k, :], x[:, k, :], m.mods[:, 1, k:k + 1],
                                  m.mods[:, 0, k:k + 1], ALU.mult, ALU.add).then_inc(y_ready, 1)
                if 2 <= k < DC - LO_POOL + 2:
                    remainder(k - 2)


class Weights:

    def __init__(self, m, sem, name, raw_at):
        self.raw = [m.at(f"{name}_raw{s}", [P, DC, P], F32, raw_at + s * 4 * KB) for s in range(2)]
        self.hi, self.lo = m.w_hi, m.w_lo
        self.arrived = [sem(f"{name}_arrived{s}") for s in range(2)]
        self.rounded, self.split, self.used = sem(f"{name}_rounded"), sem(f"{name}_split"), sem(f"{name}_used")

    def begin(self, pe):
        for s in range(2):
            pe.sem_inc(self.arrived[s], 16)
        for count, start in ((self.rounded, 2), (self.split, 4), (self.used, 2)):
            pe.sem_inc(count, start)

    def load(self, sp, pair, s, src):
        sp.wait_ge(self.split, pair * 2 + s + 1)
        sp.dma_start(self.raw[s][:, :, :], src).then_inc(self.arrived[s], 16)

    def round(self, act, pair, s):
        act.wait_ge(self.arrived[s], pair * 16 + 16)
        act.wait_ge(self.used, pair * 2 + s + 1)
        act.activation(self.hi[s][:, :, :], self.raw[s][:, :, :], ACT.Copy).then_inc(self.rounded, 1)

    def remainder(self, pool, pair, s):
        pool.wait_ge(self.rounded, pair * 2 + s + 1)
        pool.tensor_tensor(self.lo[s][:, :, :], self.raw[s][:, :, :], self.hi[s][:, :, :].bitcast(F32),
                           ALU.subtract).then_inc(self.split, 1)

    def ready(self, pe, pair, s):
        pe.wait_ge(self.split, pair * 2 + s + 3)


def project(pe, out, w_hi, w_lo, x_hi, x_lo, ks=range(DC)):
    for k in ks:
        for h in range(2):
            c = slice(h * HALF, (h + 1) * HALF)
            pe.matmul(out[:, c], w_hi[:, k, :], x_hi[:, k, c], start=(k == 0), stop=False)
            pe.matmul(out[:, c], w_hi[:, k, :], x_lo[:, k, c], start=False, stop=False)
        for h in range(2):
            c = slice(h * HALF, (h + 1) * HALF)
            mm = pe.matmul(out[:, c], w_lo[:, k, :], x_hi[:, k, c], start=False, stop=(k == DC - 1))
    return mm


def head_inputs(m):
    h, W = Mem(), 4 * KB
    h.low = [m.at(f"head_low{d}", [P, T], F32, F0 + W * d) for d in range(2)]
    h.kk = [m.at(f"head_k{d}", [P, T], F32, F0 + W * (2 + d)) for d in range(2)]
    h.q, h.vT = (m.at(f"head_{n}", [P, T], F32, F0 + W * k) for n, k in (("q", 4), ("vT", 5)))
    return h


def step2(nc, m, io, sem):
    at, col = m.at, m.col
    A_SLOTS, A_PER = 3, 12
    head0 = m.head
    f = F0 + 28 * KB
    hp = at("s2_hp", [P, T + 2 * PAD], F32, f)
    acc = at("s2_acc", [P, CONV_C, T], F32, f + 5 * KB)
    work = at("s2_work", [P, T], F32, f + 21 * KB)
    tap = at("s2_tap", [P, CONV_W + 1], F32, f + 25 * KB)
    ccol = at("s2_ccol", [P, 2], F32, f + 25 * KB + 512)
    r = at("s2_r", [P, T], F32, f + 26 * KB)
    sig = at("s2_sig", [P, T], F32, f + 38 * KB)
    e = R0 + 80 * KB
    vec = at("s2_vec", [P, 6, D], F32, e)
    ada = at("s2_ada", [P, A_SLOTS, D], F32, e + 24 * KB)
    prod = at("s2_prod", [P, 2, D], F32, e + 36 * KB)
    sq = [at(f"s2_sq{s}", [P, T], F32, (e + 44 * KB, f + 38 * KB)[s]) for s in range(2)]
    ctx = ExitStack()
    with ctx:
        w = Weights(m, sem, "s2w", f + 30 * KB)
        ps = [ctx.enter_context(nc.psum_tensor(f"s2_ps{s}", [P, T], F32)) for s in range(2)]
        ps_mu = ctx.enter_context(nc.psum_tensor("s2_mu", [P, T], F32))
        ps_var = ctx.enter_context(nc.psum_tensor("s2_var", [P, T], F32))
        sig_ready, glu_done = sem("s2_sig_r"), sem("s2_glu")
        conv_done, mu_ready, d_ready, sq_ready, sq_used = (sem(f"s2_{n}") for n in ("conv", "mu", "d", "sqr", "squ"))
        var_ready, inv_ready, r_ready, xr, stored = (sem(f"s2_{n}") for n in ("var", "inv", "r_s", "xr", "out"))
        ada_in = [sem(f"s2_ada_in{s}") for s in range(A_SLOTS)]
        ada_used, prod_ready, prod_used, vec_ready, mod_ready = (
            sem(f"s2_{n}") for n in ("adau", "pr", "pu", "vec", "mod"))
        evac = sem("s2_evac")
        H0 = 2 * CONV_C
        block = ctx.enter_context(nc.Block())

        @block.sync
        def _(sp):
            def load(c):
                for s in range(2):
                    w.load(sp, c, s, io["w_in"][bass.ds(c * 2 + s, 1)].rearrange("a p k m -> p (a k) m"))

            def rows(c, items):
                for i in items:
                    sp.wait_ge(ada_used, c * A_PER + i + 1)
                    sp.dma_start(ada[:, i % A_SLOTS, :], io["ada"][2 + i % 6][:, bass.ds(c * 2 + i // 6, 1), :]
                                 .rearrange("p a m -> p (a m)")).then_inc(ada_in[i % A_SLOTS], 16)

            with sp.Fori(0, CONV_C - 1) as c:
                load(c + 1)
                rows(c, range(A_PER))
            load(CONV_C)
            rows(CONV_C - 1, range(6))
            load(CONV_C + 1)
            rows(CONV_C - 1, range(6, A_PER))
            load(CONV_C + 2)

        @block.scalar
        def _(act):
            def sigmoid(c):
                act.wait_ge(w.used, c * 2 + 3)
                act.wait_ge(glu_done, c + 1)
                act.activation(sig[:, :], ps[0][:, :], ACT.Sigmoid).then_inc(sig_ready, 1)

            def scale_rows(c, items):
                for i in items:
                    if i == 0:
                        act.activation(ccol[:, :], m.cact[:, bass.ds(c * 2, 2)], ACT.Copy)
                        act.drain()
                    act.wait_ge(ada_in[i % A_SLOTS], (c * (A_PER // A_SLOTS) + i // A_SLOTS + 1) * 16)
                    act.wait_ge(prod_used, c * A_PER + i + 1)
                    act.activation(prod[:, i % 2, :], ada[:, i % A_SLOTS, :], ACT.Copy,
                                   scale=ccol[:, i // 6:i // 6 + 1])
                    act.drain().then_inc(prod_ready, 1)
                    act.sem_inc(ada_used, 1)

            def take(n):
                act.wait_ge(w.used, H0 + n + 3)
                src = ps[n % 2][:, :]
                if n < 2:
                    act.activation(head0.low[n][:, :], src, ACT.Sigmoid)
                    act.activation(head0.kk[n][:, :], src, ACT.Sigmoid, scale=-1.0)
                elif n == 2:
                    act.activation(head0.q[:, :], src, ACT.Silu)
                else:
                    act.activation(head0.vT[:, :], src, ACT.Copy)
                act.drain().then_inc(evac, 1)

            act.sem_inc(sig_ready, 1)
            act.sem_inc(ada_used, A_SLOTS)
            act.sem_inc(prod_used, 2)
            with act.Fori(0, CONV_C - 1) as c:
                sigmoid(c)
                w.round(act, c + 1, 0)
                w.round(act, c + 1, 1)
                scale_rows(c, range(A_PER))
            sigmoid(CONV_C - 1)
            w.round(act, CONV_C, 0)
            w.round(act, CONV_C, 1)
            scale_rows(CONV_C - 1, range(6))
            for n in range(2):
                take(n)
                w.round(act, CONV_C + 1, n)
            scale_rows(CONV_C - 1, range(6, A_PER))
            for n in range(2):
                take(2 + n)
                w.round(act, CONV_C + 2, n)
            for c in range(CONV_C):
                act.wait_ge(d_ready, c + 1)
                if c >= 2:
                    act.wait_ge(sq_used, c - 1)
                act.activation(sq[c % 2][:, :], acc[:, c, :], ACT.Square).then_inc(sq_ready, 1)
            act.wait_ge(inv_ready, 1)
            act.activation(r[:, :], r[:, :], ACT.Sqrt).then_inc(r_ready, 1)
            for c in range(CONV_C):
                act.wait_ge(xr, c + 1)
                lg, lb = COL["ln_g"][0] + c, COL["ln_b"][0] + c
                act.activation(acc[:, c, :], acc[:, c, :], ACT.Silu, scale=m.cols[:, lg:lg + 1],
                               bias=m.cols[:, lb:lb + 1])
                act.drain()
                act.dma_start(m.mix[HEADS + c], acc[:, c, :]).then_inc(stored, 16)
            act.wait_ge(stored, 16 * CONV_C)

        @block.gpsimd
        def _(pool):
            pool.memset(vec[:, :, :], 0.0)

            def remainders(c):
                for s in range(2):
                    w.remainder(pool, c, s)

            def add_rows(c, items):
                for i in items:
                    if i % 6 == 0:
                        pool.drain()
                    pool.wait_ge(prod_ready, c * A_PER + i + 1)
                    pool.tensor_tensor(vec[:, i % 6, :], vec[:, i % 6, :], prod[:, i % 2, :], ALU.add)\
                        .then_inc(prod_used, 1)

            with pool.Fori(0, CONV_C - 1) as c:
                remainders(c + 1)
                add_rows(c, range(A_PER))
            remainders(CONV_C)
            add_rows(CONV_C - 1, range(6))
            remainders(CONV_C + 1)
            add_rows(CONV_C - 1, range(6, A_PER))
            pool.drain().then_inc(vec_ready, 1)
            remainders(CONV_C + 2)

        @block.tensor
        def _(pe):
            w.begin(pe)
            with pe.Fori(0, CONV_C) as c:
                w.ready(pe, c, 0)
                pe.wait_ge(sig_ready, c + 1)
                project(pe, ps[0], w.hi[0], w.lo[0], m.hn_hi, m.hn_lo).then_inc(w.used, 1)
                w.ready(pe, c, 1)
                pe.wait_ge(glu_done, c + 1)
                project(pe, ps[1], w.hi[1], w.lo[1], m.hn_hi, m.hn_lo).then_inc(w.used, 1)
            for n in range(4):
                w.ready(pe, (H0 + n) // 2, n % 2)
                if n == 0:
                    pe.wait_ge(sig_ready, CONV_C + 1)
                elif n == 1:
                    pe.wait_ge(glu_done, CONV_C + 1)
                else:
                    pe.wait_ge(evac, n - 1)
                project(pe, ps[n % 2], w.hi[n % 2], w.lo[n % 2], m.hn_hi, m.hn_lo).then_inc(w.used, 1)
            for c in range(CONV_C):
                pe.wait_ge(conv_done, c + 1)
                for h in range(2):
                    mm = pe.matmul(ps_mu[:, h * HALF:(h + 1) * HALF], m.ones[:, :],
                                   acc[:, c, h * HALF:(h + 1) * HALF], start=(c == 0), stop=(c == CONV_C - 1))
            mm.then_inc(mu_ready, 1)
            for c in range(CONV_C):
                pe.wait_ge(sq_ready, c + 1)
                for h in range(2):
                    mm = pe.matmul(ps_var[:, h * HALF:(h + 1) * HALF], m.ones[:, :],
                                   sq[c % 2][:, h * HALF:(h + 1) * HALF], start=(c == 0), stop=(c == CONV_C - 1))
                mm.then_inc(sq_used, 1)
            pe.drain().then_inc(var_ready, 1)
            pe.wait_ge(vec_ready, 1)
            for v in range(6):
                for c in range(DC):
                    mm = pe.matmul(ps_mu[:, v * DC + c:v * DC + c + 1], vec[:, v, c * P:(c + 1) * P], m.ones[:, 0:1],
                                   start=True, stop=True)
            pe.drain().then_inc(mod_ready, 1)

        @block.vector
        def _(dve):
            dve.sem_inc(glu_done, 1)
            dve.memset(hp[:, 0:PAD], 0.0)
            dve.memset(hp[:, PAD + T:T + 2 * PAD], 0.0)
            cw = m.cols[:, COL["conv_w"][0]:COL["conv_w"][1]].rearrange("p (c k) -> p c k", c=CONV_C)
            with dve.Fori(0, CONV_C) as c:
                dve.tensor_copy(tap[:, 0:CONV_W], cw[:, bass.ds(c, 1), :])
                dve.tensor_copy(tap[:, CONV_W:CONV_W + 1], m.cols[:, bass.ds(c + COL["conv_b"][0], 1)])
                dve.wait_ge(sig_ready, c + 2)
                dve.wait_ge(w.used, c * 2 + 4)
                dve.tensor_tensor(hp[:, PAD:PAD + T], ps[1][:, :], sig[:, :], ALU.mult).then_inc(glu_done, 1)
                dve.drain()
                dve.tensor_scalar(work[:, :], hp[:, 0:T], tap[:, 0:1], tap[:, CONV_W:CONV_W + 1], ALU.mult, ALU.add)
                for k in range(1, CONV_W):
                    dve.drain()
                    dst = work[:, :] if k < CONV_W - 1 else acc[:, bass.ds(c, 1), :].rearrange("p a t -> p (a t)")
                    dve.scalar_tensor_tensor(dst, hp[:, k:k + T], tap[:, k:k + 1], work[:, :], ALU.mult, ALU.add)
                dve.drain().then_inc(conv_done, 1)
            dve.wait_ge(mu_ready, 1)
            for c in range(CONV_C):
                dve.scalar_tensor_tensor(acc[:, c, :], ps_mu[:, :], -1.0 / DCONV, acc[:, c, :], ALU.mult, ALU.add)
                dve.drain().then_inc(d_ready, 1)
            dve.wait_ge(var_ready, 1)
            dve.tensor_scalar(r[:, :], ps_var[:, :], 1.0 / DCONV, EPS, ALU.mult, ALU.add)
            dve.drain()
            dve.reciprocal(r[:, :], r[:, :]).then_inc(inv_ready, 1)
            dve.wait_ge(r_ready, 1)
            for c in range(CONV_C):
                dve.tensor_tensor(acc[:, c, :], acc[:, c, :], r[:, :], ALU.mult).then_inc(xr, 1)
            dve.wait_ge(mod_ready, 1)
            dve.tensor_tensor(m.mods[:, 2:8, :], ps_mu[:, 0:6 * DC].rearrange("p (v k) -> p v k", v=6),
                              col("mod_b")[:, 2 * DC:].rearrange("p (v k) -> p v k", v=6), ALU.add)
            dve.drain()
            for v, g in ((4, "g_ffn"), (7, "g_fin")):
                dve.scalar_tensor_tensor(m.mods[:, v, :], m.mods[:, v, :], 1.0, col(g), ALU.add, ALU.mult)
            dve.drain()


def step3(nc, m, io, sem):
    at = m.at
    W = 4 * KB
    f = [F0 + n * W for n in range(18)]
    low, kk, q, vT = m.head.low, m.head.kk, m.head.q, m.head.vT
    vtok = at("s3_vtok", [P, NB, P], F32, f[7])
    qe = [at(f"s3_qe{d}", [P, T], F32, f[8 + 4 * d]) for d in range(2)]
    ku = [at(f"s3_ku{d}", [P, T], F32, f[9 + 4 * d]) for d in range(2)]
    qr = [at(f"s3_qr{d}", [P, T], F32, f[10 + 4 * d]) for d in range(2)]
    kr = [at(f"s3_kr{d}", [P, T], F32, f[11 + 4 * d]) for d in range(2)]
    reset, o = at("s3_reset", [P, T], F32, f[16]), at("s3_o", [P, T], F32, f[17])
    e = R0 + 80 * KB
    state = [at(f"s3_state{d}", [P, NCH, P], F32, e + 8 * KB * d) for d in range(2)]
    st = [at(f"s3_st{d}", [P, NB, P], F32, e + 16 * KB + W * d) for d in range(2)]
    kt = [at(f"s3_kt{d}", [P, NB, P], F32, e + 24 * KB + W * d) for d in range(2)]
    sq = at("s3_sq", [P, T], F32, e + 24 * KB)
    r = at("s3_r", [P, T], F32, e + 41 * KB)
    dec = at("s3_dec", [P, 2, NCH], F32, e + 32 * KB)
    g = at("s3_g", [P, T], F32, f[6])
    ctx = ExitStack()
    with ctx:
        w = Weights(m, sem, "s3w", e + 33 * KB)
        ps = [ctx.enter_context(nc.psum_tensor(f"s3_ps{s}", [P, T], F32)) for s in range(2)]
        po = ctx.enter_context(nc.psum_tensor("s3_po", [P, T], F32))
        pm = [ctx.enter_context(nc.psum_tensor(f"s3_pm{s}", [P, HALF], F32)) for s in range(2)]
        const, evac = sem("s3_const"), sem("s3_evac")
        k_ready = [sem(f"s3_k_r{d}") for d in range(2)]
        log_ready = [sem(f"s3_log{d}") for d in range(2)]
        prep = [sem(f"s3_prep{d}") for d in range(2)]
        powers = [sem(f"s3_pow{d}") for d in range(2)]
        ku_power = [sem(f"s3_kup{d}") for d in range(2)]
        ku_ready = [sem(f"s3_ku_r{d}") for d in range(2)]
        factors = [sem(f"s3_fac{d}") for d in range(2)]
        q_ready, v_ready, g_ready = sem("s3_q_r"), sem("s3_v_r"), sem("s3_g_r")
        v_turned, vtok_ready = sem("s3_vturn"), sem("s3_vtok_r")
        pm_ready = [sem(f"s3_pm_r{s}") for s in range(2)]
        pm_used = [sem(f"s3_pm_u{s}") for s in range(2)]
        o_ready, o_copied, sq_ready = sem("s3_o_r"), sem("s3_o_c"), sem("s3_sq_r")
        mix_hi, mix_lo = sem("s3_mix_hi"), sem("s3_mix_lo")
        inv, root, done, stored = sem("s3_inv"), sem("s3_root"), sem("s3_done"), sem("s3_stored")
        block = ctx.enter_context(nc.Block())
        W0, NT = 2 * CONV_C + MADE, len(HEAD_TILES) - MADE

        def allowed(quad, d):
            t0 = quad // 2 * CHUNK + (quad % 2 * 32 if d == 0 else 0)
            t1 = quad // 2 * CHUNK + (CHUNK if d == 0 else quad % 2 * 32 + 32)
            return slice(32 * quad, 32 * quad + 32), t0, t1

        def place(part, d, odd, i):
            first = odd if d == 0 else 1 - odd
            n = 4 * part + 2 * i + first
            return n, (NCH - 1 - n if d else n)

        FROM_DRAM = [HEADS + c for c in range(CONV_C)] + list(range(HEADS - 1))
        raw = [x[:, :, :].rearrange("p k m -> p (k m)") for x in w.raw]

        def tile_of(kind, h):
            return HEAD_TILES.index((kind, h)) - MADE

        @block.sync
        def _(sp):
            with sp.Fori(1, NT // 2) as n:
                for s in range(2):
                    w.load(sp, n, s, io["w_in"][bass.ds(n * 2 + W0 + s, 1)].rearrange("a p k m -> p (a k) m"))

            for s in range(2):
                w.load(sp, NT // 2, s, io["w_out"][s])
            for i, k in enumerate(FROM_DRAM):
                if i < 2:
                    sp.wait_ge(w.split, NT + i + 3)
                else:
                    sp.wait_ge(mix_lo, i - 1)
                if k < HEADS:
                    sp.wait_ge(stored, 16 * (k + 1))
                sp.dma_start(raw[i % 2], m.mix[k]).then_inc(w.arrived[i % 2], 16)

        @block.gpsimd
        def _(pool):
            pool.memset(reset[:, :], 1.0)
            pool.drain()
            pool.memset(reset[:, 0::CHUNK], 0.0)
            for d in range(2):
                pool.memset(st[d][:, :, :], 0.0)
                pool.memset(state[d][:, 0, :], 0.0)
            pool.drain().then_inc(const, 1)
            with pool.Fori(1, NT // 2 + 1) as n:
                for s in range(2):
                    w.remainder(pool, n, s)
            for i, k in enumerate(FROM_DRAM + [HEADS - 1]):
                pool.wait_ge(mix_hi, i + 1)
                pool.tensor_tensor(m.hn_lo[:, k, :], raw[i % 2] if i < len(FROM_DRAM) else o[:, :],
                                   m.hn_hi[:, k, :].bitcast(F32), ALU.subtract).then_inc(mix_lo, 1)

        @block.tensor
        def _(pe):
            def project_part(kind, h, ks):
                n = tile_of(kind, h)
                if 0 in ks:
                    w.ready(pe, n // 2, n % 2)
                    if n >= 2:
                        pe.wait_ge(evac, n - 1)
                mm = project(pe, ps[n % 2], w.hi[n % 2], w.lo[n % 2], m.hn_hi, m.hn_lo, ks)
                if DC - 1 in ks:
                    mm.then_inc(w.used, 1)

            def project_tiles(h, *kinds):
                for kind in kinds:
                    project_part(kind, h, range(DC))

            def recurrence(h):
                count = [0, 0]

                def batch(i, make):
                    b = i % 2
                    if 9 * h + count[b]:
                        pe.wait_ge(pm_used[b], 9 * h + count[b])
                    count[b] += 1
                    for j in range(4):
                        mm = make(pm[b][:, j * P:(j + 1) * P], j)
                    mm.then_inc(pm_ready[b], 1)

                pe.wait_ge(v_ready, h + 1)
                if h:
                    pe.wait_ge(o_copied, h)
                    pe.wait_ge(sq_ready, h)
                for b in range(NB):
                    mm = pe.transpose(po[:, b * P:(b + 1) * P], vT[:, b * P:(b + 1) * P], m.ident[:, :])
                mm.then_inc(v_turned, 1)
                for d in range(2):
                    pe.wait_ge(ku_ready[d], h + 1)
                    for half in range(2):
                        batch(half, lambda out, j: pe.transpose(
                            out, ku[d][:, (4 * half + j) * P:(4 * half + j + 1) * P], m.ident[:, :]))
                for d in range(2):
                    pe.wait_ge(factors[d], h + 1)
                    for half in range(2):
                        def scores(out, j):
                            c = (4 * half + j) * P
                            for quad in range(4):
                                rows, t0, t1 = allowed(quad, d)
                                mm = pe.matmul(out[rows, t0:t1], kr[d][:, c + 32 * quad:c + 32 * quad + 32],
                                               qr[d][:, c + t0:c + t1], start=True, stop=True)
                            return mm
                        batch(half, scores)
                if h + 2 < HEADS:
                    project_tiles(h + 1, "v")
                pe.wait_ge(vtok_ready, h + 1)
                for part in range(4):
                    for odd in range(2):
                        def products(out, j):
                            d = j // 2
                            n, c = place(part, d, odd, j % 2)
                            rows = slice(odd * CHUNK, (odd + 1) * CHUNK)
                            return pe.matmul(out, kt[d][rows, c // 2, :], vtok[rows, c // 2, :], start=True, stop=True)
                        batch(odd, products)
                    project_part("g", h, range(2 * part, 2 * part + 2))
                for b in range(2):
                    pe.wait_ge(pm_used[b], 9 * h + 8)
                for b in range(NB):
                    c = slice(b * P, (b + 1) * P)
                    pe.matmul(po[:, c], vtok[:, b, :], st[0][:, b, :], start=True, stop=False)
                    pe.matmul(po[:, c], vtok[:, b, :], st[1][:, b, :], start=False, stop=False)
                    for n in (2 * b, 2 * b + 1):
                        t = slice(n * CHUNK, (n + 1) * CHUNK)
                        pe.matmul(po[:, t], state[0][:, n, :], qe[0][:, t], start=False, stop=False)
                        mm = pe.matmul(po[:, t], state[1][:, NCH - 1 - n, :], qe[1][:, t], start=False, stop=(n % 2 == 1))
                mm.then_inc(o_ready, 1)

            def sums(h):
                pe.wait_ge(sq_ready, h + 1)
                for b in range(2):
                    pe.matmul(pm[b][:, :], m.ones[:, :], sq[:, b * HALF:(b + 1) * HALF],
                              start=True, stop=True).then_inc(pm_ready[b], 1)

            w.begin(pe)
            project_tiles(1, "ff", "fb", "q")
            for h in range(HEADS):
                recurrence(h)
                if h + 2 < HEADS:
                    project_tiles(h + 2, "ff")
                    sums(h)
                    project_tiles(h + 2, "fb", "q")
                else:
                    if h + 2 == HEADS:
                        project_tiles(h + 1, "v")
                    sums(h)

        @block.scalar
        def _(act):
            def round_tile(n):
                if n < NT + 2:
                    w.round(act, n // 2, n % 2)

            def forget(h, d):
                n = tile_of(("ff", "fb")[d], h)
                act.wait_ge(w.used, n + 3)
                if h:
                    act.wait_ge(factors[d], h)
                act.activation(low[d][:, :], ps[n % 2][:, :], ACT.Sigmoid)
                act.activation(kk[d][:, :], ps[n % 2][:, :], ACT.Sigmoid, scale=-1.0)
                act.drain().then_inc(k_ready[d], 1)
                act.sem_inc(evac, 1)
                round_tile(n + 2)

            def query(h):
                n = tile_of("q", h)
                act.wait_ge(w.used, n + 3)
                if h:
                    act.wait_ge(factors[1], h)
                act.activation(q[:, :], ps[n % 2][:, :], ACT.Silu)
                act.drain().then_inc(q_ready, 1)
                act.sem_inc(evac, 1)
                round_tile(n + 2)

            def value(h):
                n = tile_of("v", h)
                act.wait_ge(w.used, n + 3)
                if h:
                    act.wait_ge(v_turned, h)
                act.activation(vT[:, :], ps[n % 2][:, :], ACT.Copy)
                act.drain().then_inc(v_ready, 1)
                act.sem_inc(evac, 1)
                round_tile(n + 2)

            def gate(h):
                n = tile_of("g", h)
                act.wait_ge(w.used, n + 3)
                if h:
                    act.wait_ge(done, h)
                act.activation(g[:, :], ps[n % 2][:, :], ACT.Silu)
                act.drain().then_inc(g_ready, 1)
                act.sem_inc(evac, 1)
                round_tile(n + 2)

            def power(h, d):
                act.wait_ge(prep[d], h + 1)
                last = CHUNK - 1 if d == 0 else 0
                act.activation(ku[d][:, :], ku[d][:, :], ACT.Exp).then_inc(ku_power[d], 1)
                act.activation(kr[d][:, :], qr[d][:, :], ACT.Exp, scale=-1.0)
                act.activation(dec[:, d, :], qe[d][:, last::CHUNK], ACT.Exp)
                act.drain()
                act.activation(qr[d][:, :], qr[d][:, :], ACT.Exp)
                act.activation(qe[d][:, :], qe[d][:, :], ACT.Exp)
                act.drain().then_inc(powers[d], 1)

            def root_of(h):
                act.wait_ge(inv, h + 1)
                act.activation(r[:, :], r[:, :], ACT.Sqrt)
                act.drain().then_inc(root, 1)

            def logs(h):
                for d in range(2):
                    act.activation(low[d][:, :], low[d][:, :], ACT.Ln, scale=m.omlb[:, d, h:h + 1],
                                   bias=m.lb[:, d, h:h + 1])
                    act.drain().then_inc(log_ready[d], 1)

            for made in (*k_ready, q_ready, v_ready):
                act.sem_inc(made, 1)
            logs(0)
            power(0, 0)
            power(0, 1)
            for h in range(HEADS):
                nxt = h + 1 < HEADS
                if nxt:
                    forget(h + 1, 0)
                    forget(h + 1, 1)
                    query(h + 1)
                act.wait_ge(v_turned, h + 1)
                act.activation(vtok[:, :, :], po[:, :].rearrange("p (b v) -> p b v", b=NB), ACT.Copy)
                act.drain().then_inc(vtok_ready, 1)
                if h:
                    root_of(h - 1)
                for d in range(2):
                    for half in range(2):
                        act.wait_ge(pm_ready[half], 9 * h + d + 1)
                        act.activation(kt[d][:, 4 * half:4 * half + 4, :],
                                       pm[half][:, :].rearrange("p (b v) -> p b v", b=4), ACT.Copy)
                        act.drain().then_inc(pm_used[half], 1)
                if h:
                    act.wait_ge(done, h)
                    act.dma_start(m.mix[h - 1], o[:, :]).then_inc(stored, 16)
                if nxt:
                    if h + 2 < HEADS:
                        value(h + 1)
                    logs(h + 1)
                gate(h)
                if not nxt:
                    act.wait_ge(w.used, NT + 2)
                    for i, k in enumerate(FROM_DRAM):
                        act.wait_ge(w.arrived[i % 2], 16 * (NT // 2 + i // 2 + 2))
                        act.activation(m.hn_hi[:, k, :], raw[i % 2], ACT.Copy).then_inc(mix_hi, 1)
                act.wait_ge(o_copied, h + 1)
                act.activation(sq[:, :], o[:, :], ACT.Square)
                act.drain().then_inc(sq_ready, 1)
                if nxt:
                    power(h + 1, 0)
                    if h + 2 == HEADS:
                        value(h + 1)
                if nxt:
                    power(h + 1, 1)
            root_of(HEADS - 1)
            act.wait_ge(done, HEADS)
            act.activation(m.hn_hi[:, HEADS - 1, :], o[:, :], ACT.Copy).then_inc(mix_hi, 1)
            act.wait_ge(stored, 16 * (HEADS - 1))

        @block.vector
        def _(dve):
            chunks = lambda ap: ap.rearrange("p (n c) -> p n c", c=CHUNK)
            def prepare(h):
                for d in range(2):
                    mid, last = (CHUNK // 2 - 1, CHUNK - 1) if d == 0 else (CHUNK // 2, 0)
                    dve.wait_ge(k_ready[d], h + 1)
                    dve.tensor_scalar(kk[d][:, :], kk[d][:, :], m.omlb[:, d, h:h + 1], None, ALU.mult)
                    if h:
                        dve.wait_ge(o_ready, h)
                    elif d == 0:
                        dve.wait_ge(const, 1)
                    dve.wait_ge(log_ready[d], h + 1)
                    dve.tensor_tensor_scan(rev(qe[d][:, :], d), reset[:, :], rev(low[d][:, :], d), 0.0,
                                           ALU.mult, ALU.add)
                    dve.drain()
                    b = chunks(qe[d][:, :])
                    spread = lambda i: b[:, :, i:i + 1].broadcast_to([P, NCH, CHUNK])
                    dve.tensor_tensor(chunks(qr[d][:, :]), b, spread(mid), ALU.subtract)
                    dve.tensor_tensor(chunks(ku[d][:, :]), spread(last), b, ALU.subtract)
                    dve.drain().then_inc(prep[d], 1)

            def finish(h):
                dve.reciprocal(r[:, :], r[:, :])
                dve.drain().then_inc(inv, 1)
                dve.wait_ge(root, h + 1)
                dve.wait_ge(g_ready, h + 1)
                dve.tensor_tensor(o[:, :], o[:, :], r[:, :], ALU.mult)
                dve.drain()
                gain = COL["g_hgrn"][0] + h
                dve.scalar_tensor_tensor(o[:, :], o[:, :], m.cols[:, gain:gain + 1], g[:, :], ALU.mult, ALU.mult)
                dve.drain().then_inc(done, 1)

            prepare(0)
            for h in range(HEADS):
                dve.wait_ge(q_ready, h + 1)
                for d in range(2):
                    dve.wait_ge(ku_power[d], h + 1)
                    dve.tensor_tensor(ku[d][:, :], ku[d][:, :], kk[d][:, :], ALU.mult).then_inc(ku_ready[d], 1)
                    dve.wait_ge(powers[d], h + 1)
                    dve.tensor_tensor(kr[d][:, :], kr[d][:, :], kk[d][:, :], ALU.mult)
                    dve.tensor_tensor(qr[d][:, :], qr[d][:, :], q[:, :], ALU.mult)
                    dve.tensor_tensor(qe[d][:, :], qe[d][:, :], q[:, :], ALU.mult)
                    dve.drain().then_inc(factors[d], 1)
                if h:
                    finish(h - 1)
                for d in range(2):
                    for half in range(2):
                        dve.wait_ge(pm_ready[half], 9 * h + 3 + d)
                        for quad in range(4):
                            rows, t0, t1 = allowed(quad, d)
                            mask = m.mask[rows, d:d + 1, t0:t1].broadcast_to([32, 4, t1 - t0])
                            dve.copy_predicated(st[d][rows, 4 * half:4 * half + 4, t0:t1], mask,
                                                pm[half][rows, :].rearrange("p (b t) -> p b t", b=4)[:, :, t0:t1])
                        dve.drain().then_inc(pm_used[half], 1)
                for part in range(4):
                    for odd in range(2):
                        dve.wait_ge(pm_ready[odd], 9 * h + 5 + part)
                    for j in range(4):
                        for d in range(2):
                            n = 4 * part + j
                            c = NCH - 1 - n if d else n
                            if n < NCH - 1:
                                slot = 2 * d + j // 2
                                dve.scalar_tensor_tensor(state[d][:, n + 1, :], state[d][:, n, :], dec[:, d, c:c + 1],
                                                         pm[c % 2][:, slot * P:(slot + 1) * P], ALU.mult, ALU.add)
                        dve.drain()
                    for odd in range(2):
                        dve.drain().then_inc(pm_used[odd], 1)
                dve.wait_ge(o_ready, h + 1)
                if h:
                    dve.wait_ge(stored, 16 * h)
                dve.tensor_copy(o[:, :], po[:, :])
                dve.drain().then_inc(o_copied, 1)
                if h + 1 < HEADS:
                    prepare(h + 1)
                for b in range(2):
                    dve.wait_ge(pm_ready[b], 9 * h + 9)
                    dve.tensor_scalar(r[:, b * HALF:(b + 1) * HALF], pm[b][:, :], 1.0 / P, EPS, ALU.mult, ALU.add)
                    dve.drain().then_inc(pm_used[b], 1)
            finish(HEADS - 1)


def step4(nc, m, io, sem):
    at = m.at
    h1 = at("s4_h1", [P, DC, T], F32, F0)
    x = at("s4_x", [P, 2, T], F32, F0 + 40 * KB)
    sq = at("s4_sq", [P, 2, T], F32, F0 + 56 * KB)
    r = at("s4_r", [P, T], F32, F0 + 64 * KB)
    ctx = ExitStack()
    with ctx:
        w = Weights(m, sem, "s4w", F0 + 48 * KB)
        ps = [ctx.enter_context(nc.psum_tensor(f"s4_ps{s}", [P, T], F32)) for s in range(2)]
        ps_ss = ctx.enter_context(nc.psum_tensor("s4_ss", [P, T], F32))
        x_in = [sem(f"s4_x_in{s}") for s in range(2)]
        h1_ready, sq_ready, sq_used = (sem(f"s4_{n}") for n in ("h1r", "sqr", "squ"))
        ss_ready, inv, root, xn_ready, y_hi, stored = (sem(f"s4_{n}") for n in ("ss", "inv", "root", "xn", "yhi", "st"))
        block = ctx.enter_context(nc.Block())

        @block.sync
        def _(sp):
            for k in range(DC):
                if k >= 2:
                    w.load(sp, k // 2, k % 2, io["w_out"][k])
                    sp.wait_ge(h1_ready, k - 1)
                sp.dma_start(x[:, k % 2, :], io["xT"][k]).then_inc(x_in[k % 2], 16)
            for s in range(2):
                w.load(sp, DC // 2, s, io["wq"][s])
            for k in range(DC):
                sp.wait_ge(h1_ready, k + 1)
                sp.dma_start(m.h1[k], h1[:, k, :]).then_inc(stored, 16)
            sp.wait_ge(stored, 16 * DC)

        @block.scalar
        def _(act):
            for k in range(DC):
                w.round(act, (k + 2) // 2, k % 2)
                act.wait_ge(h1_ready, k + 1)
                if k >= 2:
                    act.wait_ge(sq_used, k - 1)
                act.activation(sq[:, k % 2, :], h1[:, k, :], ACT.Square).then_inc(sq_ready, 1)
            act.wait_ge(inv, 1)
            act.activation(r[:, :], r[:, :], ACT.Sqrt).then_inc(root, 1)
            for k in range(DC):
                act.wait_ge(xn_ready, k + 1)
                act.activation(h1[:, k, :], h1[:, k, :], ACT.Identity, scale=m.mods[:, 4, k:k + 1],
                               bias=m.mods[:, 3, k:k + 1])
                act.drain()
                act.activation(m.hn_hi[:, k, :], h1[:, k, :], ACT.Copy).then_inc(y_hi, 1)

        def remainder(engine, k):
            engine.wait_ge(y_hi, k + 1)
            engine.tensor_tensor(m.hn_lo[:, k, :], h1[:, k, :], m.hn_hi[:, k, :].bitcast(F32), ALU.subtract)

        @block.gpsimd
        def _(pool):
            for k in range(2, DC + 2):
                w.remainder(pool, k // 2, k % 2)
            for k in range(0, DC, 2):
                remainder(pool, k)

        @block.tensor
        def _(pe):
            def sums(k):
                pe.wait_ge(sq_ready, k + 1)
                for h in range(2):
                    mm = pe.matmul(ps_ss[:, h * HALF:(h + 1) * HALF], m.ones[:, :],
                                   sq[:, k % 2, h * HALF:(h + 1) * HALF], start=(k == 0), stop=(k == DC - 1))
                mm.then_inc(sq_used, 1)

            w.begin(pe)
            for k in range(DC):
                w.ready(pe, k // 2, k % 2)
                if k >= 2:
                    pe.wait_ge(h1_ready, k - 1)
                project(pe, ps[k % 2], w.hi[k % 2], w.lo[k % 2], m.hn_hi, m.hn_lo).then_inc(w.used, 1)
                if k:
                    sums(k - 1)
            sums(DC - 1)
            pe.drain().then_inc(ss_ready, 1)

        @block.vector
        def _(dve):
            for k in range(DC):
                dve.wait_ge(w.used, k + 3)
                dve.wait_ge(x_in[k % 2], 16 * (k // 2 + 1))
                dve.scalar_tensor_tensor(h1[:, k, :], ps[k % 2][:, :], m.mods[:, 2, k:k + 1], x[:, k % 2, :],
                                         ALU.mult, ALU.add).then_inc(h1_ready, 1)
            dve.wait_ge(ss_ready, 1)
            dve.tensor_scalar(r[:, :], ps_ss[:, :], 1.0 / D, EPS, ALU.mult, ALU.add)
            dve.drain()
            dve.reciprocal(r[:, :], r[:, :]).then_inc(inv, 1)
            dve.wait_ge(root, 1)
            dve.wait_ge(stored, 16 * DC)
            for k in range(DC):
                dve.tensor_tensor(h1[:, k, :], h1[:, k, :], r[:, :], ALU.mult).then_inc(xn_ready, 1)
                if k >= 3 and k % 2:
                    remainder(dve, k - 2)
            remainder(dve, DC - 1)


def step5(nc, m, io, sem):
    at = m.at
    q = [at(f"s5_q{s}", [P, T], F32, F0 + s * 4 * KB) for s in range(2)]
    sc = at("s5_sc", [P, 2, NB, KEYS], F32, F0 + 8 * KB)
    ctx = ExitStack()
    with ctx:
        w = Weights(m, sem, "s5w", F0 + 16 * KB)
        ps = [ctx.enter_context(nc.psum_tensor(f"s5_ps{s}", [P, T], F32)) for s in range(2)]
        pk = [ctx.enter_context(nc.psum_tensor(f"s5_pk{s}", [P, T], F32)) for s in range(2)]
        q_ready, sc_made, sc_taken = (sem(f"s5_{n}") for n in ("qr", "scm", "sct"))
        stored = [sem(f"s5_stored{s}") for s in range(2)]
        block = ctx.enter_context(nc.Block())

        @block.sync
        def _(sp):
            with sp.Fori(1, PH) as h:
                for s in range(2):
                    w.load(sp, h, s, io["wq"][bass.ds(h * 2 + s, 1)].rearrange("a p k m -> p (a k) m"))
            for s in range(2):
                w.load(sp, PH, s, io["u"][s])

        @block.gpsimd
        def _(pool):
            with pool.Fori(1, PH + 1) as h:
                for s in range(2):
                    w.remainder(pool, h, s)

        def scores(pe, h, s):
            pe.wait_ge(q_ready, h * 2 + s + 3)
            pe.wait_ge(sc_taken, h * 2 + s + 1)
            for b in range(NB):
                mm = pe.matmul(pk[s][:, b * P:(b + 1) * P], q[s][:, b * P:(b + 1) * P], m.keysT[:, s, :],
                               start=True, stop=True)
            mm.then_inc(sc_made, 1)

        @block.tensor
        def _(pe):
            w.begin(pe)
            pe.sem_inc(q_ready, 2)
            with pe.Fori(0, PH) as h:
                for s in range(2):
                    w.ready(pe, h, s)
                    pe.wait_ge(q_ready, h * 2 + s + 1)
                    project(pe, ps[s], w.hi[s], w.lo[s], m.hn_hi, m.hn_lo).then_inc(w.used, 1)
                    if s:
                        scores(pe, h, 0)
                scores(pe, h, 1)

        @block.scalar
        def _(act):
            def query(h, s, again=True):
                act.wait_ge(w.used, h * 2 + s + 3)
                if again:
                    act.wait_ge(sc_made, h * 2 + s - 1)
                act.activation(q[s][:, :], ps[s][:, :], ACT.Copy).then_inc(q_ready, 1)

            def store(h, s):
                act.wait_ge(sc_taken, h * 2 + s + 3)
                act.dma_start(m.scores[:, :, bass.ds(h * 2 + s, 1), :].rearrange("b p c k -> p (b c) k"),
                              sc[:, s, :, :]).then_inc(stored[s], 16)

            query(0, 0, again=False)
            w.round(act, 1, 0)
            query(0, 1, again=False)
            w.round(act, 1, 1)
            store(0, 0)
            store(0, 1)
            with act.Fori(1, PH - 1) as h:
                query(h, 0)
                w.round(act, h + 1, 0)
                query(h, 1)
                w.round(act, h + 1, 1)
                store(h, 0)
                store(h, 1)
            for s in range(2):
                query(PH - 1, s)
                w.round(act, PH, s)
            for s in range(2):
                store(PH - 1, s)
            for s in range(2):
                act.wait_ge(stored[s], 16 * PH)

        @block.vector
        def _(dve):
            dve.sem_inc(sc_taken, 2)
            for h in range(PH):
                for s in range(2):
                    dve.wait_ge(sc_made, h * 2 + s + 1)
                    if h:
                        dve.wait_ge(stored[s], h * 16)
                    dve.tensor_copy(sc[:, s, :, :], pk[s][:, :].rearrange("p (b k) -> p b k", b=NB))\
                       .then_inc(sc_taken, 1)
                dve.drain()
                for part in range(3):
                    m.picks.part(dve, h, part, sc[:, :, 0, :])


class Picks:

    def __init__(self, m, at):
        def buffer(name, shape, dt=F32):
            t = m.at(f"pk_{name}", shape, dt, self.end)
            self.end += -(-int(np.prod(shape[1:])) * 4 // 32) * 32
            return t

        self.end = at
        self.val = buffer("val", [P, 2 * PH, TOPK])
        self.key = buffer("key", [P, 2 * PH, TOPK], U32)
        self.rep = [buffer(f"rep{s}", [P, KEYS]) for s in range(2)]
        self.cand = buffer("cand", [P, TOPK, TOPK])
        self.cand2 = buffer("cand2", [P, TOPK, TOPK])
        self.best = buffer("best", [P, PH, TOPK])
        self.place = buffer("place", [P, PH, TOPK], U32)

    def part(self, dve, h, part, sc):
        (self.best8, self.next8, self.best_sums)[part](dve, h, sc)

    def best8(self, dve, h, sc):
        for n in (2 * h, 2 * h + 1):
            dve.max(out=self.val[:, n, 0:8], in_=sc[:, n % 2, :])
        dve.drain()
        for n in (2 * h, 2 * h + 1):
            dve.max_index(self.key[:, n, 0:8], self.val[:, n, 0:8], sc[:, n % 2, :])
            dve.match_replace(out=self.rep[n % 2][:, :], in_to_replace=self.val[:, n, 0:8], in_values=sc[:, n % 2, :],
                              imm_value=LOWEST)
        dve.drain()

    def next8(self, dve, h, sc):
        for n in (2 * h, 2 * h + 1):
            dve.max(out=self.val[:, n, 8:16], in_=self.rep[n % 2][:, :])
        dve.drain()
        for n in (2 * h, 2 * h + 1):
            dve.max_index(self.key[:, n, 8:16], self.val[:, n, 8:16], self.rep[n % 2][:, :])
        dve.tensor_tensor(self.cand[:, :, :], self.val[:, 2 * h, :].unsqueeze(2).broadcast_to([P, TOPK, TOPK]),
                          self.val[:, 2 * h + 1, :].unsqueeze(1).broadcast_to([P, TOPK, TOPK]), ALU.add)
        dve.drain()

    def best_sums(self, dve, h, sc):
        flat = [x[:, :, :].rearrange("p a b -> p (a b)") for x in (self.cand, self.cand2)]
        dve.max(out=self.best[:, h, 0:8], in_=flat[0])
        dve.drain()
        dve.max_index(self.place[:, h, 0:8], self.best[:, h, 0:8], flat[0])
        dve.match_replace(out=flat[1], in_to_replace=self.best[:, h, 0:8], in_values=flat[0], imm_value=LOWEST)
        dve.drain()
        dve.max(out=self.best[:, h, 8:16], in_=flat[1])
        dve.drain()
        dve.max_index(self.place[:, h, 8:16], self.best[:, h, 8:16], flat[1])
        dve.drain()


def step6(nc, m, io, sem):
    at = m.at
    G0 = R0 + 80 * KB
    wb = [at(f"s6_wb{s}", [P, KEYS, CHUNK], F32, F0 + 32 * KB * s) for s in range(2)]
    gst = [at(f"s6_g{s}", [P, T], F32, G0 + 4 * KB * s) for s in range(2)]
    oh = [at(f"s6_oh{s}", [P, 3, 4, KEYS], F32R, G0 + 8 * KB + 6 * KB * s) for s in range(2)]
    TW = 8
    sc = at("s6_sc", [P, 2 * PH, KEYS], F32, G0 + 20 * KB)
    eq = at("s6_eq", [P, P, TOPK], BF16, G0 + 28 * KB)
    c = m.picks.end

    def small(name, shape, dt=F32):
        nonlocal c
        t = at(f"s6_{name}", shape, dt, c)
        c += -(-int(np.prod(shape[1:])) * (2 if dt == BF16 else 4) // 32) * 32
        return t

    picks = m.picks
    key, best, place = picks.key, picks.best, picks.place
    keyf = small("keyf", [P, 2 * PH, TOPK], BF16)
    half = [small(f"half{s}", [P, P], U32) for s in range(2)]
    halff = [small(f"halff{s}", [P, P], BF16) for s in range(2)]
    count = small("count", [P, TOPK], BF16)
    pick = small("pick", [P, 3, P])
    pickT = small("pickT", [P, 3, P])
    w_hi = small("w_hi", [P, P], F32R)
    norm = small("norm", [P, 2, PH])
    w_lo = small("w_lo", [P, TW, KEYS])
    assert c <= R0 + 128 * KB
    ctx = ExitStack()
    with ctx:
        w = Weights(m, sem, "s6u", F0 + 64 * KB)
        ps = [ctx.enter_context(nc.psum_tensor(f"s6_ps{s}", [P, T], F32)) for s in range(2)]
        pw = ctx.enter_context(nc.psum_tensor("s6_pw", [P, TW, 2, KEYS], F32))
        pt = pw[:, 0:2, :, :].rearrange("p t s k -> p (t s) k")
        gelu = sem("s6_gelu")
        g_stored = [sem(f"s6_gst{s}") for s in range(2)]
        oh_ready, oh_used = sem("s6_ohr"), sem("s6_ohu")
        w_taken, w_added = sem("s6_wt"), sem("s6_wa")
        w_stored = [sem(f"s6_wst{s}") for s in range(2)]
        sc_in, sc_used = sem("s6_scin"), sem("s6_scu")
        ex_in, ex_out, pick_ready, turned = (sem(f"s6_{n}") for n in ("exi", "exo", "pick", "turn"))
        block = ctx.enter_context(nc.Block())
        PAIRS = 4


        @block.sync
        def _(sp):
            def tiles(b, last=False):
                with sp.Fori(1, 2 * PAIRS + (0 if last else 1)) as i:
                    for s in range(2):
                        w.load(sp, b * 2 * PAIRS + i, s,
                               io["u"][bass.ds((b * 2 * PAIRS + i) * 2 + s, 1)].rearrange("a p k m -> p (a k) m"))

            with sp.Fori(0, NB - 1) as b:
                sp.wait_ge(sc_used, b + 1)
                sp.dma_start(sc[:, :, :], m.scores[bass.ds(b + 1, 1)].rearrange("b p c k -> p (b c) k")).then_inc(sc_in, 16)
                tiles(b)
            tiles(NB - 1, last=True)

        @block.scalar
        def _(act):
            def gelu_tile(n, s):
                act.wait_ge(w.used, n * 2 + s + 3)
                act.wait_ge(g_stored[s], n * 16 + 16)
                act.activation(gst[s][:, :], ps[s][:, :], ACT.Gelu)
                act.drain().then_inc(gelu, 1)
                act.dma_start(m.g[bass.ds(n * 2 + s, 1)].rearrange("a p t -> p (a t)"), gst[s][:, :])\
                   .then_inc(g_stored[s], 16)

            def take_w(b, hh, i, s):
                n = (b * 2 + hh) * 2 * PAIRS + i * 2 + s
                act.wait_ge(oh_used, n * 2 + 4)
                act.activation(wb[hh][:, :, bass.ds((i * 2 + s) * TW, TW)].rearrange("p k t -> p t k"),
                               pw[:, :, 0, :], ACT.Copy)
                act.wait_ge(w_added, n + 1)
                act.activation(w_lo[:, :, :], pw[:, :, 1, :], ACT.Copy)
                act.drain().then_inc(w_taken, 1)

            def pair(b, hh, i, last):
                for s in range(2):
                    n = (b * 2 + hh) * PAIRS + i
                    gelu_tile(n, s)
                    if not last:
                        w.round(act, n + 1, s)
                    take_w(b, hh, i, s)

            def store_w(b, hh):
                act.wait_ge(w_added, (b * 2 + hh) * 2 * PAIRS + 2 * PAIRS + 1)
                act.dma_start(m.w[bass.ds(b * 2 + hh, 1)].rearrange("a p k -> p (a k)"),
                              wb[hh][:, :, :].rearrange("p k t -> p (k t)")).then_inc(w_stored[hh], 16)

            def softmax(b):
                act.wait_ge(ex_in, b + 1)
                act.activation(pick[:, 2, :], pick[:, 2, :], ACT.Exp)
                act.drain().then_inc(ex_out, 1)

            def whole_block(b, last=False):
                for hh in range(2):
                    act.wait_ge(w_stored[hh], b * 16 + 16)
                    with act.Fori(0, PAIRS - hh) as i:
                        pair(b, hh, i, False)
                    if hh:
                        if not last:
                            softmax(b + 1)
                        pair(b, hh, PAIRS - 1, last)
                    store_w(b, hh)

            for s in range(2):
                act.sem_inc(g_stored[s], 16)
                act.sem_inc(w_stored[s], 16)
            softmax(0)
            with act.Fori(0, NB - 1) as b:
                whole_block(b)
            whole_block(NB - 1, last=True)
            for s in range(2):
                act.wait_ge(w_stored[s], 16 * NB + 16)
                act.wait_ge(g_stored[s], 16 * NB * 2 * PAIRS + 16)

        @block.gpsimd
        def _(pool):
            pool.sem_inc(w_added, 1)
            def pair(b, hh, i, last=False):
                for s in range(2):
                    n = (b * 2 + hh) * PAIRS + i
                    out = wb[hh][:, :, bass.ds((i * 2 + s) * TW, TW)].rearrange("p k t -> p t k")
                    pool.wait_ge(w_taken, n * 2 + s + 2)
                    pool.tensor_tensor(out, out, w_lo[:, :, :], ALU.add).then_inc(w_added, 1)
                    if not last:
                        w.remainder(pool, n + 1, s)

            with pool.Fori(0, NB - 1) as b:
                for hh in range(2):
                    with pool.Fori(0, PAIRS) as i:
                        pair(b, hh, i)
            for hh in range(2):
                with pool.Fori(0, PAIRS - hh) as i:
                    pair(NB - 1, hh, i)
            pair(NB - 1, 1, PAIRS - 1, last=True)

        @block.tensor
        def _(pe):
            def pair(b, hh, i, first=False):
                for s in range(2):
                    n = (b * 2 + hh) * PAIRS + i
                    w.ready(pe, n, s)
                    pe.wait_ge(gelu, n * 2 + s + 1)
                    tile = (ps[s], w.hi[s], w.lo[s], m.hn_hi, m.hn_lo)
                    if first and s == 0:
                        project(pe, *tile, ks=range(DC // 4))
                        turn_picks(b)
                        mm = project(pe, *tile, ks=range(DC // 4, DC))
                    else:
                        mm = project(pe, *tile)
                    mm.then_inc(w.used, 1)
                    pe.wait_ge(w_taken, n * 2 + s + 1)
                    for q in range(2):
                        pe.wait_ge(oh_ready, (n * 2 + s) * 2 + q + 1)
                        for j in range(4):
                            mm = pe.matmul(pw[:, 4 * q + j, :, :], oh[q][:, 0, j, :], oh[q][:, 1:3, j, :],
                                           start=True, stop=True)
                        mm.then_inc(oh_used, 1)

            def turn_picks(b):
                pe.wait_ge(pick_ready, b + 1)
                pe.wait_ge(w_taken, b * 2 * 2 * PAIRS + 1)
                for v in range(3):
                    mm = pe.transpose(pt[:, v, :], pick[:, v, :], m.ident[:, :])
                mm.then_inc(turned, 1)

            w.begin(pe)
            pe.sem_inc(gelu, 2)
            pe.sem_inc(oh_used, 2)
            pe.sem_inc(w_taken, 1)
            with pe.Fori(0, NB) as b:
                pair(b, 0, 0, first=True)
                with pe.Fori(1, PAIRS) as i:
                    pair(b, 0, i)
                with pe.Fori(0, PAIRS) as i:
                    pair(b, 1, i)

        @block.vector
        def _(dve):
            def one_hots(r, x):
                dve.wait_ge(oh_used, r * 32 + x + 1)
                for j in range(4):
                    t, o = 4 * x + j, oh[x % 2]
                    dve.tensor_scalar(o[:, 0, j, :], m.iota[:, :], pickT[:, 1, t:t + 1], None, ALU.is_equal)
                    dve.tensor_scalar(o[:, 1, j, :], m.iota[:, :], pickT[:, 0, t:t + 1],
                                      w_hi[:, t:t + 1].bitcast(F32), ALU.is_equal, ALU.mult)
                    dve.tensor_scalar(o[:, 2, j, :], m.iota[:, :], pickT[:, 0, t:t + 1], pickT[:, 2, t:t + 1],
                                      ALU.is_equal, ALU.mult)
                dve.drain().then_inc(oh_ready, 1)

            weights = pick[:, 2, :].rearrange("p (h j) -> p h j", h=PH)
            eq4 = eq[:, :, :].rearrange("p (h j) a -> p h j a", h=PH)

            def places(b):
                flat = place[:, :, :].rearrange("p h j -> p (h j)")
                dve.wait_ge(turned, b + 1)
                dve.tensor_tensor(weights, best[:, :, :], best[:, :, 0:1].broadcast_to([P, PH, TOPK]), ALU.subtract)
                dve.tensor_scalar(half[0][:, :], flat, 4, None, ALU.logical_shift_right)
                dve.tensor_scalar(half[1][:, :], flat, 15, None, ALU.bitwise_and)
                dve.tensor_copy(keyf[:, :, :], key[:, :, :])
                dve.drain().then_inc(ex_in, 1)
                for s in range(2):
                    dve.tensor_copy(halff[s][:, :], half[s][:, :])
                dve.drain()

            def ranked_key(s, part):
                if part == 0:
                    dve.tensor_tensor(eq[:, :, :], halff[s][:, :].unsqueeze(2).broadcast_to([P, P, TOPK]),
                                      count[:, :].unsqueeze(1).broadcast_to([P, P, TOPK]), ALU.is_equal)
                elif part == 1:
                    ranked = keyf[:, :, :].rearrange("p (h s) a -> p h s a", s=2)[:, :, s, :].unsqueeze(2)
                    dve.tensor_tensor(eq4, eq4, ranked.broadcast_to([P, PH, TOPK, TOPK]), ALU.mult)
                else:
                    dve.tensor_reduce(pick[:, s, :], eq[:, :, :], AX.X, ALU.add)
                dve.drain()

            def normalise(b):
                dve.wait_ge(ex_out, b + 1)
                dve.tensor_reduce(norm[:, 0, :], weights, AX.X, ALU.add)
                dve.drain()
                dve.reciprocal(norm[:, 1, :], norm[:, 0, :])
                dve.drain()
                dve.tensor_tensor(weights, weights, norm[:, 1, :].unsqueeze(2).broadcast_to([P, PH, TOPK]), ALU.mult)
                dve.drain().then_inc(pick_ready, 1)

            def take_picks(b):
                dve.wait_ge(turned, b + 2)
                dve.tensor_copy(pickT[:, 0:2, :], pt[:, 0:2, :])
                dve.tensor_copy(w_hi[:, :], pt[:, 2, :])
                dve.drain()
                dve.tensor_tensor(pickT[:, 2, :], pt[:, 2, :], w_hi[:, :].bitcast(F32), ALU.subtract)
                dve.drain()

            def ranking(b, x):
                if x < 3 * PH:
                    picks.part(dve, x // 3, x % 3, sc[:, x // 3 * 2:x // 3 * 2 + 2, :])
                elif x == 24:
                    dve.drain().then_inc(sc_used, 1)
                    places(b)
                elif x < 31:
                    ranked_key((x - 25) // 3, (x - 25) % 3)
                else:
                    normalise(b)
                    take_picks(b)

            dve.sem_inc(turned, 1)
            dve.sem_inc(sc_used, 1)
            dve.tensor_copy(count[:, :], m.iota[:, 0:TOPK])
            dve.memset(norm[:, :, :], 0.0)
            dve.drain()
            places(0)
            for x in range(25, 31):
                ranking(0, x)
            normalise(0)
            take_picks(0)
            with dve.Fori(0, NB - 1) as b:
                dve.wait_ge(sc_in, b * 16 + 16)
                dve.memset(norm[:, :, :], 0.0)
                dve.drain()
                for x in range(32):
                    one_hots(b, x)
                    ranking(b + 1, x)
            for x in range(32):
                one_hots(NB - 1, x)


def step7(nc, m, io, sem):
    GT, Q = 4, 4
    NG = KEYS // GT
    at = m.at
    v_hi = [at(f"s7_vhi{g}", [P, GT, D], F32R, R0 + 32 * KB * g) for g in range(2)]
    v_lo = [at(f"s7_vlo{g}", [P, GT, D], F32R, R0 + 32 * KB * g + 16 * KB) for g in range(2)]
    c_hi = [at(f"s7_chi{g}", [P, GT, T], F32R, R0 + 64 * KB + 32 * KB * g) for g in range(2)]
    c_lo = [at(f"s7_clo{g}", [P, GT, T], F32R, R0 + 64 * KB + 32 * KB * g + 16 * KB) for g in range(2)]
    y = m.y
    vr = [at(f"s7_vr{s}", [P, D], F32, F0 + 32 * KB + 4 * KB * s) for s in range(2)]
    gr = [at(f"s7_gr{s}", [P, T], F32, F0 + 40 * KB + 4 * KB * s) for s in range(2)]
    wr = [at(f"s7_wr{s}", [P, 2 * NB, 2, CHUNK], F32, F0 + 48 * KB + 8 * KB * s) for s in range(2)]
    ctx = ExitStack()
    with ctx:
        ps = [ctx.enter_context(nc.psum_tensor(f"s7_ps{s}", [P, 2, T], F32)) for s in range(2)]
        v_in = [sem(f"s7_v_in{s}") for s in range(2)]
        g_in = [sem(f"s7_g_in{s}") for s in range(2)]
        w_in = [sem(f"s7_w_in{s}") for s in range(2)]
        v_rounded, v_split, coef, c_rounded, c_split = (sem(f"s7_{n}") for n in ("vr_", "vs", "co", "cr", "cs"))
        made, taken = sem("s7_made"), sem("s7_taken")
        h1_in = sem("s7_h1_in")
        block = ctx.enter_context(nc.Block())
        PER = 2 * GT
        w4 = m.w.rearrange("n p (k t) -> p n k t", t=CHUNK)

        @block.sync
        def _(sp):
            with sp.Fori(0, NG // 2) as it:
                for t in range(PER):
                    n = it * PER + t
                    s, p = t % 2, t // 2 % 2
                    sp.wait_ge(v_split, n + 1)
                    sp.dma_start(vr[s][:, :], io["v"][bass.ds(n, 1)].rearrange("a p d -> p (a d)")).then_inc(v_in[s], 16)
                    sp.wait_ge(c_split, n + 1)
                    sp.dma_start(gr[s][:, :], m.g[bass.ds(n, 1)].rearrange("a p t -> p (a t)")).then_inc(g_in[s], 16)
                    if s == 0:
                        sp.dma_start(wr[p][:, :, :, :], w4[:, :, bass.ds(n, 2), :]).then_inc(w_in[p], 16)
            sp.wait_ge(made, (NG + 1) * Q)
            sp.dma_start(m.h1_back[:, :, :], m.h1.rearrange("k p t -> p k t")).then_inc(h1_in, 16)
            sp.wait_ge(h1_in, 16)

        @block.scalar
        def _(act):
            with act.Fori(0, NG // 2) as it:
                for t in range(PER):
                    n, s, g = it * PER + t, t % 2, t // GT
                    if t % GT == 0:
                        act.wait_ge(made, (it * 2 + g + 1) * Q)
                    act.wait_ge(v_in[s], (it * (PER // 2) + t // 2 + 1) * 16)
                    act.activation(v_hi[g][:, t % GT, :], vr[s][:, :], ACT.Copy).then_inc(v_rounded, 1)
                    act.wait_ge(coef, n + 1)
                    act.activation(c_hi[g][:, t % GT, :], gr[s][:, :], ACT.Copy).then_inc(c_rounded, 1)

        @block.gpsimd
        def _(pool):
            pool.sem_inc(v_split, 2)
            with pool.Fori(0, NG // 2) as it:
                for t in range(PER):
                    n, s, g = it * PER + t, t % 2, t // GT
                    pool.wait_ge(v_rounded, n + 1)
                    pool.tensor_tensor(v_lo[g][:, t % GT, :], vr[s][:, :], v_hi[g][:, t % GT, :].bitcast(F32),
                                       ALU.subtract).then_inc(v_split, 1)

        @block.tensor
        def _(pe):
            pe.sem_inc(made, 2 * Q)
            pe.sem_inc(taken, 2)
            with pe.Fori(0, NG // 2) as it:
                for g in range(2):
                    for qd in range(Q):
                        out = ps[qd % 2]
                        pe.wait_ge(taken, (it * 2 + g) * Q + qd + 1)
                        for dc in range(2):
                            d = slice((2 * qd + dc) * P, (2 * qd + dc + 1) * P)
                            for t in range(GT):
                                if qd == 0 and dc == 0:
                                    pe.wait_ge(v_split, (it * 2 + g) * GT + t + 3)
                                    pe.wait_ge(c_split, (it * 2 + g) * GT + t + 3)
                                halves = [slice(h * HALF, (h + 1) * HALF) for h in range(2)]
                                for c in halves:
                                    pe.matmul(out[:, dc, c], v_hi[g][:, t, d], c_hi[g][:, t, c], start=(t == 0), stop=False)
                                    pe.matmul(out[:, dc, c], v_hi[g][:, t, d], c_lo[g][:, t, c], start=False, stop=False)
                                for c in halves:
                                    mm = pe.matmul(out[:, dc, c], v_lo[g][:, t, d], c_hi[g][:, t, c], start=False,
                                                   stop=(t == GT - 1))
                        mm.then_inc(made, 1)

        @block.vector
        def _(dve):
            def coefficients(it, t):
                n, s, g, p = it * PER + t, t % 2, t // GT, t // 2 % 2
                dve.wait_ge(g_in[s], (it * (PER // 2) + t // 2 + 1) * 16)
                dve.wait_ge(w_in[p], (it * (PER // 4) + t // 4 + 1) * 16)
                if t % GT == 0:
                    dve.wait_ge(made, (it * 2 + g + 1) * Q)
                g3 = gr[s][:, :].rearrange("p (n t) -> p n t", t=CHUNK)
                dve.tensor_tensor(g3, g3, wr[p][:, :, s, :], ALU.mult)
                dve.drain().then_inc(coef, 1)
                dve.wait_ge(c_rounded, n + 1)
                dve.tensor_tensor(c_lo[g][:, t % GT, :], gr[s][:, :], c_hi[g][:, t % GT, :].bitcast(F32),
                                  ALU.subtract).then_inc(c_split, 1)

            def add(group, qd):
                dve.wait_ge(made, (group + 2) * Q + qd + 1)
                dve.tensor_tensor(y[:, 2 * qd:2 * qd + 2, :], y[:, 2 * qd:2 * qd + 2, :], ps[qd % 2][:, :, :], ALU.add)\
                   .then_inc(taken, 1)

            dve.sem_inc(c_split, 2)
            dve.memset(y[:, :, :], 0.0)
            for t in range(GT):
                coefficients(0, t)
            def turn(it, more):
                for g in range(2):
                    for qd in range(Q):
                        if g == 0:
                            coefficients(it, GT + qd)
                        elif more:
                            coefficients(it + 1, qd)
                        add(it * 2 + g, qd)

            with dve.Fori(0, NG // 2 - 1) as it:
                turn(it, True)
            turn(NG // 2 - 1, False)


def step8(nc, m, io, sem):
    at, y = m.at, m.y
    h1 = m.h1_back
    sq = at("s8_sq", [P, 2, T], F32, R0 + 32 * KB)
    r = at("s8_r", [P, T], F32, R0 + 40 * KB)
    ctx = ExitStack()
    with ctx:
        ps_ss = ctx.enter_context(nc.psum_tensor("s8_ss", [P, T], F32))
        h2_ready, sq_ready, sq_used, ss_ready, inv, root, xn_ready, done, stored = (
            sem(f"s8_{n}") for n in ("h2", "sqr", "squ", "ss", "inv", "root", "xn", "done", "st"))
        block = ctx.enter_context(nc.Block())

        @block.sync
        def _(sp):
            for k in range(DC):
                sp.wait_ge(done, k + 1)
                sp.dma_start(io["out"][k], y[:, k, :]).then_inc(stored, 16)
            sp.wait_ge(stored, 16 * DC)

        @block.scalar
        def _(act):
            for k in range(DC):
                act.wait_ge(h2_ready, k + 1)
                if k >= 2:
                    act.wait_ge(sq_used, k - 1)
                act.activation(sq[:, k % 2, :], y[:, k, :], ACT.Square).then_inc(sq_ready, 1)
            act.wait_ge(inv, 1)
            act.activation(r[:, :], r[:, :], ACT.Sqrt).then_inc(root, 1)
            for k in range(DC):
                act.wait_ge(xn_ready, k + 1)
                act.activation(y[:, k, :], y[:, k, :], ACT.Identity, scale=m.mods[:, 7, k:k + 1],
                               bias=m.mods[:, 6, k:k + 1]).then_inc(done, 1)

        @block.tensor
        def _(pe):
            for k in range(DC):
                pe.wait_ge(sq_ready, k + 1)
                for h in range(2):
                    mm = pe.matmul(ps_ss[:, h * HALF:(h + 1) * HALF], m.ones[:, :],
                                   sq[:, k % 2, h * HALF:(h + 1) * HALF], start=(k == 0), stop=(k == DC - 1))
                mm.then_inc(sq_used, 1)
            pe.drain().then_inc(ss_ready, 1)

        @block.vector
        def _(dve):
            for k in range(DC):
                dve.scalar_tensor_tensor(y[:, k, :], y[:, k, :], m.mods[:, 5, k:k + 1], h1[:, k, :], ALU.mult,
                                         ALU.add).then_inc(h2_ready, 1)
            dve.wait_ge(ss_ready, 1)
            dve.tensor_scalar(r[:, :], ps_ss[:, :], 1.0 / D, EPS, ALU.mult, ALU.add)
            dve.drain()
            dve.reciprocal(r[:, :], r[:, :]).then_inc(inv, 1)
            dve.wait_ge(root, 1)
            for k in range(DC):
                dve.tensor_tensor(y[:, k, :], y[:, k, :], r[:, :], ALU.mult).then_inc(xn_ready, 1)


STEPS = (step1, step2, step3, step4, step5, step6, step7, step8)


def encoder_layer(nc, io, out, steps=8, scratch="Internal"):
    m = Mem()
    m.at = lambda name, shape, dt, off: nc.alloc_sbuf_tensor_at(name, shape, dt, offset=off)
    m.arena = nc.alloc_sbuf_tensor("arena", [P, (C0 + CB - BASE) // 4], F32)
    free = C0

    def constant(name, shape, dt=F32):
        nonlocal free
        t = m.at(name, shape, dt, free)
        free += -(-int(np.prod(shape[1:])) * 4 // 32) * 32
        assert free <= C0 + CB
        return t

    m.cols = constant("cols", [P, NCOL])
    m.ident = constant("ident", [P, P])
    m.ones = constant("ones", [P, P])
    m.iota = constant("iota", [P, KEYS])
    m.mask = constant("mask", [P, 2, P], I32)
    m.keysT = constant("keysT", [P, 2, KEYS])
    m.mods = constant("mods", [P, 8, DC])
    m.cact = constant("cact", [P, DC])
    m.lb = constant("lb", [P, 2, HEADS])
    m.omlb = constant("omlb", [P, 2, HEADS])
    m.hn_hi = m.at("hn_hi", [P, DC, T], F32R, R0)
    m.hn_lo = m.at("hn_lo", [P, DC, T], F32R, R0 + 32 * KB)
    m.w_hi = [m.at(f"w_hi{s}", [P, DC, P], F32R, R0 + 64 * KB + s * 8 * KB) for s in range(2)]
    m.w_lo = [m.at(f"w_lo{s}", [P, DC, P], F32R, R0 + 68 * KB + s * 8 * KB) for s in range(2)]
    m.head = head_inputs(m)
    m.picks = Picks(m, R0 + 112 * KB)
    m.h1_back = m.at("h1_back", [P, DC, T], F32, R0)
    m.y = m.at("y", [P, DC, T], F32, F0)
    m.col = lambda name: m.cols[:, COL[name][0]:COL[name][1]]
    dram = lambda name, shape: nc.dram_tensor(name, shape, F32, kind=scratch).ap()
    m.mix = dram("s_mix", [2 * HEADS, P, T])
    m.h1 = dram("s_h1", [DC, P, T])
    m.scores = dram("s_scores", [NB, P, 2 * PH, KEYS])
    m.g = dram("s_g", [KEYS, KEYS, T])
    m.w = dram("s_w", [2 * NB, P, KEYS * CHUNK])
    for n, step in enumerate((constants,) + STEPS[:steps]):
        sems = []

        def sem(name):
            sems.append(nc.alloc_semaphore(name))
            return sems[-1]

        step(nc, m, io if n < 8 else {**io, "out": out}, sem)
        nc.clear_and_free_semaphores(sems)
        nc.all_engine_barrier()


def kernel(**inputs):
    from concourse import bacc
    from concourse.bass_utils import run_bass_kernel_spmd

    arrays = layouts(inputs)
    nc = bacc.Bacc("TRN2", target_bir_lowering=False, num_devices=1)
    io = {k: nc.dram_tensor(f"in_{k}", v.shape, mybir.dt.from_np(v.dtype), kind="ExternalInput").ap()
          for k, v in arrays.items()}
    out = nc.dram_tensor("out_T", (DC, P, T), F32, kind="ExternalOutput").ap()
    encoder_layer(nc, io, out)
    r = run_bass_kernel_spmd(nc, [{f"in_{k}": v for k, v in arrays.items()}], core_ids=[0])
    got = r.results[0]["out_T"].reshape(D, T)
    return np.ascontiguousarray(got.T).reshape(1, T, D)


def layouts(inputs):
    a = {k: np.asarray(v) for k, v in inputs.items()}
    chunks = lambda v: v.reshape(-1, P).T

    def tiles(w):
        return w.reshape(DC, P, -1, P).transpose(2, 1, 0, 3)

    w = tiles(a["w_in"][0])
    q, ff, fb, i, g, ca, cg = (4 * n for n in range(7))
    order = [x for c in range(CONV_C) for x in (cg + c, ca + c)]
    first = {"ff": ff, "fb": fb, "q": q, "v": i, "g": g}
    order += [first[kind] + h for kind, h in HEAD_TILES]
    mods = np.concatenate([a["ada_w"][0], a["final_ada_w"]], axis=1)
    cols = np.concatenate(
        [chunks(a["ada_b"][0]), chunks(a["final_ada_b"]), chunks(a["norm_mix_g"][0]), chunks(a["norm_ffn_g"][0]),
         chunks(a["final_norm_g"]), chunks(a["c"][0]), chunks(a["hgrn_norm_g"][0]), chunks(a["conv_b"][0]),
         chunks(a["conv_ln_g"][0]), chunks(a["conv_ln_b"][0]), chunks(a["lb_gamma_fwd"]),
         chunks(a["lb_gamma_bwd"]),
         a["conv_w"][0].T.reshape(CONV_C, P, CONV_W).transpose(1, 0, 2).reshape(P, -1)], axis=1)
    out = {
        "xT": a["x"][0].T.reshape(DC, P, T),
        "cols": cols,
        "ada": mods.reshape(DC, P, 8, D).transpose(2, 1, 0, 3),
        "w_in": w[order],
        "w_out": tiles(a["w_out"][0]),
        "wq": tiles(a["peer_wq"][0]),
        "keysT": np.stack([a["peer_keys1"][0].T, a["peer_keys2"][0].T], axis=1),
        "u": a["peer_u"][0].reshape(KEYS, KEYS, DC, P).transpose(0, 3, 2, 1),
        "v": a["peer_v"][0].reshape(KEYS, KEYS, D),
    }
    return {k: np.ascontiguousarray(v) for k, v in out.items()}
```
